# Optimizing a Trainium2 kernel written in Bass

```python
import jax, jax.numpy as jnp
from jax import lax
import numpy as np

D_MODEL = 1024
BATCH = 1
SEQ = 256
DEPTH = 2

GRID_W = 64
CTX_LEN = 256
D_FF = ((8 * D_MODEL // 3 + 255) // 256) * 256
HALF_STEP = 0.5
N_MOD = 9
RMS_EPS = 1e-6
NEG_INF = -1e30

CONV_CH = D_MODEL // 4
CONV_K = 3
POOL_CH = D_MODEL // 4
POOL_WINDOWS = (2, 4, 8, 16)
POOL_GROUP = POOL_CH // 4
NA_HEAD_DIM = 64
NA_CH = D_MODEL // 2
NA_HEADS = NA_CH // NA_HEAD_DIM
NA_KH_MAX = 8
NA_KW = 16
NA_QC = 16
NA_KB = NA_QC + NA_KW - 1
D_MIX = CONV_CH + POOL_CH + NA_CH
OFF_B = CONV_CH
OFF_C = 2 * CONV_CH
OFF_P = 3 * CONV_CH
OFF_Q = 3 * CONV_CH + POOL_CH
OFF_K = OFF_Q + NA_CH
OFF_V = OFF_K + NA_CH
D_IN = OFF_V + NA_CH


def rms_norm(x, g):
    xf = x.astype(jnp.float32)
    y = xf * lax.rsqrt(jnp.mean(xf * xf, axis=-1, keepdims=True) + RMS_EPS)
    return (y * g.astype(jnp.float32)).astype(x.dtype)

def mod_norm(x, m, i, g):
    return rms_norm(x, g) * (1 + m[:, 3 * i + 1, None]) + m[:, 3 * i, None]

def swiglu(h, w1, w2):
    a, b = jnp.split(h @ w1, 2, axis=-1)
    return (jax.nn.silu(a) * b) @ w2

def ffn_sublayer(x, m, i, g, w1, w2):
    return x + HALF_STEP * m[:, 3 * i + 2, None] * swiglu(mod_norm(x, m, i, g), w1, w2)

def short_conv(u, w):
    return lax.conv_general_dilated(
        u, w[:, None, :].astype(u.dtype), window_strides=(1,),
        padding=[(CONV_K // 2, CONV_K // 2)],
        dimension_numbers=('NWC', 'WIO', 'NWC'), feature_group_count=u.shape[-1])

def gated_conv_mixer(h, b_gate, c_gate, conv_w):
    return b_gate * short_conv(c_gate * h, conv_w)

def multiscale_pool_mixer(v, pool_w, pool_scale):
    L = v.shape[1]
    vf = v.astype(jnp.float32)
    cs = jnp.concatenate([jnp.zeros_like(vf[:, :1]), jnp.cumsum(vf, axis=1)], axis=1)
    t = jnp.arange(L)
    outs = []
    for g, w in enumerate(POOL_WINDOWS):
        left = w // 2
        right = w - 1 - left
        lo = jnp.clip(t - left, 0, L)
        hi = jnp.clip(t + right + 1, 0, L)
        sl = slice(g * POOL_GROUP, (g + 1) * POOL_GROUP)
        mean = (cs[:, hi, sl] - cs[:, lo, sl]) / (hi - lo).astype(jnp.float32)[None, :, None]
        outs.append((mean - vf[..., sl]).astype(v.dtype) @ pool_w[g])
    return jnp.concatenate(outs, axis=-1) * pool_scale

def context_attention(q, k, v):
    B, L = q.shape[:2]
    s = jnp.einsum('bqhd,bkhd->bhqk', q, k, preferred_element_type=jnp.float32) * (NA_HEAD_DIM ** -0.5)
    p = jax.nn.softmax(s, axis=-1).astype(v.dtype)
    return jnp.einsum('bhqk,bkhd->bqhd', p, v).reshape(B, L, NA_CH)

def neighbourhood_attention(q, k, v, k_ctx, v_ctx, rpb):
    B, S = q.shape[:2]
    rows = S // GRID_W
    kh = min(NA_KH_MAX, rows)
    nj = GRID_W // NA_QC
    scale = NA_HEAD_DIM ** -0.5
    qg = q.reshape(B, rows, GRID_W, NA_HEADS, NA_HEAD_DIM)
    kg = k.reshape(B, rows, GRID_W, NA_HEADS, NA_HEAD_DIM)
    vg = v.reshape(B, rows, GRID_W, NA_HEADS, NA_HEAD_DIM)
    qcol = jnp.arange(GRID_W).reshape(nj, NA_QC)
    band0 = jnp.clip(jnp.arange(nj) * NA_QC - NA_KW // 2, 0, GRID_W - NA_KB)
    kcol = band0[:, None] + jnp.arange(NA_KB)
    cstart = jnp.clip(qcol - NA_KW // 2, 0, GRID_W - NA_KW)
    col_valid = (kcol[:, None, :] >= cstart[..., None]) & (kcol[:, None, :] < cstart[..., None] + NA_KW)
    col_off = kcol[:, None, :] - qcol[..., None] + NA_KW - 1
    n_loc = kh * NA_KB

    def row_block(r):
        rs = jnp.clip(r - kh // 2, 0, rows - kh)
        q_r = lax.dynamic_index_in_dim(qg, r, axis=1, keepdims=False).reshape(
            B, nj, NA_QC, NA_HEADS, NA_HEAD_DIM)
        k_b = lax.dynamic_slice_in_dim(kg, rs, kh, axis=1)[:, :, kcol]
        v_b = lax.dynamic_slice_in_dim(vg, rs, kh, axis=1)[:, :, kcol]
        row_off = rs + jnp.arange(kh) - r + NA_KH_MAX - 1
        bias = rpb[:, row_off[None, None, :, None], col_off[:, :, None, :]].astype(jnp.float32)
        bias = jnp.where(col_valid[None, :, :, None, :], bias, NEG_INF)
        s_loc = jnp.einsum('bjqhd,bijkhd->bhjqik', q_r, k_b,
                           preferred_element_type=jnp.float32) * scale + bias
        s_ctx = jnp.einsum('bjqhd,bchd->bhjqc', q_r, k_ctx,
                           preferred_element_type=jnp.float32) * scale
        s = jnp.concatenate([s_loc.reshape(B, NA_HEADS, nj, NA_QC, n_loc), s_ctx], axis=-1)
        p = jax.nn.softmax(s, axis=-1).astype(v.dtype)
        p_loc = p[..., :n_loc].reshape(B, NA_HEADS, nj, NA_QC, kh, NA_KB)
        o = (jnp.einsum('bhjqik,bijkhd->bjqhd', p_loc, v_b)
             + jnp.einsum('bhjqc,bchd->bjqhd', p[..., n_loc:], v_ctx))
        return o.reshape(B, GRID_W, NA_CH)

    out = lax.map(row_block, jnp.arange(rows))
    return out.transpose(1, 0, 2, 3).reshape(B, S, NA_CH)

def heads(t):
    return t.reshape(t.shape[0], t.shape[1], NA_HEADS, NA_HEAD_DIM)

def first_inputs(seed: int = 0) -> dict:
    key = jax.random.key(seed)
    ks = jax.random.split(key, 16)
    f32 = jnp.float32
    nrm = lambda k, shape, s: jax.random.normal(k, shape, f32) * s
    return {
        'x': nrm(ks[0], (BATCH, SEQ, D_MODEL), 1.0),
        'c': nrm(ks[1], (BATCH, D_MODEL), 1.0),
        'ctx': nrm(ks[2], (BATCH, CTX_LEN, D_MODEL), 1.0),
        'c_ctx': nrm(ks[3], (D_MODEL,), 1.0),
        'w_mod': nrm(ks[4], (DEPTH, D_MODEL, N_MOD * D_MODEL), 0.5 * D_MODEL ** -0.5),
        'b_mod': nrm(ks[5], (DEPTH, N_MOD * D_MODEL), 0.01),
        'norm_g': 1.0 + nrm(ks[6], (DEPTH, 3, D_MODEL), 0.02),
        'ffn_w_in': nrm(ks[7], (DEPTH, 2, D_MODEL, 2 * D_FF), D_MODEL ** -0.5),
        'ffn_w_out': nrm(ks[8], (DEPTH, 2, D_FF, D_MODEL), D_FF ** -0.5),
        'w_in': nrm(ks[9], (DEPTH, D_MODEL, D_IN), D_MODEL ** -0.5),
        'conv_w': nrm(ks[10], (DEPTH, CONV_K, CONV_CH), CONV_K ** -0.5),
        'pool_w': nrm(ks[11], (DEPTH, len(POOL_WINDOWS), POOL_GROUP, POOL_GROUP), POOL_GROUP ** -0.5),
        'pool_scale': 1.0 + nrm(ks[12], (DEPTH, POOL_CH), 0.1),
        'rpb': nrm(ks[13], (DEPTH, NA_HEADS, 2 * NA_KH_MAX - 1, 2 * NA_KW - 1), 0.1),
        'w_out': nrm(ks[14], (DEPTH, D_MIX, D_MODEL), D_MIX ** -0.5),
        'final_g': 1.0 + nrm(ks[15], (D_MODEL,), 0.02),
    }

def first_block(x, c, ctx, c_ctx, w_mod, b_mod, norm_g, ffn_w_in, ffn_w_out, w_in,
              conv_w, pool_w, pool_scale, rpb, w_out, final_g):
    B = x.shape[0]
    xc = ctx
    for l in range(DEPTH):
        last = l == DEPTH - 1
        m = (jax.nn.silu(c) @ w_mod[l] + b_mod[l]).reshape(B, N_MOD, D_MODEL)
        mc = (jax.nn.silu(c_ctx) @ w_mod[l] + b_mod[l]).reshape(1, N_MOD, D_MODEL)

        x = ffn_sublayer(x, m, 0, norm_g[l, 0], ffn_w_in[l, 0], ffn_w_out[l, 0])
        xc = ffn_sublayer(xc, mc, 0, norm_g[l, 0], ffn_w_in[l, 0], ffn_w_out[l, 0])

        h = mod_norm(x, m, 1, norm_g[l, 1])
        hc = mod_norm(xc, mc, 1, norm_g[l, 1])
        u = h @ w_in[l]
        if last:
            uc_kv = hc @ w_in[l][:, OFF_K:]
            kc, vc = heads(uc_kv[..., :NA_CH]), heads(uc_kv[..., NA_CH:])
        else:
            uc = hc @ w_in[l]
            kc, vc = heads(uc[..., OFF_K:OFF_V]), heads(uc[..., OFF_V:])
            yc = jnp.concatenate([
                gated_conv_mixer(uc[..., :OFF_B], uc[..., OFF_B:OFF_C], uc[..., OFF_C:OFF_P], conv_w[l]),
                multiscale_pool_mixer(uc[..., OFF_P:OFF_Q], pool_w[l], pool_scale[l]),
                context_attention(heads(uc[..., OFF_Q:OFF_K]), kc, vc),
            ], axis=-1) @ w_out[l]
            xc = xc + mc[:, 5, None] * yc
            xc = ffn_sublayer(xc, mc, 2, norm_g[l, 2], ffn_w_in[l, 1], ffn_w_out[l, 1])
        y = jnp.concatenate([
            gated_conv_mixer(u[..., :OFF_B], u[..., OFF_B:OFF_C], u[..., OFF_C:OFF_P], conv_w[l]),
            multiscale_pool_mixer(u[..., OFF_P:OFF_Q], pool_w[l], pool_scale[l]),
            neighbourhood_attention(heads(u[..., OFF_Q:OFF_K]), heads(u[..., OFF_K:OFF_V]),
                                    heads(u[..., OFF_V:]), kc, vc, rpb[l]),
        ], axis=-1) @ w_out[l]
        x = x + m[:, 5, None] * y

        x = ffn_sublayer(x, m, 2, norm_g[l, 2], ffn_w_in[l, 1], ffn_w_out[l, 1])
    return rms_norm(x, final_g)


HEAD_DIM = 64
SWA_Q_HEADS = 8
SWA_KV_HEADS = 2
SWA_WINDOW = 128
SB_HEADS = 8
SB_Q_BLOCK = 128
MOBA_HEADS = 8
MOBA_BLOCK = 256
MOBA_TOPK = 3
MOBA_Q_CHUNK = 16
BRANCH_WIDTH = 512
N_BRANCHES = 3
D_FF_2 = 2816
CONV_WIDTH = 3
ROPE_THETA = 10000.0

IN_SIZES = (
    SWA_Q_HEADS * HEAD_DIM, SWA_KV_HEADS * HEAD_DIM, SWA_KV_HEADS * HEAD_DIM,
    SB_HEADS * HEAD_DIM, SB_HEADS * HEAD_DIM, SB_HEADS * HEAD_DIM,
    MOBA_HEADS * HEAD_DIM, MOBA_HEADS * HEAD_DIM, MOBA_HEADS * HEAD_DIM,
    N_BRANCHES * D_MODEL,
)
D_IN_2 = sum(IN_SIZES)


def rmsnorm(x, g):
    xf = x.astype(jnp.float32)
    y = xf * lax.rsqrt(jnp.mean(xf * xf, axis=-1, keepdims=True) + RMS_EPS)
    return (y * g.astype(jnp.float32)).astype(x.dtype)

def rope_tables(seq):
    inv = ROPE_THETA ** (-jnp.arange(0, HEAD_DIM, 2, dtype=jnp.float32) / HEAD_DIM)
    ang = jnp.arange(seq, dtype=jnp.float32)[:, None] * inv[None, :]
    return jnp.cos(ang), jnp.sin(ang)

def apply_rope(x, cos, sin):
    x1, x2 = jnp.split(x.astype(jnp.float32), 2, axis=-1)
    c = cos[None, :, None, :]
    s = sin[None, :, None, :]
    return jnp.concatenate([x1 * c - x2 * s, x2 * c + x1 * s], axis=-1).astype(x.dtype)

def swa_sink_attention(q, k, v, sinks):
    B, S = q.shape[0], q.shape[1]
    W = SWA_WINDOW
    nblk = S // W
    G = SWA_Q_HEADS // SWA_KV_HEADS
    scale = HEAD_DIM ** -0.5
    qb = q.reshape(B, nblk, W, SWA_KV_HEADS, G, HEAD_DIM)
    kb = k.reshape(B, nblk, W, SWA_KV_HEADS, HEAD_DIM)
    vb = v.reshape(B, nblk, W, SWA_KV_HEADS, HEAD_DIM)
    pad = ((0, 0), (1, 0), (0, 0), (0, 0), (0, 0))
    kk = jnp.concatenate([jnp.pad(kb, pad)[:, :-1], kb], axis=2)
    vv = jnp.concatenate([jnp.pad(vb, pad)[:, :-1], vb], axis=2)
    scores = jnp.einsum('bnqhgd,bnkhd->bnhgqk', qb, kk).astype(jnp.float32) * scale
    qpos = jnp.arange(W)[:, None] + W
    kpos = jnp.arange(2 * W)[None, :]
    diff = qpos - kpos
    band = (diff >= 0) & (diff < W)
    blk = jnp.arange(nblk)[:, None, None]
    valid = band[None] & ((blk * W + kpos[None] - W) >= 0)
    scores = jnp.where(valid[None, :, None, None], scores, -jnp.inf)
    sink = sinks.astype(jnp.float32).reshape(SWA_KV_HEADS, G)[None, None, :, :, None, None]
    sink = jnp.broadcast_to(sink, scores.shape[:-1] + (1,))
    probs = jax.nn.softmax(jnp.concatenate([scores, sink], axis=-1), axis=-1)[..., :-1]
    out = jnp.einsum('bnhgqk,bnkhd->bnqhgd', probs.astype(v.dtype), vv)
    return out.reshape(B, S, SWA_Q_HEADS * HEAD_DIM)

def stick_breaking_attention(q, k, v):
    B, S, H, dh = q.shape
    nblk = S // SB_Q_BLOCK
    scale = dh ** -0.5
    q_blocks = q.reshape(B, nblk, SB_Q_BLOCK, H, dh).transpose(1, 0, 2, 3, 4)
    kpos = jnp.arange(S)

    def block(args):
        q_blk, i = args
        z = jnp.einsum('bqhd,bkhd->bhqk', q_blk, k).astype(jnp.float32) * scale
        qpos = i * SB_Q_BLOCK + jnp.arange(SB_Q_BLOCK)
        past = kpos[None, :] < qpos[:, None]
        log_beta = jax.nn.log_sigmoid(z)
        log_one_minus = jnp.where(past, jax.nn.log_sigmoid(-z), 0.0)
        remain = lax.cumsum(log_one_minus, axis=3, reverse=True) - log_one_minus
        w = jnp.where(past, jnp.exp(log_beta + remain), 0.0)
        return jnp.einsum('bhqk,bkhd->bqhd', w.astype(v.dtype), v)

    out = lax.map(block, (q_blocks, jnp.arange(nblk)))
    return out.transpose(1, 0, 2, 3, 4).reshape(B, S, H * dh)

def moba_attention(q, k, v):
    B, S, H, dh = q.shape
    nb = -(-S // MOBA_BLOCK)
    pad = nb * MOBA_BLOCK - S
    ksel = min(MOBA_TOPK, nb)
    scale = dh ** -0.5
    kp = jnp.pad(k, ((0, 0), (0, pad), (0, 0), (0, 0)))
    vp = jnp.pad(v, ((0, 0), (0, pad), (0, 0), (0, 0)))
    kb = kp.reshape(B, nb, MOBA_BLOCK, H, dh)
    vb = vp.reshape(B, nb, MOBA_BLOCK, H, dh)
    k_mean = jnp.mean(kb.astype(jnp.float32), axis=2)
    gate = jnp.einsum('bshd,bnhd->bhsn', q.astype(jnp.float32), k_mean)
    q_blk = jnp.arange(S) // MOBA_BLOCK
    past_blk = jnp.arange(nb)[None, :] < q_blk[:, None]
    gate = jnp.where(past_blk[None, None], gate, -jnp.inf)
    _, sel = lax.top_k(gate, ksel)
    sel_valid = sel < q_blk[None, None, :, None]

    C = MOBA_Q_CHUNK
    nchunk = S // C
    q_c = q.reshape(B, nchunk, C, H, dh).transpose(1, 0, 2, 3, 4)
    sel_c = sel.reshape(B, H, nchunk, C, ksel).transpose(2, 0, 1, 3, 4)
    valid_c = sel_valid.reshape(B, H, nchunk, C, ksel).transpose(2, 0, 1, 3, 4)
    kb_h = kb.transpose(0, 3, 1, 2, 4)
    vb_h = vb.transpose(0, 3, 1, 2, 4)
    gather = jax.vmap(jax.vmap(lambda blocks, idx: blocks[idx]))

    def chunk(args):
        q_blk, sel_blk, valid_blk, i = args
        t0 = i * C
        qpos = t0 + jnp.arange(C)
        own_start = (t0 // MOBA_BLOCK) * MOBA_BLOCK
        k_own = lax.dynamic_slice_in_dim(kp, own_start, MOBA_BLOCK, axis=1)
        v_own = lax.dynamic_slice_in_dim(vp, own_start, MOBA_BLOCK, axis=1)
        k_sel = gather(kb_h, sel_blk)
        v_sel = gather(vb_h, sel_blk)
        s_sel = jnp.einsum('bqhd,bhqnkd->bhqnk', q_blk, k_sel).astype(jnp.float32) * scale
        s_sel = jnp.where(valid_blk[..., None], s_sel, -jnp.inf).reshape(B, H, C, ksel * MOBA_BLOCK)
        s_own = jnp.einsum('bqhd,bkhd->bhqk', q_blk, k_own).astype(jnp.float32) * scale
        kpos_own = own_start + jnp.arange(MOBA_BLOCK)
        s_own = jnp.where(kpos_own[None, :] <= qpos[:, None], s_own, -jnp.inf)
        p = jax.nn.softmax(jnp.concatenate([s_sel, s_own], axis=-1), axis=-1)
        p_sel = p[..., :ksel * MOBA_BLOCK].reshape(B, H, C, ksel, MOBA_BLOCK).astype(v.dtype)
        p_own = p[..., ksel * MOBA_BLOCK:].astype(v.dtype)
        return (jnp.einsum('bhqnk,bhqnkd->bqhd', p_sel, v_sel)
                + jnp.einsum('bhqk,bkhd->bqhd', p_own, v_own))

    out = lax.map(chunk, (q_c, sel_c, valid_c, jnp.arange(nchunk)))
    return out.transpose(1, 0, 2, 3, 4).reshape(B, S, H * dh)

def causal_depthwise_conv(u, w, b):
    S = u.shape[1]
    up = jnp.pad(u, ((0, 0), (CONV_WIDTH - 1, 0), (0, 0)))
    out = b
    for tap in range(CONV_WIDTH):
        out = out + w[tap] * up[:, tap:tap + S]
    return out

def hybrid_layer(x, cos, sin, norm_mix, w_in, b_gate, sinks, w_branch, w_out,
                 norm_ffn, w_up, conv_w, conv_b, w_down):
    B, S, _ = x.shape
    h = rmsnorm(x, norm_mix)
    proj = h @ w_in
    points = np.cumsum(IN_SIZES)[:-1].tolist()
    qa, ka, va, qb, kb, vb, qc, kc, vc, gates = jnp.split(proj, points, axis=-1)
    heads = lambda t, n: t.reshape(B, S, n, HEAD_DIM)
    o_a = swa_sink_attention(apply_rope(heads(qa, SWA_Q_HEADS), cos, sin),
                             apply_rope(heads(ka, SWA_KV_HEADS), cos, sin),
                             heads(va, SWA_KV_HEADS), sinks)
    o_b = stick_breaking_attention(heads(qb, SB_HEADS), heads(kb, SB_HEADS), heads(vb, SB_HEADS))
    o_c = moba_attention(apply_rope(heads(qc, MOBA_HEADS), cos, sin),
                         apply_rope(heads(kc, MOBA_HEADS), cos, sin),
                         heads(vc, MOBA_HEADS))
    g = jax.nn.sigmoid(gates.reshape(B, S, N_BRANCHES, D_MODEL) + b_gate.reshape(N_BRANCHES, D_MODEL))
    merged = (g[:, :, 0] * (o_a @ w_branch[0])
              + g[:, :, 1] * (o_b @ w_branch[1])
              + g[:, :, 2] * (o_c @ w_branch[2]))
    x = x + merged @ w_out
    h = rmsnorm(x, norm_ffn)
    u = causal_depthwise_conv(h @ w_up, conv_w, conv_b)
    u_a, u_v = jnp.split(u, 2, axis=-1)
    return x + (jax.nn.silu(u_a) * u_v) @ w_down

def second_inputs(seed: int = 0) -> dict:
    key = jax.random.key(seed)
    ks = jax.random.split(key, 13)
    f32 = jnp.float32
    nrm = lambda k, shape, s: jax.random.normal(k, shape, f32) * s
    return {
        "x": nrm(ks[0], (BATCH, SEQ, D_MODEL), 1.0),
        "norm_mix": 1.0 + nrm(ks[1], (DEPTH, D_MODEL), 0.02),
        "w_in": nrm(ks[2], (DEPTH, D_MODEL, D_IN_2), D_MODEL ** -0.5),
        "b_gate": nrm(ks[3], (DEPTH, N_BRANCHES * D_MODEL), 0.1),
        "sinks": nrm(ks[4], (DEPTH, SWA_Q_HEADS), 0.5),
        "w_branch": nrm(ks[5], (DEPTH, N_BRANCHES, BRANCH_WIDTH, D_MODEL), BRANCH_WIDTH ** -0.5),
        "w_out": nrm(ks[6], (DEPTH, D_MODEL, D_MODEL), D_MODEL ** -0.5),
        "norm_ffn": 1.0 + nrm(ks[7], (DEPTH, D_MODEL), 0.02),
        "w_up": nrm(ks[8], (DEPTH, D_MODEL, 2 * D_FF_2), D_MODEL ** -0.5),
        "conv_w": nrm(ks[9], (DEPTH, CONV_WIDTH, 2 * D_FF_2), CONV_WIDTH ** -0.5),
        "conv_b": nrm(ks[10], (DEPTH, 2 * D_FF_2), 0.01),
        "w_down": nrm(ks[11], (DEPTH, D_FF_2, D_MODEL), D_FF_2 ** -0.5),
        "norm_final": 1.0 + nrm(ks[12], (D_MODEL,), 0.02),
    }

def second_block(x, norm_mix, w_in, b_gate, sinks, w_branch, w_out, norm_ffn,
              w_up, conv_w, conv_b, w_down, norm_final):
    cos, sin = rope_tables(x.shape[1])
    for layer in range(DEPTH):
        x = hybrid_layer(x, cos, sin, norm_mix[layer], w_in[layer], b_gate[layer],
                         sinks[layer], w_branch[layer], w_out[layer], norm_ffn[layer],
                         w_up[layer], conv_w[layer], conv_b[layer], w_down[layer])
    return rmsnorm(x, norm_final)


def setup_inputs(seed=0):
    out = dict(first_inputs(seed))
    for name, value in second_inputs(seed + 1).items():
        if name != "x":
            out[name + "_2"] = value
    return out


def reference(
    x, c, ctx, c_ctx, w_mod, b_mod, norm_g, ffn_w_in, ffn_w_out, w_in, conv_w, pool_w,
    pool_scale, rpb, w_out, final_g, norm_mix_2, w_in_2, b_gate_2, sinks_2, w_branch_2, w_out_2,
    norm_ffn_2, w_up_2, conv_w_2, conv_b_2, w_down_2, norm_final_2,
):
    x = first_block(
        x, c, ctx, c_ctx, w_mod, b_mod, norm_g, ffn_w_in, ffn_w_out, w_in, conv_w, pool_w,
        pool_scale, rpb, w_out, final_g,
    )
    return second_block(
        x, norm_mix_2, w_in_2, b_gate_2, sinks_2, w_branch_2, w_out_2, norm_ffn_2, w_up_2,
        conv_w_2, conv_b_2, w_down_2, norm_final_2,
    )


_drawn_inputs = setup_inputs


def setup_inputs(seed=0):
    import zlib

    import numpy as np

    out = dict(_drawn_inputs(seed))
    spreads = {}
    factors = {'b_mod': 2.696,
     'norm_g': 3.592,
     'rpb': 8.0,
     'norm_mix_2': 3.762,
     'sinks_2': 7.261,
     'norm_ffn_2': 2.798,
     'conv_b_2': 5.707,
     'norm_final_2': 2.822}
    for name, (base, spread) in spreads.items():
        noise = np.random.default_rng([zlib.crc32(name.encode()), seed]).standard_normal(out[name].shape)
        drawn = base * np.exp(spread * noise) if base else spread * noise
        out[name] = __import__('jax').numpy.asarray(drawn.astype(out[name].dtype))
    for name, factor in factors.items():
        out[name] = (out[name] * factor).astype(out[name].dtype)
    return out
```

```python
import concourse.bass as bass
from concourse import mybir
from contextlib import ExitStack
import numpy as np

F32 = mybir.dt.float32
F32R = mybir.dt.float32r
ALU = mybir.AluOpType
ACT = mybir.ActivationFunctionType
AX = mybir.AxisListType
P = 128
D = 1024
KD = D // P
S = 256
DEPTH = 2
DFF = 2816
FT = DFF // P
THIRDS = (8, 8, 6)
EPS = 1e-6
NEG = -1e30
HD = 64
SCALE = HD ** -0.5
N_IN = 20
N_QKV = 30
N_GATE = 24
SLOTS = 4
AHEAD = 3
ROLL = 15 * 31


def constant_table():
    parts = {}
    row = np.arange(P)
    parts["ident"] = np.eye(P)
    rot = np.zeros((P, P))
    for m in range(P):
        if m % HD < HD // 2:
            rot[m + HD // 2, m] = -1.0
        else:
            rot[m - HD // 2, m] = 1.0
    parts["rot"] = rot
    parts["turn"] = (row[:, None] // 64 * 64 + 63 - row[:, None] % 64 == row[None, :]).astype(float)
    parts["tri"] = (row[:, None] >= row[None, :]).astype(float)
    inv = (np.float32(10000.0) ** (-np.arange(0, HD, 2, dtype=np.float32) / np.float32(HD))).astype(np.float32)
    ang = np.arange(S, dtype=np.float32)[None, :] * inv[row % (HD // 2)][:, None]
    parts["cos"] = np.cos(ang.astype(np.float32))
    parts["sin"] = np.sin(ang.astype(np.float32))
    causal = np.where(row[None, :] <= row[:, None], 0.0, NEG)
    parts["m_causal"] = np.concatenate([causal, np.zeros((P, P)), causal], 1)
    parts["m_band"] = np.concatenate([causal, np.where(row[None, :] > row[:, None], 0.0, NEG), causal], 1)
    past = np.where(row[:, None] < row[None, :], 0.0, NEG)
    parts["m_past"] = np.concatenate([past, np.zeros((P, P)), past], 1)
    qcol, kcol = row % 64, np.arange(64)
    start = np.clip(qcol - 8, 0, 48)[:, None]
    ok = (kcol[None, :] >= start) & (kcol[None, :] < start + 16)
    parts["m_near"] = np.where(ok, 3.0e38, NEG)
    t = np.arange(S)
    cnt = np.zeros((P, 2, S))
    for g, w in enumerate((2, 4, 8, 16)):
        lo, hi = np.clip(t - w // 2, 0, S), np.clip(t + w - w // 2, 0, S)
        cnt[HD * (g % 2):HD * (g % 2) + HD, g // 2, :] = 1.0 / (hi - lo).astype(np.float32)
    parts["inv_count"] = cnt.reshape(P, 2 * S)
    at, cols = 0, {}
    for name, a in parts.items():
        cols[name] = (at, at + a.shape[1])
        at += a.shape[1]
    return np.concatenate([a.astype(np.float32) for a in parts.values()], 1), cols


CONSTS, CONST_COLS = constant_table()


class Phase:

    def __init__(self, kind, n, k, width, source, start, view="std", **more):
        self.kind, self.n, self.k, self.width, self.source, self.start, self.view = kind, n, k, width, source, start, view
        self.more = more


def build_program(nc, x, c, ctx, c_ctx, w_mod, b_mod, norm_g, ffn_w_in, ffn_w_out, w_in, conv_w, pool_w,
                  pool_scale, rpb, w_out, final_g, norm_mix_2, w_in_2, b_gate_2, sinks_2, w_branch_2,
                  w_out_2, norm_ffn_2, w_up_2, conv_w_2, conv_b_2, w_down_2, norm_final_2, consts, out):
    K = 1024
    base = 17 * K
    region = {}
    at = base
    for name, size in (("x", 16 * K), ("h", 32 * K), ("g", 40 * K), ("raw", 16 * K), ("hi", 16 * K), ("lo", 16 * K),
                       ("mod_raw", 16 * K), ("bias", 12 * K), ("vt", 9 * K + 256), ("scr", 16 * K)):
        region[name] = at
        at += size
    top = [at]

    def fixed(name, shape, dt, offset):
        return nc.alloc_sbuf_tensor_at(name, shape, dt, offset=offset)

    def small(name, shape, dt=F32):
        t = fixed(name, shape, dt, top[0])
        top[0] += (int(np.prod(shape[1:])) * 4 + 31) // 32 * 32
        return t

    X = fixed("X", [P, KD, 512], F32, region["x"])
    H_hi = fixed("H_hi", [P, KD, 512], F32R, region["h"])
    H_lo = fixed("H_lo", [P, KD, 512], F32R, region["h"] + 16 * K)
    G_hi = fixed("G_hi", [P, 8, 512], F32R, region["g"])
    G_lo = fixed("G_lo", [P, 8, 512], F32R, region["g"] + 16 * K)
    U = fixed("U", [P, N_IN, 512], F32, region["g"])
    T1 = fixed("T1", [P, KD, 512], F32, region["g"])
    pool_a = fixed("pool_a", [P, 2, 280], F32, region["h"] + 8 * K)
    pool_b = fixed("pool_b", [P, 2, 280], F32, region["h"] + 8 * K + 2240)
    pool_c = fixed("pool_c", [P, 2, S], F32, region["h"] + 8 * K + 4480)
    tokens_in = fixed("tokens_in", [P, 4, D], F32, region["g"])
    rows_in = fixed("rows_in", [P, 6, P], F32, region["g"] + 16 * K)
    bias_t = fixed("bias_t", [P, 8, 6, 64], F32, region["bias"])
    mod_raw = fixed("mod_raw", [P, 2, KD, 256], F32, region["mod_raw"])
    X2 = fixed("X2", [P, KD, S], F32, region["x"])
    gates = fixed("gates", [P, N_GATE, S], F32, region["x"] + 8 * K)
    H2_hi = fixed("H2_hi", [P, KD, S], F32R, region["x"] + 32 * K)
    H2_lo = fixed("H2_lo", [P, KD, S], F32R, region["x"] + 40 * K)
    U2 = fixed("U2", [P, N_QKV, S], F32, region["g"])
    merged = fixed("merged", [P, KD, S], F32, region["g"] + 30 * K)
    T2 = fixed("T2", [P, KD, S], F32, region["g"])
    G2_hi = fixed("G2_hi", [P, 8, S], F32R, region["g"])
    G2_lo = fixed("G2_lo", [P, 8, S], F32R, region["g"] + 8 * K)
    O_hi = fixed("O_hi", [P, 12, S], F32R, region["mod_raw"])
    O_lo = fixed("O_lo", [P, 12, S], F32R, region["mod_raw"] + 12 * K)
    tokens_out = fixed("tokens_out", [P, 2, D], F32, region["g"] + 16 * K)
    raw = fixed("raw", [P, 2, 2048], F32, region["raw"])
    w_hi = fixed("w_hi", [P, SLOTS, 1024], F32R, region["hi"])
    w_lo = fixed("w_lo", [P, SLOTS, 1024], F32R, region["lo"])
    vt = fixed("vt", [P, 9 * S], F32, region["vt"])
    probs = fixed("probs", [P, 4, 512], F32, region["scr"])
    probs_t = fixed("probs_t", [P, 2, 1024], F32, region["scr"] + 8 * K)
    sil = fixed("sil", [P, 2, 512], F32, region["scr"])
    g32 = fixed("g32", [P, 2, 512], F32, region["scr"] + 4 * K)
    sq = fixed("sq", [P, 512], F32, region["scr"] + 8 * K)
    sq_sum = fixed("sq_sum", [P, 512], F32, region["scr"] + 10 * K)
    rstd = fixed("rstd", [P, 512], F32, region["scr"] + 12 * K)
    sb_z = fixed("sb_z", [P, 2, 384], F32, region["scr"])
    sb_e = fixed("sb_e", [P, 2, 384], F32, region["scr"] + 3 * K)
    sb_s = fixed("sb_s", [P, 2, 384], F32, region["scr"] + 6 * K)
    sb_w = fixed("sb_w", [P, 2, 384], F32, region["scr"] + 9 * K)
    k_swap = fixed("k_swap", [P, S], F32, region["scr"] + 14 * K)
    rope_t = fixed("rope_t", [P, 2, S], F32, region["scr"] + 12 * K)

    const = small("const", [P, CONSTS.shape[1]])
    ones = small("ones", [P, P])
    eps = small("eps", [P, 1])
    silu_c = small("silu_c", [P, KD, 2])
    modv = small("modv", [P, 6, 3, KD, 2])
    neg_max = small("neg_max", [P, 16])
    row_sum = small("row_sum", [P, 16])
    row_inv = small("row_inv", [P, 16])
    sink = small("sink", [P, DEPTH * 8])
    sink_e = small("sink_e", [P, 16])
    pool_bd = small("pool_bd", [P, 2, P])
    vec_rows, vec_at = [], {}

    def rows(name, ap):
        vec_at[name] = sum(a.shape[0] for a in vec_rows)
        vec_rows.append(ap)

    rows("c", c.rearrange("b (n p) -> (b n) p", p=P))
    rows("c_ctx", c_ctx.rearrange("(n p) -> n p", p=P))
    rows("b_mod", b_mod.rearrange("l (n p) -> (l n) p", p=P))
    rows("norm_g", norm_g.rearrange("l i (n p) -> (l i n) p", p=P))
    rows("final_g", final_g.rearrange("(n p) -> n p", p=P))
    rows("conv_w", conv_w.rearrange("l w (n p) -> (l w n) p", p=P))
    rows("pool_scale", pool_scale.rearrange("l (n p) -> (l n) p", p=P))
    rows("norm_mix", norm_mix_2.rearrange("l (n p) -> (l n) p", p=P))
    rows("b_gate", b_gate_2.rearrange("l (n p) -> (l n) p", p=P))
    rows("norm_ffn", norm_ffn_2.rearrange("l (n p) -> (l n) p", p=P))
    rows("conv_w_2", conv_w_2.rearrange("l w (n p) -> (l w n) p", p=P))
    rows("conv_b_2", conv_b_2.rearrange("l (n p) -> (l n) p", p=P))
    rows("norm_final", norm_final_2.rearrange("(n p) -> n p", p=P))
    n_rows = sum(a.shape[0] for a in vec_rows)
    n_row_tiles = (n_rows + P - 1) // P
    assert n_row_tiles <= 6, n_rows
    vecs = small("vecs", [P, n_row_tiles * P])
    assert top[0] <= nc.sbuf_usable_end, (top[0], nc.sbuf_usable_end)

    row_pieces = []
    r = 0
    for ap in vec_rows:
        done = 0
        while done < ap.shape[0]:
            n = min(ap.shape[0] - done, P - r % P)
            row_pieces.append((r % P, r // P, n, ap[done:done + n, :]))
            done += n
            r += n

    def vec(name, index, n=1):
        i = vec_at[name] + index
        return vecs[:, bass.ds(i, n)] if not isinstance(i, int) else vecs[:, i:i + n]

    def table(name):
        a, b = CONST_COLS[name]
        return const[:, a:b]

    ident, rot, tri = table("ident"), table("rot"), table("tri")

    bank = [nc.alloc_psum_tensor(f"bank{b}", [P, 512], F32) for b in range(8)]
    STAT = bank[4]

    def sem(name):
        return nc.alloc_semaphore(name)

    raw_in = [sem("raw_in0"), sem("raw_in1")]
    mod_in = [sem("mod_in0"), sem("mod_in1")]
    s_const = sem("s_const")
    s_rows = sem("s_rows")
    s_tok = sem("s_tok")
    s_bias = sem("s_bias")
    s_small = sem("s_small")
    s_out = sem("s_out")
    hi_done = sem("hi_done")
    lo_done = sem("lo_done")
    acc_done = sem("acc_done")
    acc_free = sem("acc_free")
    mod_done = sem("mod_done")
    mod_ready = sem("mod_ready")
    mod_step = sem("mod_step")
    silu_done = sem("silu_done")
    g_hi_done = sem("g_hi_done")
    g_lo_done = sem("g_lo_done")
    conv1_done = sem("conv1_done")
    g_mul_done = sem("g_mul_done")
    conv0_done = sem("conv0_done")
    sq_step = sem("sq_step")
    stat_done = sem("stat_done")
    rms_done = sem("rms_done")
    rstd_done = sem("rstd_done")
    n_mul = sem("n_mul")
    n_aff = sem("n_aff")
    h_hi_done = sem("h_hi_done")
    h_lo_done = sem("h_lo_done")
    memset_done = sem("memset_done")
    init_t = sem("init_t")
    init_copy = sem("init_copy")
    silu_c_done = sem("silu_c_done")
    bias_done = sem("bias_done")
    bias_pe = sem("bias_pe")
    mix_pe = sem("mix_pe")
    mix_act = sem("mix_act")
    mix_dve = sem("mix_dve")
    vt_t = sem("vt_t")
    vt_copy = sem("vt_copy")
    sc_done = sem("sc_done")
    bias_add = sem("bias_add")
    max_step = sem("max_step")
    max_done = sem("max_done")
    exp_done = sem("exp_done")
    inv_step = sem("inv_step")
    p_ready = sem("p_ready")
    pt_done = sem("pt_done")
    pt_copy = sem("pt_copy")
    pv_done = sem("pv_done")
    o_step = sem("o_step")
    o_done = sem("o_done")
    sb_pe = sem("sb_pe")
    sb_dve = sem("sb_dve")
    sb_act = sem("sb_act")
    rope_pe = sem("rope_pe")
    rope_dve = sem("rope_dve")
    rope_pool = sem("rope_pool")
    gate_done = sem("gate_done")
    k_swap_done = sem("k_swap_done")
    merge_step = sem("merge_step")
    final_mul = sem("final_mul")
    final_t = sem("final_t")
    final_copy = sem("final_copy")
    s_store = sem("s_store")

    plan = []
    units = [0]
    hidden = [0]
    splits = [0]
    GLU_TILES = 2 * DEPTH * FT

    def gemm(kind, n, k, width, source, view="std", **more):
        ph = Phase(kind, n, k, width, source, units[0], view, **more)
        ph.g0 = hidden[0]
        ph.gm0 = hidden[0] - GLU_TILES
        ph.h0 = splits[0] - KD
        if kind == "branch":
            ph.merge0 = 8 * ph.more["layer"]
            ph.h0 = splits[0]
            splits[0] += KD
        if kind in ("glu", "conv_glu"):
            hidden[0] += n // 2
        units[0] += n
        plan.append(("gemm", ph))
        return ph

    n_norm = [0]
    affines = [0]

    def norm(kind, **more):
        nm = dict(kind=kind, r=n_norm[0], h0=splits[0], a0=affines[0], **more)
        if kind in ("mod", "plain"):
            splits[0] += KD
            affines[0] += KD
        plan.append(("norm", nm))
        n_norm[0] += 1

    def kpc(w2d):
        return w2d.rearrange("(k p) c -> p k c", p=P)

    def pair_source(w, third):
        view = kpc(w)

        def source(j, half):
            return view[:, :, bass.ds(half * DFF + third * 1024 + j * 256, 256)]
        return source

    def plain_source(w, col0=0, k0=0, k=KD):
        view = kpc(w)

        def source(cidx):
            return view[:, k0:k0 + k, bass.ds(col0 + cidx * 256, 256)]
        return source

    def ffn(width, w1, w2, seg, stats, conv_layer=None):
        for third, tiles in enumerate(THIRDS):
            gemm("glu" if conv_layer is None else "conv_glu", 2 * tiles, KD, width, pair_source(w1, third),
                 pair=True, layer=conv_layer, third=third, norm=n_norm[0] - 1)
            gemm("residual", KD, tiles, width, plain_source(w2, 0, third * 8, tiles), seg=seg,
                 stats=stats and third == 2, moving="g", norm_next=n_norm[0], hidden_end=hidden[0])

    n_mod = [0]
    atts = []
    n_mix = [0]

    for layer in range(DEPTH):
        last = layer == DEPTH - 1
        for i in range(3):
            plan.append(("mod", dict(seg=layer * 3 + i)))
        norm("mod", width=512, seg=layer * 3)
        ffn(512, ffn_w_in[layer, 0], ffn_w_out[layer, 0], layer * 3, True)
        norm("mod", width=512, seg=layer * 3 + 1)
        if last:
            gemm("store", 12, KD, S, plain_source(w_in[layer]), moving="h", dst="U", f0=0, norm=n_norm[0] - 1)
            gemm("store", 8, KD, 512, plain_source(w_in[layer], 1536), moving="h", dst="U", f0=12, norm=n_norm[0] - 1)
        else:
            gemm("store", N_IN, KD, 512, plain_source(w_in[layer]), moving="h", dst="U", f0=0, norm=n_norm[0] - 1)
        plan.append(("mixers", dict(layer=layer, streams=1 if last else 2, index=layer)))
        plan.append(("attend", dict(block=1, layer=layer, streams=1 if last else 2)))
        width = S if last else 512
        gemm("residual", KD, KD, width, plain_source(w_out[layer]), seg=layer * 3 + 1, stats=True, moving="y",
             norm_next=n_norm[0])
        norm("mod", width=width, seg=layer * 3 + 2)
        ffn(width, ffn_w_in[layer, 1], ffn_w_out[layer, 1], layer * 3 + 2, True)
    norm("renorm", gain=("final_g", 0))
    for layer in range(DEPTH):
        norm("plain", gain=("norm_mix", layer * KD))
        gemm("store", N_QKV, KD, S, plain_source(w_in_2[layer]), moving="h", dst="U2", f0=0, norm=n_norm[0] - 1)
        gemm("gate", N_GATE, KD, S, plain_source(w_in_2[layer], N_QKV * P), moving="h", layer=layer)
        plan.append(("attend", dict(block=2, layer=layer, streams=1)))
        br = w_branch_2[layer]

        def branch_source(cidx, br=br):
            return br[cidx // 2].rearrange("(k p) c -> p k c", p=P)[:, :, 512 * (cidx % 2):512 * (cidx % 2) + 512]
        gemm("branch", 12, 4, S, branch_source, view="branch", layer=layer)
        gemm("residual", KD, KD, S, plain_source(w_out_2[layer]), seg=None, stats=True, moving="merged",
             norm_next=n_norm[0])
        norm("plain", gain=("norm_ffn", layer * KD))
        ffn(S, w_up_2[layer], w_down_2[layer], None, True, conv_layer=layer)
    norm("final", gain=("norm_final", 0))
    total = units[0]
    phases = [p for kind, p in plan if kind == "gemm"]
    for a, b in zip(phases, phases[1:] + [None]):
        a.next = b
    unit_view = {}
    for ph in phases:
        for t in range(ph.start, ph.start + ph.n):
            unit_view[t] = ph.view

    calls = []

    def attention(**a):
        calls.append(a)
        return a

    counts = dict(group=0, seg=0, pair=0, head=0, vt=0, sb=0, rope=0)
    for kind, ph in plan:
        if kind != "attend":
            continue
        ph["vt0"] = counts["vt"]
        ph["calls"] = []
        b1 = ph["block"] == 1
        if b1:
            ph["vt_jobs"] = [(tile, 4) for tile in range(4)]
            todo = (["ctx"] if ph["streams"] == 2 else []) + ["near"]
        else:
            ph["vt_jobs"] = [(tile, 2) for tile in range(9)]
            todo = ["swa", "moba"]
        counts["vt"] += len(ph["vt_jobs"])
        ph["rope0"] = counts["rope"]
        if not b1:
            counts["rope"] += 13
        if not b1:
            ph["sb0"] = counts["sb"]
            counts["sb"] += 4
            ph["sb_pair0"] = counts["pair"]
            counts["pair"] += 4
        for what in todo:
            groups = []
            for head in range(8):
                if what == "near":
                    for qt in range(2):
                        groups.append(dict(head=head, segs=[(qt, 0, 512)], blocks=[(0, kb) for kb in range(4)],
                                           last=qt == 1, qt=qt))
                elif what == "ctx":
                    groups.append(dict(head=head, segs=[(0, 0, 256), (1, 256, 512)],
                                       blocks=[(256 * qt + 128 * kb, kb) for kb in range(2) for qt in range(2)],
                                       last=True, qt=None))
                else:
                    groups.append(dict(head=head, segs=[(0, 0, 128), (1, 128, 384)],
                                       blocks=[(0, 0), (128, 0), (256, 1)], last=True, qt=None))
            for g in groups:
                g["n"] = counts["group"]
                counts["group"] += 1
                g["seg0"] = counts["seg"]
                counts["seg"] += len(g["segs"])
            call = dict(what=what, groups=groups, pair0=counts["pair"], head0=counts["head"], layer=ph["layer"],
                        n0=groups[0]["n"])
            if b1:
                call.update(score_banks=[0, 1, 2, 3], pt_banks=[4, 5], out_banks=[6, 7])
            else:
                call.update(score_banks=[4, 5], pt_banks=[6], out_banks=[7])
            counts["pair"] += 4
            counts["head"] += 8
            ph["calls"].append(call)

    unit_at = mix_d = mix_a = mix_p = 0
    max_count = inv_count = 0
    mix_end = pairs_end = 0
    for kind, ph in plan:
        if kind == "gemm":
            unit_at = ph.start + ph.n
            ph.more["pairs"], ph.more["mix_end"] = pairs_end, mix_end
        elif kind == "mixers":
            n_s = ph["streams"]
            ph.update(dve0=mix_d, act0=mix_a, pe0=mix_p, unit_end=unit_at)
            at0 = mix_d + 1 + 4 * n_s + 3
            ph["d_z"] = mix_d + 1
            ph["d_pool"] = [at0 + 14 * s + 12 for s in range(n_s)]
            mix_end = mix_d = at0 + 14 * n_s
            mix_a += 4 * n_s
            mix_p += 2 * n_s
        elif kind == "attend":
            ph.update(unit_end=unit_at, mix_end=mix_end)
            for call in ph["calls"]:
                for g in call["groups"]:
                    max_count += call["what"] in ("ctx", "swa")
                    inv_count += 2 if call["what"] == "swa" else 1
                    g["max_count"], g["inv_count"] = max_count, inv_count
            pairs_end = ph["calls"][-1]["pair0"] + 4

    def attend_order(at_):
        if at_["block"] == 1:
            return [(call["what"], call) for call in at_["calls"]]
        return [("sb", None)] + [(call["what"], call) for call in at_["calls"]]

    def rope_tiles():
        return [0, 1, 2, 3, 4, 18, 19, 20, 21, 22, 23, 24, 25]

    def out_tiles(call, hp):
        what = call["what"]
        if what == "near":
            return H_hi[:, 4 + hp, 0:S], H_lo[:, 4 + hp, 0:S]
        if what == "ctx":
            return H_hi[:, 4 + hp, S:512], H_lo[:, 4 + hp, S:512]
        f = hp + (0 if what == "swa" else 8)
        return O_hi[:, f, :], O_lo[:, f, :]

    def out_of(call, hp):
        return bank[call["out_banks"][hp % len(call["out_banks"])]][:, 0:S]

    def moving_wait(ph, k):
        m = ph.more.get("moving", "h")
        if ph.kind == "branch" or m == "y":
            return None
        if m == "g":
            return g_lo_done, ph.more["hidden_end"] - ph.k + k + 1
        return h_lo_done, ph.h0 + k + 1

    def repeat(eng, n, body, peel_last=False):
        body(0, True, n == 1)
        stop = n - 1 if peel_last else n
        if stop > 2:
            with eng.Fori(1, stop) as i:
                body(i, False, False)
        elif stop == 2:
            body(1, False, n == 2)
        if peel_last and n > 1 and stop >= 1:
            body(n - 1, False, True)

    def at_least(eng, semaphore, value):
        if isinstance(value, int) and value <= 0:
            return
        eng.wait_ge(semaphore, value)

    def needs_peel(ph):
        return ph.next is None or ph.next.view != ph.view

    def half_view(tensor_ap, view, half):
        if view == "std":
            return tensor_ap.rearrange("p (k c) -> p k c", c=256)[:, :, half * P:half * P + P]
        return tensor_ap.rearrange("p (k c) -> p k c", c=512)[:, :, half * 256:half * 256 + 256]

    def slot_view(tensor_ap, view):
        return tensor_ap.rearrange("p (k c) -> p k c", c=P if view == "std" else 256)

    def phase_steps(ph):
        return ph.n // 4, ph.n % 4

    def moving_of(ph):
        m = ph.more.get("moving", "h")
        if ph.kind in ("glu",) or (m == "h" and ph.more.get("dst") == "U") or m == "y":
            return H_hi, H_lo
        if m == "g":
            return (G_hi, G_lo) if ph.more["seg"] is not None else (G2_hi, G2_lo)
        return H2_hi, H2_lo

    def q_tile(what):
        return dict(near=8, ctx=8, swa=0, sb=6, moba=18)[what]

    stack = ExitStack()
    blk = stack.enter_context(nc.Block())

    @blk.sync
    def _(sp):
        sp.dma_start(const[:, :], consts).then_inc(s_const, 16)
        for p0, tile, n, ap in row_pieces:
            sp.dma_start(rows_in[p0:p0 + n, tile, :], ap).then_inc(s_rows, 16)
        sp.dma_start(tokens_in[:, 0:2, :], x.rearrange("b (t p) d -> p (b t) d", p=P)).then_inc(s_tok, 16)
        sp.dma_start(tokens_in[:, 2:4, :], ctx.rearrange("b (t p) d -> p (b t) d", p=P)).then_inc(s_tok, 16)

        def load(ph, chunk, source_ap):
            slot = (ph.start // 2 + chunk[1]) % 2
            at_least(sp, lo_done, 2 * chunk[0] - 2)
            kk, cc = source_ap.shape[1], source_ap.shape[2]
            dst = raw[:, slot, 0:kk * cc].rearrange("p (k c) -> p k c", c=cc)
            sp.dma_start(dst, source_ap).then_inc(raw_in[slot], 16)

        ahead = set()
        for at_plan, (kind, ph) in enumerate(plan):
            if kind == "mod":
                nxt = next(p for what, p in plan[at_plan:] if what == "gemm")
                if nxt.start not in ahead:
                    ahead.add(nxt.start)
                    load(nxt, (nxt.start // 2, 0), nxt.source(0, 0))
                    load(nxt, (nxt.start // 2 + 1, 1), nxt.source(0, 1))
                seg = ph["seg"]
                view = kpc(w_mod[seg // 3])

                def body(i, first, last):
                    for j in range(2):
                        m = seg * 12 + 2 * i + j
                        at_least(sp, mod_done, m - 1)
                        col = (seg % 3) * 3 * D + (2 * i + j) * 256
                        sp.dma_start(mod_raw[:, j, :, :], view[:, :, bass.ds(col, 256)]).then_inc(mod_in[j], 16)
                repeat(sp, 6, body)
            elif kind == "gemm":
                c0 = ph.start // 2
                if ph.more.get("pair"):
                    def body(i, first, last):
                        if first and ph.start in ahead:
                            return
                        load(ph, (c0 + 2 * i, 0), ph.source(i, 0))
                        load(ph, (c0 + 2 * i + 1, 1), ph.source(i, 1))
                    repeat(sp, ph.n // 4, body)
                elif ph.kind == "branch":
                    for i in range(6):
                        load(ph, (c0 + i, i), ph.source(i))
                else:
                    def body(i, first, last):
                        load(ph, (c0 + 2 * i, 0), ph.source(2 * i))
                        load(ph, (c0 + 2 * i + 1, 1), ph.source(2 * i + 1))
                    repeat(sp, ph.n // 4, body)
                    if ph.n % 4:
                        load(ph, (c0 + 2 * (ph.n // 4), 0), ph.source(2 * (ph.n // 4)))
        sp.wait_ge(final_copy, 4)
        sp.dma_start(out.rearrange("b (t p) d -> p (b t) d", p=P), tokens_out[:, :, :]).then_inc(s_store, 16)
        sp.wait_ge(s_store, 16)

    @blk.scalar
    def _(act):
        def split(ph, u, i, view):
            t_static = ph.start + u + AHEAD
            tmod = t_static % 4
            slot, half = tmod // 2, tmod % 2
            act.wait_ge(raw_in[slot], 16 * (t_static // 4 + 1) + 16 * i)
            at_least(act, acc_done, ph.start + u + AHEAD - 3 + 4 * i)
            act.activation(slot_view(w_hi[:, tmod, :], view), half_view(raw[:, slot, :], view, half),
                           ACT.Copy).then_inc(hi_done, 1)

        def split_ahead(ph, u, i, last):
            if isinstance(i, int) and ph.start + 4 * i + u + AHEAD >= total:
                return
            view = ph.view
            if isinstance(i, int):
                view = unit_view[ph.start + 4 * i + u + AHEAD]
            split(ph, u, i, view)

        act.wait_ge(init_copy, n_row_tiles)
        for s, name in enumerate(("c", "c_ctx")):
            act.activation(silu_c[:, :, s], vec(name, 0, KD), ACT.Silu).then_inc(silu_c_done, 1)
        for t in range(AHEAD):
            act.wait_ge(raw_in[t // 2], 16)
            act.activation(slot_view(w_hi[:, t, :], "std"), half_view(raw[:, t // 2, :], "std", t % 2),
                           ACT.Copy).then_inc(hi_done, 1)

        def act_gemm(ph):
            k = ph.kind
            width = ph.width

            def step(i, first, last, n_units=4):
                for u in range(n_units):
                    t = ph.start + u + 4 * i
                    b = (ph.start + u) % 4
                    split_ahead(ph, u, i, last)
                    if k == "glu":
                        if u < 2:
                            act.wait_ge(acc_done, t + 1)
                            at_least(act, acc_free, t - 2 + u)
                            act.activation(sil[:, u, 0:width], bank[b][:, 0:width], ACT.Silu).then_inc(silu_done, 1)
                        else:
                            act.wait_ge(acc_free, ph.start + 4 * i + 2 * (u - 1))
                            act.activation(G_hi[:, 2 * i + u - 2, 0:width], g32[:, u - 2, 0:width],
                                           ACT.Copy).then_inc(g_hi_done, 1)
                    elif k == "conv_glu":
                        layer, third = ph.more["layer"], ph.more["third"]
                        f = (0 if u < 2 else FT) + third * 8 + 2 * i + u % 2
                        g = ph.g0 + 2 * i + u % 2
                        if u == 1:
                            silu_conv(ph, i, 0)
                        if u == 2:
                            silu_conv(ph, i, 1)
                        act.wait_ge(acc_done, t + 1)
                        if u < 2:
                            at_least(act, g_mul_done, g - GLU_TILES - 1)
                            dst = sil
                        else:
                            at_least(act, g_lo_done, g - 1)
                            dst = g32
                        act.activation(dst[:, u % 2, 0:S], bank[b][:, 0:S], ACT.Identity,
                                       scale=vec("conv_w_2", (layer * 3 + 2) * 2 * FT + f),
                                       bias=vec("conv_b_2", layer * 2 * FT + f)).then_inc(conv0_done, 1)
                        if u == 3:
                            for e in range(2):
                                gg = ph.gm0 + 2 * i + e
                                act.wait_ge(g_mul_done, gg + 1)
                                act.activation(G2_hi[:, 2 * i + e, :], g32[:, e, 0:S], ACT.Copy).then_inc(g_hi_done, 1)
                    elif k == "gate":
                        act.wait_ge(acc_done, t + 1)
                        act.activation(gates[:, 4 * i + u, :], bank[b][:, 0:S], ACT.Sigmoid,
                                       bias=vec("b_gate", ph.more["layer"] * N_GATE + 4 * i + u)).then_inc(gate_done, 1)
                    elif k == "branch" and i == 2:
                        for e in range(2):
                            f = 2 * u + e
                            act.wait_ge(merge_step, ph.merge0 + 4 + u + 1)
                            ins = act.activation(H2_hi[:, f, :], merged[:, f, :], ACT.Copy)
                        ins.then_inc(h_hi_done, 2)
            n4, left = phase_steps(ph)
            if k == "branch":
                for i in range(n4):
                    step(i, i == 0, i == n4 - 1)
            else:
                repeat(act, n4, step, needs_peel(ph) and not left)
            if left:
                step(n4, False, True, left)

        def silu_conv(ph, i, e):
            act.wait_ge(acc_free, ph.start + 4 * i + e + 1)
            act.activation(sil[:, e, 0:S], sil[:, e, 0:S], ACT.Silu).then_inc(silu_done, 1)

        def act_norm(nm):
            r, width = nm["r"], nm.get("width", S)
            act.wait_ge(stat_done, r + 1)
            act.activation(rstd[:, 0:width], STAT[:, 0:width], ACT.Sqrt, scale=1.0 / D, bias=eps[:, 0:1]) \
               .then_inc(rms_done, 1)
            if nm["kind"] == "mod":
                seg = nm["seg"]
                for k in range(KD):
                    act.wait_ge(n_mul, nm["a0"] + k + 1)
                    for s in range(width // S):
                        ins = act.activation(T1[:, k, s * S:s * S + S], T1[:, k, s * S:s * S + S], ACT.Identity,
                                             scale=modv[:, seg, 1, k, s:s + 1], bias=modv[:, seg, 0, k, s:s + 1])
                    ins.then_inc(n_aff, 1)
            elif nm["kind"] == "plain":
                name, at0 = nm["gain"]
                for k in range(KD):
                    act.wait_ge(n_mul, nm["a0"] + k + 1)
                    act.activation(T2[:, k, :], T2[:, k, :], ACT.Copy, scale=vec(name, at0 + k)).then_inc(n_aff, 1)

        def act_mixers(mx):
            layer = mx["layer"]
            base_a, base_d = (mx["act0"], dict(z=mx["d_z"], pool=mx["d_pool"], end=mx["d_pool"][-1] + 2))
            n = 0
            for s in range(mx["streams"]):
                cols = slice(s * S, s * S + S)
                for j in range(2):
                    act.wait_ge(mix_dve, base_d["z"])
                    act.activation(U[:, 4 + j, cols], U[:, j, cols], ACT.Copy,
                                   scale=vec("conv_w", (layer * 3 + 1) * 2 + j)).then_inc(mix_act, 1)
            for s in range(mx["streams"]):
                for j in range(2):
                    act.wait_ge(mix_pe, mx["pe0"] + 2 * s + j + 1)
                    act.activation(U[:, 6 + j, s * S:s * S + S], bank[j][:, 0:S], ACT.Copy,
                                   scale=vec("pool_scale", layer * 2 + j)).then_inc(mix_act, 1)

        def act_attend(at_):
            for what, call in attend_order(at_):
                if what == "sb":
                    act_stick(at_)
                else:
                    act_call(call)

        def act_call(call):
            groups = call["groups"]
            n_g = len(groups)
            for j in range(n_g + 1):
                if j < n_g:
                    g = groups[j]
                    n = g["n"]
                    act.wait_ge(max_done, n + 1)
                    at_least(act, pt_done, n - 3)
                    for si, (qt, a, b) in enumerate(g["segs"]):
                        col = (g["seg0"] + si) % 16
                        ins = act.activation(probs[:, n % 4, a:b], bank[call["score_banks"][(n - call["n0"]) % len(call["score_banks"])]][:, a:b],
                                             ACT.Exp, bias=neg_max[:, col:col + 1],
                                             scale=SCALE if call["what"] == "ctx" else 1.0,
                                             accum_out=row_sum[:, col:col + 1])
                        if call["what"] == "swa":
                            h = call["layer"] * 8 + g["head"]
                            ins = act.activation(sink_e[:, col:col + 1], sink[:, h:h + 1], ACT.Exp,
                                                 bias=neg_max[:, col:col + 1])
                    ins.then_inc(exp_done, 1)
                if j >= 1:
                    g = groups[j - 1]
                    n = g["n"]
                    act.wait_ge(pt_done, n + 1)
                    head = 2 * call["pair0"] + g["head"]
                    at_least(act, pv_done, head - 1)
                    pb = bank[call["pt_banks"][(n - call["n0"]) % len(call["pt_banks"])]]
                    e = g["head"] % 2
                    if g["qt"] is None:
                        w = P * len(g["blocks"])
                        act.activation(probs_t[:, e, 0:w], pb[:, 0:w], ACT.Copy).then_inc(pt_copy, 1)
                    else:
                        dst = probs_t[:, e, :].rearrange("p (k q) -> p k q", q=S)[:, :, g["qt"] * P:g["qt"] * P + P]
                        act.activation(dst, pb[:, :].rearrange("p (k q) -> p k q", q=P), ACT.Copy).then_inc(pt_copy, 1)

        def act_stick(at_):
            for j in range(4):
                m = at_["sb0"] + j
                act.wait_ge(sb_dve, 4 * m + 1)
                act.activation(sb_e[:, :, :], sb_z[:, :, :], ACT.Abs).then_inc(sb_act, 1)
                act.wait_ge(sb_act, 4 * m + 1)
                act.activation(sb_e[:, :, :], sb_e[:, :, :], ACT.Exp, scale=-1.0).then_inc(sb_act, 1)
                act.wait_ge(sb_act, 4 * m + 2)
                act.activation(sb_e[:, :, :], sb_e[:, :, :], ACT.Ln, bias=ones[:, 0:1]).then_inc(sb_act, 1)
                act.wait_ge(sb_dve, 4 * m + 3)
                act.activation(sb_w[:, :, :], sb_w[:, :, :], ACT.Exp).then_inc(sb_act, 1)

        for kind, ph in plan:
            if kind == "gemm":
                act_gemm(ph)
            elif kind == "norm":
                act_norm(ph)
            elif kind == "mixers":
                act_mixers(ph)
            elif kind == "attend":
                act_attend(ph)

    @blk.vector
    def _(dve):
        def split_ahead(ph, u, i):
            if isinstance(i, int) and ph.start + 4 * i + u + AHEAD >= total:
                return
            view = ph.view if not isinstance(i, int) else unit_view[ph.start + 4 * i + u + AHEAD]
            tmod = (ph.start + u + AHEAD) % 4
            slot, half = tmod // 2, tmod % 2
            dve.wait_ge(hi_done, ph.start + u + AHEAD + 1 + 4 * i)
            dve.tensor_tensor(slot_view(w_lo[:, tmod, :], view), half_view(raw[:, slot, :], view, half),
                              slot_view(w_hi[:, tmod, :], view).bitcast(F32), ALU.subtract).then_inc(lo_done, 1)

        for tile in range(n_row_tiles):
            dve.wait_ge(init_t, tile + 1)
            used = min(P, n_rows - tile * P)
            dve.tensor_copy(vecs[:, tile * P:tile * P + used], bank[4 + tile % 2][:, 0:used]).then_inc(init_copy, 1)
        for f in range(KD):
            dve.wait_ge(init_t, n_row_tiles + f + 1)
            dve.tensor_copy(X[:, f, :], bank[f % 4][:, :]).then_inc(init_copy, 1)
        for t in range(AHEAD):
            dve.wait_ge(hi_done, t + 1)
            dve.tensor_tensor(slot_view(w_lo[:, t, :], "std"), half_view(raw[:, t // 2, :], "std", t % 2),
                              slot_view(w_hi[:, t, :], "std").bitcast(F32), ALU.subtract).then_inc(lo_done, 1)

        def dve_mod(md):
            seg = md["seg"]
            layer, i = seg // 3, seg % 3
            dve.wait_ge(mod_done, 12 * (seg + 1))
            src = bank[6 + seg % 2][:, 0:48].rearrange("p (n s) -> p n s", s=2)
            dst = modv[:, seg, :, :, :].rearrange("p a k s -> p (a k) s")
            for s in range(2):
                ins = dve.tensor_tensor(dst[:, :, s], src[:, :, s], vec("b_mod", layer * 72 + i * 24, 24), ALU.add)
            ins.then_inc(mod_step, 1)
            dve.wait_ge(mod_step, seg + 1)
            for s in range(2):
                ins = dve.scalar_tensor_tensor(modv[:, seg, 1, :, s], modv[:, seg, 1, :, s], 1.0,
                                               vec("norm_g", layer * 24 + i * 8, KD), ALU.add, ALU.mult)
            if i != 1:
                ins = dve.tensor_scalar(modv[:, seg, 2, :, :], modv[:, seg, 2, :, :], 0.5, None, ALU.mult)
            ins.then_inc(mod_ready, 1)

        def dve_gemm(ph):
            k, width = ph.kind, ph.width
            if k == "residual":
                dve.wait_ge(acc_free, ph.start)
                if ph.more["seg"] is not None:
                    dve.wait_ge(mod_ready, ph.more["seg"] + 1)

            def step(i, first, last, n_units=4):
                for u in range(n_units):
                    t = ph.start + u + 4 * i
                    b = (ph.start + u) % 4
                    split_ahead(ph, u, i)
                    if k == "glu":
                        if u >= 2:
                            g = ph.g0 + 2 * i + u - 2
                            dve.wait_ge(acc_done, t + 1)
                            dve.wait_ge(silu_done, ph.g0 + 2 * i + u - 1)
                            at_least(dve, g_lo_done, g - 1)
                            dve.tensor_tensor(g32[:, u - 2, 0:width], bank[b][:, 0:width], sil[:, u - 2, 0:width],
                                              ALU.mult).then_inc(acc_free, 2)
                    elif k == "conv_glu":
                        layer, third = ph.more["layer"], ph.more["third"]
                        f = (0 if u < 2 else FT) + third * 8 + 2 * i + u % 2
                        dst = (sil if u < 2 else g32)[:, u % 2, 0:S]
                        m = 2 * ph.gm0 + 4 * i + u
                        dve.wait_ge(conv0_done, m + 1)
                        dve.scalar_tensor_tensor(dst[:, 1:S], bank[b][:, 0:S - 1],
                                                 vec("conv_w_2", (layer * 3 + 1) * 2 * FT + f), dst[:, 1:S],
                                                 ALU.mult, ALU.add).then_inc(conv1_done, 1)
                        dve.wait_ge(conv1_done, m + 1)
                        dve.scalar_tensor_tensor(dst[:, 2:S], bank[b][:, 0:S - 2],
                                                 vec("conv_w_2", layer * 3 * 2 * FT + f), dst[:, 2:S],
                                                 ALU.mult, ALU.add).then_inc(acc_free, 1)
                        if u >= 2:
                            dve.wait_ge(acc_free, t + 1)
                            dve.wait_ge(silu_done, ph.g0 + 2 * i + u - 1)
                            dve.tensor_tensor(g32[:, u - 2, 0:S], g32[:, u - 2, 0:S], sil[:, u - 2, 0:S], ALU.mult) \
                               .then_inc(g_mul_done, 1)
                    elif k == "residual":
                        f = 4 * i + u
                        dve.wait_ge(acc_done, t + 1)
                        if ph.more["seg"] is None:
                            dve.tensor_tensor(X2[:, f, :], bank[b][:, 0:S], X2[:, f, :], ALU.add).then_inc(acc_free, 1)
                        else:
                            for s in range(width // S):
                                cols = slice(s * S, s * S + S)
                                ins = dve.scalar_tensor_tensor(X[:, f, cols], bank[b][:, cols],
                                                               modv[:, ph.more["seg"], 2, f, s:s + 1], X[:, f, cols],
                                                               ALU.mult, ALU.add)
                            ins.then_inc(acc_free, 1)
                    elif k == "store":
                        f = ph.more["f0"] + 4 * i + u
                        dst = U if ph.more["dst"] == "U" else U2
                        dve.wait_ge(acc_done, t + 1)
                        dve.tensor_copy(dst[:, f, 0:width], bank[b][:, 0:width]).then_inc(acc_free, 1)
                    elif k == "gate":
                        dve.wait_ge(gate_done, ph.more["layer"] * N_GATE + 4 * i + u + 1)
                        dve.wait_ge(acc_free, t)
                        dve.nop().then_inc(acc_free, 1)
                    elif k == "branch":
                        g = gates[:, 8 * i + 2 * u:8 * i + 2 * u + 2, :].rearrange("p f t -> p (f t)")
                        m = merged[:, 2 * u:2 * u + 2, :].rearrange("p f t -> p (f t)")
                        tmp = sil[:, u % 2, :]
                        dve.wait_ge(acc_done, t + 1)
                        if i == 0:
                            dve.tensor_tensor(m, bank[b][:, :], g, ALU.mult).then_inc(acc_free, 1)
                        else:
                            dve.tensor_tensor(tmp, bank[b][:, :], g, ALU.mult).then_inc(acc_free, 1)
                            dve.wait_ge(acc_free, t + 1)
                            dve.tensor_tensor(m, m, tmp, ALU.add).then_inc(merge_step, 1)
                            dve.wait_ge(merge_step, ph.merge0 + 4 * (i - 1) + u + 1)
            n4, left = phase_steps(ph)
            if k == "branch":
                for i in range(n4):
                    step(i, i == 0, i == n4 - 1)
            else:
                repeat(dve, n4, step, needs_peel(ph) and not left)
            if left:
                step(n4, False, True, left)

        def dve_norm(nm):
            r, width, kind = nm["r"], nm.get("width", S), nm["kind"]
            dve.wait_ge(rms_done, r + 1)
            dve.reciprocal(rstd[:, 0:width], rstd[:, 0:width]).then_inc(rstd_done, 1)
            dve.wait_ge(rstd_done, r + 1)
            if kind in ("mod", "plain"):
                src, dst, hi = (X, T1, H_hi) if kind == "mod" else (X2, T2, H2_hi)
                if kind == "mod":
                    dve.wait_ge(mod_ready, nm["seg"] + 1)
                m0 = nm["a0"]
                for k in range(KD + 2):
                    if k < KD:
                        dve.tensor_tensor(dst[:, k, 0:width], src[:, k, 0:width], rstd[:, 0:width], ALU.mult) \
                           .then_inc(n_mul, 1)
                    if k >= 2:
                        dve.wait_ge(n_aff, m0 + k - 1)
                        dve.tensor_copy(hi[:, k - 2, 0:width], dst[:, k - 2, 0:width]).then_inc(h_hi_done, 1)
            else:
                name, at0 = nm["gain"]
                for k in range(KD):
                    src, dst = (X, X2) if kind == "renorm" else (X2, T2)
                    if kind == "renorm":
                        dst = T2
                    dve.scalar_tensor_tensor(dst[:, k, :], src[:, k, 0:S], vec(name, at0 + k), rstd[:, 0:S],
                                             ALU.mult, ALU.mult).then_inc(final_mul, 1)
                if kind == "renorm":
                    dve.wait_ge(final_mul, KD)
                    dve.tensor_copy(X2[:, :, :], T2[:, :, :]).then_inc(final_mul, 1)

        def dve_mixers(mx):
            layer, streams = mx["layer"], mx["streams"]
            _, bd = (mx["act0"], dict(z=mx["d_z"], pool=mx["d_pool"], end=mx["d_pool"][-1] + 2))
            w = streams * S
            n = [mx["dve0"]]

            def step(ins):
                ins.then_inc(mix_dve, 1)
                n[0] += 1
                dve.wait_ge(mix_dve, n[0])
            dve.wait_ge(acc_free, mx["unit_end"])
            dve.wait_ge(acc_done, mx["unit_end"])
            step(dve.tensor_tensor(U[:, 0:2, 0:w], U[:, 4:6, 0:w], U[:, 0:2, 0:w], ALU.mult))
            assert n[0] == bd["z"]
            for s in range(streams):
                a = s * S
                for j in range(2):
                    dve.wait_ge(mix_act, mx["act0"] + 2 * s + j + 1)
                    step(dve.scalar_tensor_tensor(U[:, 4 + j, a + 1:a + S], U[:, j, a:a + S - 1],
                                                  vec("conv_w", layer * 6 + j), U[:, 4 + j, a + 1:a + S],
                                                  ALU.mult, ALU.add))
                    step(dve.scalar_tensor_tensor(U[:, 4 + j, a:a + S - 1], U[:, j, a + 1:a + S],
                                                  vec("conv_w", layer * 6 + 4 + j), U[:, 4 + j, a:a + S - 1],
                                                  ALU.mult, ALU.add))
            step(dve.tensor_tensor(U[:, 4:6, 0:w], U[:, 4:6, 0:w], U[:, 2:4, 0:w], ALU.mult))
            step(dve.tensor_copy(H_hi[:, 0:2, 0:w], U[:, 4:6, 0:w]))
            step(dve.tensor_tensor(H_lo[:, 0:2, 0:w], U[:, 4:6, 0:w], H_hi[:, 0:2, 0:w].bitcast(F32), ALU.subtract))
            for s in range(streams):
                a, pad = s * S, 12
                if s > 0:
                    dve.wait_ge(mix_pe, mx["pe0"] + 2 * s)
                step(dve.memset(pool_a[:, :, :], 0.0))
                step(dve.memset(pool_b[:, :, :], 0.0))
                step(dve.tensor_copy(pool_a[:, :, pad:pad + S], U[:, 6:8, a:a + S]))
                ic = table("inv_count").rearrange("p (j t) -> p j t", t=S)
                src, dst = pool_a, pool_b
                for g, (left, right, lo_, hi_) in enumerate(((1, 0, 1, 280), (1, 1, 2, 279), (2, 2, 4, 277), (4, 4, 8, 272))):
                    step(dve.tensor_tensor(dst[:, :, lo_:hi_], src[:, :, lo_ - left:hi_ - left],
                                           src[:, :, lo_ + right:hi_ + right], ALU.add))
                    rows_ = slice(HD * (g % 2), HD * (g % 2) + HD)
                    step(dve.tensor_tensor(pool_c[rows_, g // 2, :], dst[rows_, g // 2, pad:pad + S], ic[rows_, g // 2, :],
                                           ALU.mult))
                    src, dst = dst, src
                step(dve.tensor_tensor(pool_c[:, :, :], pool_c[:, :, :], U[:, 6:8, a:a + S], ALU.subtract))
                assert n[0] == bd["pool"][s]
                dve.wait_ge(mix_act, mx["act0"] + 2 * streams + 2 * s + 2)
                step(dve.tensor_copy(H_hi[:, 2:4, a:a + S], U[:, 6:8, a:a + S]))
                step(dve.tensor_tensor(H_lo[:, 2:4, a:a + S], U[:, 6:8, a:a + S], H_hi[:, 2:4, a:a + S].bitcast(F32),
                                       ALU.subtract))
            assert n[0] == bd["end"], (n[0], bd)

        def dve_bias(layer):
            near = table("m_near").unsqueeze(1).to_broadcast([P, 8, 64])
            flat = bias_t[:, :, :, :].rearrange("p h r k -> p (h r) k")
            for j in range(6):
                dve.wait_ge(bias_pe, layer * 6 + j + 1)
                dve.tensor_tensor(flat[:, 8 * j:8 * j + 8, :], bank[j % 4][:, :].rearrange("p (r k) -> p r k", k=64), near,
                                  ALU.min).then_inc(bias_done, 1)

        def dve_attend(at_):
            b1 = at_["block"] == 1
            if b1:
                dve_bias(at_["layer"])
                dve.wait_ge(bias_done, 6 * (at_["layer"] + 1))
            for j, (tile, nb) in enumerate(at_["vt_jobs"]):
                m = at_["vt0"] + j
                dve.wait_ge(vt_t, m + 1)
                w = nb * P
                dve.tensor_copy(vt[:, j * w:j * w + w], bank[4 + m % 2][:, 0:w]).then_inc(vt_copy, 1)
            if not b1:
                for j in range(13):
                    m = at_["rope0"] + j
                    tile = rope_tiles()[j]
                    dve.wait_ge(rope_pe, m + 1)
                    at_least(dve, rope_dve, 2 * m - 2)
                    dve.tensor_tensor(rope_t[:, m % 2, :], bank[6 + m % 2][:, 0:S], table("sin"), ALU.mult) \
                       .then_inc(rope_dve, 1)
                    dve.wait_ge(rope_pool, m + 1)
                    dve.wait_ge(rope_dve, 2 * m + 1)
                    dve.tensor_tensor(U2[:, tile, :], U2[:, tile, :], rope_t[:, m % 2, :], ALU.add).then_inc(rope_dve, 1)
                dve.wait_ge(rope_dve, 2 * (at_["rope0"] + 13))
                dve.tensor_copy(k_swap[0:HD, :], U2[HD:P, 4, :])
                dve.tensor_copy(k_swap[HD:P, :], U2[0:HD, 4, :]).then_inc(k_swap_done, 1)
            for what, call in attend_order(at_):
                if what == "sb":
                    dve_stick(at_)
                else:
                    dve_call(call)

        def dve_out(pair, src, hi, lo):
            dve.wait_ge(pv_done, 2 * (pair + 1))
            dve.tensor_copy(hi, src).then_inc(o_step, 1)
            dve.wait_ge(o_step, pair + 1)
            dve.tensor_tensor(lo, src, hi.bitcast(F32), ALU.subtract).then_inc(o_done, 1)

        def dve_call(call):
            groups, what = call["groups"], call["what"]
            n_g = len(groups)
            per_head = n_g // 8
            if what == "swa":
                dve.wait_ge(s_small, 16 + 64 * DEPTH)
            for j in range(n_g + 3 + per_head):
                if j < n_g:
                    g = groups[j]
                    n = g["n"]
                    sb_ = bank[call["score_banks"][(n - call["n0"]) % len(call["score_banks"])]]
                    dve.wait_ge(sc_done, n + 1)
                    if what == "near":
                        rr = 2 - 2 * g["qt"]
                        dve.scalar_tensor_tensor(sb_[:, 0:S], sb_[:, 0:S], SCALE,
                                                 bias_t[:, g["head"], rr:rr + 4, :].rearrange("p r k -> p (r k)"),
                                                 ALU.mult, ALU.add)
                        dve.tensor_scalar(sb_[:, S:512], sb_[:, S:512], SCALE, None, ALU.mult).then_inc(bias_add, 1)
                    elif what == "ctx":
                        at_least(dve, bias_add, n)
                        dve.nop().then_inc(bias_add, 1)
                    else:
                        mask = table("m_band" if what == "swa" else "m_causal")
                        dve.scalar_tensor_tensor(sb_[:, 0:384], sb_[:, 0:384], SCALE, mask, ALU.mult, ALU.add) \
                           .then_inc(bias_add, 1)
                    dve.wait_ge(bias_add, n + 1)
                    at_least(dve, p_ready, n - 3)
                    c0 = g["seg0"] % 16
                    ns = len(g["segs"])
                    for si, (qt, a, b) in enumerate(g["segs"]):
                        ins = dve.tensor_reduce(neg_max[:, c0 + si:c0 + si + 1], sb_[:, a:b], AX.X, ALU.max,
                                                negate=what != "ctx" and what != "swa")
                    if what == "ctx":
                        ins.then_inc(max_step, 1)
                        dve.wait_ge(max_step, g["max_count"])
                        dve.tensor_scalar(neg_max[:, c0:c0 + ns], neg_max[:, c0:c0 + ns], -SCALE, None, ALU.mult) \
                           .then_inc(max_done, 1)
                    elif what == "swa":
                        ins.then_inc(max_step, 1)
                        dve.wait_ge(max_step, g["max_count"])
                        h = call["layer"] * 8 + g["head"]
                        dve.tensor_scalar(neg_max[:, c0:c0 + ns], neg_max[:, c0:c0 + ns], sink[:, h:h + 1], -1.0,
                                          ALU.max, ALU.mult).then_inc(max_done, 1)
                    else:
                        ins.then_inc(max_done, 1)
                if 1 <= j <= n_g:
                    g = groups[j - 1]
                    n = g["n"]
                    c0, ns = g["seg0"] % 16, len(g["segs"])
                    dve.wait_ge(exp_done, n + 1)
                    if what == "swa":
                        dve.tensor_tensor(row_sum[:, c0:c0 + ns], row_sum[:, c0:c0 + ns], sink_e[:, c0:c0 + ns], ALU.add) \
                           .then_inc(inv_step, 1)
                        dve.wait_ge(inv_step, g["inv_count"] - 1)
                    dve.reciprocal(row_inv[:, c0:c0 + ns], row_sum[:, c0:c0 + ns]).then_inc(inv_step, 1)
                    dve.wait_ge(inv_step, g["inv_count"])
                    for si, (qt, a, b) in enumerate(g["segs"]):
                        ins = dve.tensor_scalar(probs[:, n % 4, a:b], probs[:, n % 4, a:b],
                                                row_inv[:, c0 + si:c0 + si + 1], None, ALU.mult)
                    ins.then_inc(p_ready, 1)
                jj = j - 2 - per_head
                if jj >= 0 and jj < n_g and groups[jj]["last"] and groups[jj]["head"] % 2 == 1:
                    hp = groups[jj]["head"] // 2
                    hi, lo = out_tiles(call, hp)
                    ob = out_of(call, hp)
                    dve_out(call["pair0"] + hp, ob, hi, lo)

        def dve_stick(at_):
            for j in range(4):
                m = at_["sb0"] + j
                mask = table("m_past")
                dve.wait_ge(sb_pe, 2 * m + 1)
                for e in range(2):
                    ins = dve.scalar_tensor_tensor(sb_z[:, e, :], bank[4 + e][:, 0:384], SCALE, mask, ALU.mult, ALU.add)
                ins.then_inc(sb_dve, 1)
                dve.wait_ge(sb_act, 4 * m + 3)
                dve.wait_ge(sb_dve, 4 * m + 1)
                dve.scalar_tensor_tensor(sb_s[:, :, :], sb_z[:, :, :], 0.0, sb_e[:, :, :], ALU.max, ALU.add) \
                   .then_inc(sb_dve, 1)
                dve.wait_ge(sb_pe, 2 * m + 2)
                for e in range(2):
                    ins = dve.tensor_tensor(sb_w[:, e, :], sb_z[:, e, :], bank[4 + e][:, 0:384], ALU.subtract)
                ins.then_inc(sb_dve, 1)
                pair = at_["sb_pair0"] + j
                ob = bank[6 + j % 2][:, 0:S]
                dve_out(pair, ob, O_hi[:, 4 + j, :], O_lo[:, 4 + j, :])
                dve.wait_ge(sb_dve, 4 * m + 3)
                dve.nop().then_inc(sb_dve, 1)

        for kind, ph in plan:
            if kind == "mod":
                dve_mod(ph)
            elif kind == "gemm":
                dve_gemm(ph)
            elif kind == "norm":
                dve_norm(ph)
            elif kind == "mixers":
                dve_mixers(ph)
            elif kind == "attend":
                dve_attend(ph)
        for q in range(4):
            dve.wait_ge(final_t, q + 1)
            tb, fh = q // 2, q % 2
            dve.tensor_copy(tokens_out[:, tb, fh * 512:fh * 512 + 512], bank[q][:, :]).then_inc(final_copy, 1)

    @blk.gpsimd
    def _(pool):
        pool.memset(ones[:, :], 1.0)
        pool.memset(eps[:, :], EPS)
        pool.memset(pool_bd[:, :, :], 0.0).then_inc(memset_done, 3)
        pool.dma_start(sink[:, :], sinks_2.rearrange("l h -> (l h)").partition_broadcast(P)).then_inc(s_small, 16)

        def pool_w_load(layer):
            for g in range(4):
                lo = HD * (g % 2)
                pool.dma_start(pool_bd[lo:lo + HD, g // 2, lo:lo + HD], pool_w[layer, g]).then_inc(s_small, 16)

        def bias_load(layer):
            for b in range(2):
                for h in range(8):
                    src = bass.AP(tensor=rpb.tensor, offset=rpb[layer, h].offset + (5 - b) * 31 - 48,
                                  ap=[[1, 64], [31, 6], [1, 64]])
                    pool.dma_start(bias_t[64 * b:64 * b + 64, h, :, :], src).then_inc(s_bias, 16)

        pool.wait_ge(memset_done, 3)
        pool_w_load(0)
        bias_load(0)

        def stats_start(r):
            at_least(pool, stat_done, r)
            pool.memset(sq_sum[:, :], 0.0).then_inc(sq_step, 1)

        def stats_tile(r, k, src, width):
            pool.wait_ge(sq_step, 17 * r + 1 + 2 * k)
            pool.tensor_tensor(sq[:, 0:width], src, src, ALU.mult).then_inc(sq_step, 1)
            pool.wait_ge(sq_step, 17 * r + 2 + 2 * k)
            pool.tensor_tensor(sq_sum[:, 0:width], sq_sum[:, 0:width], sq[:, 0:width], ALU.add).then_inc(sq_step, 1)

        stats_start(0)
        for k in range(KD):
            pool.wait_ge(init_copy, n_row_tiles + k + 1)
            stats_tile(0, k, X[:, k, :], 512)

        def pool_gemm(ph):
            k, width = ph.kind, ph.width
            if k in ("glu", "conv_glu"):
                hi, lo = (G_hi, G_lo) if k == "glu" else (G2_hi, G2_lo)

                def step(i, first, last):
                    for e in range(2):
                        g = ph.g0 + 2 * i + e
                        pool.wait_ge(g_hi_done, g + 1)
                        pool.tensor_tensor(lo[:, 2 * i + e, 0:width], g32[:, e, 0:width],
                                           hi[:, 2 * i + e, 0:width].bitcast(F32), ALU.subtract).then_inc(g_lo_done, 1)
                repeat(pool, ph.n // 4, step)
            elif k == "residual" and ph.more["stats"]:
                r = ph.more["norm_next"]
                pool.wait_ge(acc_done, ph.start + 1)
                stats_start(r)

                def step(i, first, last):
                    for u in range(4):
                        f = 4 * i + u
                        pool.wait_ge(acc_free, ph.start + f + 1)
                        src = X[:, f, 0:width] if ph.more["seg"] is not None else X2[:, f, :]
                        stats_tile(r, f, src, width)
                repeat(pool, 2, step)
            elif k == "branch":
                for u in range(4):
                    for e in range(2):
                        f = 2 * u + e
                        pool.wait_ge(h_hi_done, ph.h0 + 2 * u + 2)
                        pool.tensor_tensor(H2_lo[:, f, :], merged[:, f, :], H2_hi[:, f, :].bitcast(F32),
                                           ALU.subtract).then_inc(h_lo_done, 1)

        def pool_norm(nm):
            kind, width = nm["kind"], nm.get("width", S)
            if kind in ("mod", "plain"):
                src, hi, lo = (T1, H_hi, H_lo) if kind == "mod" else (T2, H2_hi, H2_lo)
                for k in range(KD):
                    pool.wait_ge(h_hi_done, nm["h0"] + k + 1)
                    pool.tensor_tensor(lo[:, k, 0:width], src[:, k, 0:width], hi[:, k, 0:width].bitcast(F32),
                                       ALU.subtract).then_inc(h_lo_done, 1)
            elif kind == "renorm":
                r = nm["r"] + 1
                pool.wait_ge(final_mul, KD + 1)
                stats_start(r)
                for k in range(KD):
                    stats_tile(r, k, X2[:, k, :], S)

        for kind, ph in plan:
            if kind == "gemm":
                pool_gemm(ph)
            elif kind == "norm":
                pool_norm(ph)
            elif kind == "attend":
                if ph["block"] == 1:
                    if ph["layer"] + 1 < DEPTH:
                        pool.wait_ge(o_done, ph["calls"][-1]["pair0"] + 4)
                        pool.wait_ge(mix_pe, 4)
                        pool_w_load(ph["layer"] + 1)
                        bias_load(ph["layer"] + 1)
                else:
                    for j in range(13):
                        m = ph["rope0"] + j
                        tile = rope_tiles()[j]
                        pool.wait_ge(rope_pe, m + 1)
                        pool.tensor_tensor(U2[:, tile, :], U2[:, tile, :], table("cos"), ALU.mult).then_inc(rope_pool, 1)

    @blk.tensor
    def _(pe):
        pe.wait_ge(s_const, 16)
        pe.wait_ge(memset_done, 3)
        pe.wait_ge(s_rows, 16 * len(row_pieces))
        for tile in range(n_row_tiles):
            used = min(P, n_rows - tile * P)
            if tile >= 2:
                pe.wait_ge(init_copy, tile - 1)
            pe.transpose(bank[4 + tile % 2][:, 0:used], rows_in[0:used, tile, :], ident[0:used, 0:used]).then_inc(init_t, 1)
        pe.wait_ge(s_tok, 32)
        for f in range(KD):
            if f >= 4:
                pe.wait_ge(init_copy, n_row_tiles + f - 3)
            for tb in range(4):
                ins = pe.transpose(bank[f % 4][:, tb * P:tb * P + P], tokens_in[:, tb, f * P:f * P + P], ident)
            ins.then_inc(init_t, 1)

        def pe_mod(md):
            seg = md["seg"]
            if seg == 0:
                pe.wait_ge(silu_c_done, 2)
            at_least(pe, mod_ready, seg - 1)

            def body(i, first, last):
                for j in range(2):
                    pe.wait_ge(mod_in[j], 16 * (seg * 6 + 1) + 16 * i)
                    for half in range(2):
                        col = 8 * i + 4 * j + 2 * half
                        for k in range(KD):
                            ins = pe.matmul(bank[6 + seg % 2][:, bass.ds(col, 2)], mod_raw[:, j, k, half * P:half * P + P],
                                            silu_c[:, k, :], start=k == 0, stop=k == KD - 1)
                    ins.then_inc(mod_done, 1)
            repeat(pe, 6, body)

        def pe_gemm(ph):
            xh, xl = moving_of(ph)
            if ph.kind == "branch":
                xh, xl = O_hi, O_lo
            width, kk = ph.width, ph.k
            m = ph.more.get("moving", "h")
            if ph.kind == "branch":
                pe.wait_ge(o_done, ph.more["pairs"])
            elif m == "y":
                pe.wait_ge(o_done, ph.more["pairs"])
                pe.wait_ge(mix_dve, ph.more["mix_end"])

            def step(i, first, last, n_units=4):
                for u in range(n_units):
                    t = ph.start + u + 4 * i
                    b = (ph.start + u) % 4
                    pe.wait_ge(lo_done, t + 1)
                    if first or ph.more.get("pair"):
                        value = ph.start + 4 * i - (2 if u == 0 else 0)
                    else:
                        value = t - 3
                    at_least(pe, acc_free, value)
                    if ph.kind == "branch":
                        for half in range(2):
                            for k in range(kk):
                                wh = w_hi[:, b, k * 256 + half * P:k * 256 + half * P + P]
                                wl = w_lo[:, b, k * 256 + half * P:k * 256 + half * P + P]
                                o = bank[b][:, half * S:half * S + S]
                                pe.matmul(o, wh, xh[:, 4 * i + k, :], start=k == 0, stop=False)
                                pe.matmul(o, wl, xh[:, 4 * i + k, :], start=False, stop=False)
                                ins = pe.matmul(o, wh, xl[:, 4 * i + k, :], start=False, stop=k == kk - 1)
                    else:
                        for k in range(kk):
                            if first and u == 0 and moving_wait(ph, k):
                                pe.wait_ge(*moving_wait(ph, k))
                            wh, wl = w_hi[:, b, k * P:k * P + P], w_lo[:, b, k * P:k * P + P]
                            o = bank[b][:, 0:width]
                            pe.matmul(o, wh, xh[:, k, 0:width], start=k == 0, stop=False)
                            pe.matmul(o, wl, xh[:, k, 0:width], start=False, stop=False)
                            ins = pe.matmul(o, wh, xl[:, k, 0:width], start=False, stop=k == kk - 1)
                    ins.then_inc(acc_done, 1)
            n4, left = phase_steps(ph)
            if ph.kind == "branch":
                for i in range(n4):
                    step(i, i == 0, i == n4 - 1)
            else:
                repeat(pe, n4, step)
            if left:
                step(n4, False, True, left)

        def pe_norm(nm):
            r, width = nm["r"], nm.get("width", S)
            pe.wait_ge(sq_step, 17 * (r + 1))
            at_least(pe, rms_done, r)
            pe.matmul(STAT[:, 0:width], ones[:, :], sq_sum[:, 0:width], start=True, stop=True).then_inc(stat_done, 1)
            if nm["kind"] == "final":
                pe.wait_ge(acc_free, total)
                for q in range(4):
                    tb, fh = q // 2, q % 2
                    pe.wait_ge(final_mul, KD + 1 + KD)
                    for f4 in range(4):
                        ins = pe.transpose(bank[q][:, f4 * P:f4 * P + P], T2[:, fh * 4 + f4, tb * P:tb * P + P], ident)
                    ins.then_inc(final_t, 1)

        def pe_mixers(mx):
            pe.wait_ge(s_small, 16 + 64 * (mx["layer"] + 1))
            _, bd = (mx["act0"], dict(z=mx["d_z"], pool=mx["d_pool"], end=mx["d_pool"][-1] + 2))
            pe.wait_ge(acc_free, mx["unit_end"])
            for s in range(mx["streams"]):
                pe.wait_ge(mix_dve, bd["pool"][s])
                if s > 0:
                    pe.wait_ge(mix_act, mx["act0"] + 2 * mx["streams"] + 2 * s)
                for j in range(2):
                    pe.matmul(bank[j][:, 0:S], pool_bd[:, j, :], pool_c[:, j, :], start=True, stop=True).then_inc(mix_pe, 1)

        def pe_attend(at_):
            b1 = at_["block"] == 1
            if b1:
                pe.wait_ge(mix_dve, at_["mix_end"])
                layer = at_["layer"]
                pe.wait_ge(s_bias, 16 * 16 * (layer + 1))
                flat = bias_t[:, :, :, :].rearrange("p h r k -> p (h r k)")
                for j in range(6):
                    if j >= 4:
                        pe.wait_ge(bias_done, layer * 6 + j - 3)
                    pe.matmul(bank[j % 4][:, :], table("turn"), flat[:, 512 * j:512 * j + 512], start=True, stop=True) \
                      .then_inc(bias_pe, 1)
                pe.wait_ge(bias_done, layer * 6 + 6)
            else:
                pe.wait_ge(acc_free, at_["unit_end"])
            src = U if b1 else U2
            v_tiles = [16, 17, 18, 19] if b1 else [5] + [14, 15, 16, 17] + [26, 27, 28, 29]
            for j, (tile, nb) in enumerate(at_["vt_jobs"]):
                m = at_["vt0"] + j
                at_least(pe, vt_copy, m - 1)
                for tb in range(nb):
                    ins = pe.transpose(bank[4 + m % 2][:, tb * P:tb * P + P],
                                       src[:, v_tiles[j], tb * P:tb * P + P], ident)
                ins.then_inc(vt_t, 1)
            pe.wait_ge(vt_copy, at_["vt0"] + len(at_["vt_jobs"]))
            if not b1:
                for j in range(13):
                    m = at_["rope0"] + j
                    tile = rope_tiles()[j]
                    at_least(pe, rope_dve, 2 * (m - 1))
                    pe.matmul(bank[6 + m % 2][:, 0:S], rot, U2[:, tile, :], start=True, stop=True).then_inc(rope_pe, 1)
                pe.wait_ge(rope_dve, 2 * (at_["rope0"] + 13))
            for what, call in attend_order(at_):
                if what == "sb":
                    pe_stick(at_)
                else:
                    pe_call(at_, call)

        def pv(e, cols_banks, v_cols, pt, ob, q_lists):
            for idx, (vc, pcols, qcols) in enumerate(q_lists):
                ins = pe.matmul(ob[HD * e:HD * e + HD, qcols[0]:qcols[1]], vt[:, vc:vc + HD], pt[:, pcols[0]:pcols[1]],
                                start=idx == 0, stop=idx == len(q_lists) - 1)
            return ins

        def pe_call(at_, call):
            groups, what = call["groups"], call["what"]
            n_g = len(groups)
            per_head = n_g // 8
            src = U if at_["block"] == 1 else U2
            nb = len(call["score_banks"])
            npt = len(call["pt_banks"])
            at_least(pe, o_done, call["pair0"])
            if what == "swa":
                pe.wait_ge(k_swap_done, call["layer"] + 1)
            at_least(pe, exp_done, call["n0"])
            at_least(pe, pt_copy, call["n0"])
            for j in range(n_g + 1 + per_head):
                if j < n_g:
                    g = groups[j]
                    n, h = g["n"], g["head"]
                    e = h % 2
                    rows_ = slice(HD * e, HD * e + HD)
                    if n - call["n0"] >= nb:
                        pe.wait_ge(exp_done, n - nb + 1)
                    sb_ = bank[call["score_banks"][(n - call["n0"]) % nb]]
                    for si, (qt, a, b) in enumerate(g["segs"]):
                        if what == "near":
                            q = U[rows_, 8 + h // 2, qt * P:qt * P + P]
                            kk = U[rows_, 12 + h // 2, 0:512]
                        elif what == "ctx":
                            q = U[rows_, 8 + h // 2, S + qt * P:S + qt * P + P]
                            kk = U[rows_, 12 + h // 2, S:512]
                        elif what == "swa":
                            q = U2[rows_, h // 2, qt * P:qt * P + P]
                            kk = U2[rows_, 4, 0:b - a] if h // 4 == e else k_swap[rows_, 0:b - a]
                        else:
                            q = U2[rows_, 18 + h // 2, qt * P:qt * P + P]
                            kk = U2[rows_, 22 + h // 2, 0:b - a]
                        ins = pe.matmul(sb_[:, a:b], q, kk, start=True, stop=True)
                    ins.then_inc(sc_done, 1)
                if 1 <= j <= n_g:
                    g = groups[j - 1]
                    n = g["n"]
                    pe.wait_ge(p_ready, n + 1)
                    at_least(pe, pt_copy, n - npt + 1)
                    pb = bank[call["pt_banks"][(n - call["n0"]) % npt]]
                    for bi, (col, kb) in enumerate(g["blocks"]):
                        pc = col + (P * kb if what == "near" else 0)
                        ins = pe.transpose(pb[:, bi * P:bi * P + P], probs[:, n % 4, pc:pc + P], ident)
                    ins.then_inc(pt_done, 1)
                jj = j - 1 - per_head
                if 0 <= jj < n_g and groups[jj]["last"]:
                    g = groups[jj]
                    h, n = g["head"], g["n"]
                    e, hp = h % 2, h // 2
                    pe.wait_ge(pt_copy, n + 1)
                    if e == 0:
                        at_least(pe, o_done, call["pair0"] + hp - len(call["out_banks"]) + 1)
                    ob = out_of(call, hp)
                    if what == "near":
                        ql = [(hp * 512 + kb * P + HD * e, (kb * S, kb * S + S), (0, S)) for kb in range(4)]
                    elif what == "ctx":
                        ql = [(hp * 512 + (2 + kb) * P + HD * e, (kb * S, kb * S + S), (0, S)) for kb in range(2)]
                    else:
                        if what == "swa":
                            v0 = [0 + HD * (h // 4), P + HD * (h // 4)]
                        else:
                            v0 = [(5 + hp) * S + HD * e, (5 + hp) * S + P + HD * e]
                        ql = [(v0[0], (0, S), (0, S)), (v0[1], (S, 384), (P, S))]
                    pv(e, None, None, probs_t[:, e, :], ob, ql).then_inc(pv_done, 1)

        def pe_stick(at_):
            at_least(pe, o_done, at_["sb_pair0"])
            for j in range(4):
                m = at_["sb0"] + j
                at_least(pe, sb_dve, 4 * m)
                for e in range(2):
                    rows_ = slice(HD * e, HD * e + HD)
                    q, kk = U2[rows_, 6 + j, :], U2[rows_, 10 + j, :]
                    pe.matmul(bank[4 + e][:, 0:S], kk[:, 0:P], q, start=True, stop=True)
                    ins = pe.matmul(bank[4 + e][:, S:384], kk[:, P:S], q[:, P:S], start=True, stop=True)
                ins.then_inc(sb_pe, 1)
                pe.wait_ge(sb_dve, 4 * m + 2)
                for e in range(2):
                    pe.matmul(bank[4 + e][:, 0:S], tri, sb_s[:, e, 0:S], start=True, stop=False)
                    pe.matmul(bank[4 + e][:, P:S], ones[:, :], sb_s[:, e, S:384], start=False, stop=True)
                    ins = pe.matmul(bank[4 + e][:, S:384], tri, sb_s[:, e, S:384], start=True, stop=True)
                ins.then_inc(sb_pe, 1)
                pe.wait_ge(sb_act, 4 * m + 4)
                ob = bank[6 + j % 2][:, 0:S]
                at_least(pe, o_done, at_["sb_pair0"] + j - 1)
                for e in range(2):
                    ql = [((1 + j) * S + HD * e, (0, S), (0, S)), ((1 + j) * S + P + HD * e, (S, 384), (P, S))]
                    pv(e, None, None, sb_w[:, e, :], ob, ql).then_inc(pv_done, 1)

        for kind, ph in plan:
            if kind == "mod":
                pe_mod(ph)
            elif kind == "gemm":
                pe_gemm(ph)
            elif kind == "norm":
                pe_norm(ph)
            elif kind == "mixers":
                pe_mixers(ph)
            elif kind == "attend":
                pe_attend(ph)

    stack.close()


INPUTS = ["x", "c", "ctx", "c_ctx", "w_mod", "b_mod", "norm_g", "ffn_w_in", "ffn_w_out", "w_in", "conv_w", "pool_w",
          "pool_scale", "rpb", "w_out", "final_g", "norm_mix_2", "w_in_2", "b_gate_2", "sinks_2", "w_branch_2",
          "w_out_2", "norm_ffn_2", "w_up_2", "conv_w_2", "conv_b_2", "w_down_2", "norm_final_2"]


def kernel(**inputs):
    import numpy as _np
    import concourse.bacc as _bacc
    from concourse.bass_utils import run_bass_kernel_spmd as _run

    nc = _bacc.Bacc("TRN2", target_bir_lowering=False, num_devices=1)
    arrays, aps = {}, {}
    for name in INPUTS:
        arrays[name] = _np.ascontiguousarray(inputs[name])
    arrays["consts"] = CONSTS
    for name, a in arrays.items():
        aps[name] = nc.dram_tensor(name, a.shape, mybir.dt.from_np(a.dtype), kind="ExternalInput").ap()
    aps["out"] = nc.dram_tensor("out", (1, S, D), F32, kind="ExternalOutput").ap()
    build_program(nc, **aps)
    r = _run(nc, [arrays], core_ids=[0])
    return r.results[0]["out"]
```

```python
import concourse.bass as bass
from concourse import mybir
from contextlib import ExitStack
import numpy as np

F32 = mybir.dt.float32
F32R = mybir.dt.float32r
ALU = mybir.AluOpType
ACT = mybir.ActivationFunctionType
AX = mybir.AxisListType
P = 128
D = 1024
KD = D // P
S = 256
DEPTH = 2
DFF = 2816
FT = DFF // P
THIRDS = (8, 8, 6)
EPS = 1e-6
NEG = -1e30
HD = 64
SCALE = HD ** -0.5
N_IN = 20
N_QKV = 30
N_GATE = 24
SLOTS = 4
AHEAD = 3
ROLL = 15 * 31


def constant_table():
    parts = {}
    row = np.arange(P)
    parts["ident"] = np.eye(P)
    rot = np.zeros((P, P))
    for m in range(P):
        if m % HD < HD // 2:
            rot[m + HD // 2, m] = -1.0
        else:
            rot[m - HD // 2, m] = 1.0
    parts["rot"] = rot
    pick = np.zeros((P, 2))
    pick[0:2, 0] = pick[2:4, 1] = 1.0
    parts["pick"] = pick
    parts["turn"] = (row[:, None] // 64 * 64 + 63 - row[:, None] % 64 == row[None, :]).astype(float)
    parts["tri"] = (row[:, None] >= row[None, :]).astype(float)
    inv = (np.float32(10000.0) ** (-np.arange(0, HD, 2, dtype=np.float32) / np.float32(HD))).astype(np.float32)
    ang = np.arange(S, dtype=np.float32)[None, :] * inv[row % (HD // 2)][:, None]
    parts["cos"] = np.cos(ang.astype(np.float32))
    parts["sin"] = np.sin(ang.astype(np.float32))
    causal = np.where(row[None, :] <= row[:, None], 0.0, NEG)
    parts["m_causal"] = np.concatenate([causal, np.zeros((P, P)), causal], 1)
    parts["m_band"] = np.concatenate([causal, np.where(row[None, :] > row[:, None], 0.0, NEG), causal], 1)
    past = np.where(row[:, None] < row[None, :], 0.0, NEG)
    parts["m_past"] = np.concatenate([past, np.zeros((P, P)), past], 1)
    qcol, kcol = row % 64, np.arange(64)
    start = np.clip(qcol - 8, 0, 48)[:, None]
    ok = (kcol[None, :] >= start) & (kcol[None, :] < start + 16)
    parts["m_near"] = np.where(ok, 3.0e38, NEG)
    t = np.arange(S)
    cnt = np.zeros((P, 2, S))
    for g, w in enumerate((2, 4, 8, 16)):
        lo, hi = np.clip(t - w // 2, 0, S), np.clip(t + w - w // 2, 0, S)
        cnt[HD * (g % 2):HD * (g % 2) + HD, g // 2, :] = 1.0 / (hi - lo).astype(np.float32)
    parts["inv_count"] = cnt.reshape(P, 2 * S)
    at, cols = 0, {}
    for name, a in parts.items():
        cols[name] = (at, at + a.shape[1])
        at += a.shape[1]
    return np.concatenate([a.astype(np.float32) for a in parts.values()], 1), cols


CONSTS, CONST_COLS = constant_table()


class Phase:

    def __init__(self, kind, n, k, width, source, start, view="std", **more):
        self.kind, self.n, self.k, self.width, self.source, self.start, self.view = kind, n, k, width, source, start, view
        self.more = more
        self.side = more.get("side", False)
        self.stride = 8 if self.side else 4


def build_program(nc, x, c, ctx, c_ctx, w_mod, b_mod, norm_g, ffn_w_in, ffn_w_out, w_in, conv_w, pool_w,
                  pool_scale, rpb, w_out, final_g, norm_mix_2, w_in_2, b_gate_2, sinks_2, w_branch_2,
                  w_out_2, norm_ffn_2, w_up_2, conv_w_2, conv_b_2, w_down_2, norm_final_2, consts, out):
    K = 1024
    base = 17 * K
    region = {}
    at = base
    for name, size in (("x", 16 * K), ("h", 32 * K), ("g", 40 * K), ("raw", 16 * K), ("hi", 16 * K), ("lo", 16 * K),
                       ("mod", 16 * K), ("bias", 12 * K), ("vt", 9 * K + 256), ("scr", 16 * K)):
        region[name] = at
        at += size
    top = [at]

    def fixed(name, shape, dt, offset):
        return nc.alloc_sbuf_tensor_at(name, shape, dt, offset=offset)

    def small(name, shape, dt=F32):
        t = fixed(name, shape, dt, top[0])
        top[0] += (int(np.prod(shape[1:])) * 4 + 31) // 32 * 32
        return t

    X = fixed("X", [P, KD, 512], F32, region["x"])
    H_hi = fixed("H_hi", [P, KD, 512], F32R, region["h"])
    H_lo = fixed("H_lo", [P, KD, 512], F32R, region["h"] + 16 * K)
    G_hi = fixed("G_hi", [P, 8, 512], F32R, region["g"])
    G_lo = fixed("G_lo", [P, 8, 512], F32R, region["g"] + 16 * K)
    U = fixed("U", [P, N_IN, 512], F32, region["g"])
    T1 = fixed("T1", [P, KD, 512], F32, region["g"])
    pool_a = fixed("pool_a", [P, 2, 280], F32, region["mod"] + 6 * K)
    pool_b = fixed("pool_b", [P, 2, 280], F32, region["mod"] + 6 * K + 2240)
    pool_c = fixed("pool_c", [P, 2, 2, S], F32, region["mod"] + 6 * K + 4480)
    tokens_in = fixed("tokens_in", [P, 4, D], F32, region["g"])
    rows_in = fixed("rows_in", [P, 6, P], F32, region["g"] + 16 * K)
    bias_t = fixed("bias_t", [P, 8, 6, 64], F32, region["bias"])
    c_pad = fixed("c_pad", [P, KD, P], F32R, region["mod"])
    mod_rows = fixed("mod_rows", [P, 2, 256], F32, region["mod"] + 4 * K)
    X2 = fixed("X2", [P, KD, S], F32, region["x"])
    gates = fixed("gates", [P, N_GATE, S], F32, region["x"] + 8 * K)
    H2_hi = fixed("H2_hi", [P, KD, S], F32R, region["x"] + 32 * K)
    H2_lo = fixed("H2_lo", [P, KD, S], F32R, region["x"] + 40 * K)
    U2 = fixed("U2", [P, N_QKV, S], F32, region["g"])
    merged = fixed("merged", [P, KD, S], F32, region["g"] + 30 * K)
    T2 = fixed("T2", [P, KD, S], F32, region["g"])
    G2_hi = fixed("G2_hi", [P, 8, S], F32R, region["g"])
    G2_lo = fixed("G2_lo", [P, 8, S], F32R, region["g"] + 8 * K)
    O_hi = fixed("O_hi", [P, 12, S], F32R, region["mod"])
    O_lo = fixed("O_lo", [P, 12, S], F32R, region["mod"] + 12 * K)
    tokens_out = fixed("tokens_out", [P, 2, D], F32, region["g"] + 16 * K)
    raw = fixed("raw", [P, 2, 2048], F32, region["raw"])
    w_hi = fixed("w_hi", [P, SLOTS, 1024], F32R, region["hi"])
    w_lo = fixed("w_lo", [P, SLOTS, 1024], F32R, region["lo"])
    vt = fixed("vt", [P, 9 * S], F32, region["vt"])
    probs = fixed("probs", [P, 4, 512], F32, region["scr"])
    probs_t = fixed("probs_t", [P, 2, 1024], F32, region["scr"] + 8 * K)
    sil = fixed("sil", [P, 2, 512], F32, region["scr"])
    g32 = fixed("g32", [P, 2, 512], F32, region["scr"] + 4 * K)
    sq = fixed("sq", [P, 512], F32, region["scr"] + 8 * K)
    sq_sum = fixed("sq_sum", [P, 512], F32, region["scr"] + 10 * K)
    rstd = fixed("rstd", [P, 512], F32, region["scr"] + 12 * K)
    sb_z = fixed("sb_z", [P, 2, 2, 384], F32, region["scr"])
    sb_e = fixed("sb_e", [P, 2, 2, 384], F32, region["scr"] + 6 * K)
    k_swap = fixed("k_swap", [P, S], F32, region["scr"] + 14 * K)
    rope_t = fixed("rope_t", [P, 2, S], F32, region["scr"] + 12 * K)

    const = small("const", [P, CONSTS.shape[1]])
    ones = small("ones", [P, P])
    eps = small("eps", [P, 1])
    warm = small("warm", [P, 5 + 8 * DEPTH])
    silu_c = small("silu_c", [P, KD, 2])
    modv = small("modv", [P, 6, 3, KD, 2])
    neg_max = small("neg_max", [P, 16])
    row_sum = small("row_sum", [P, 16])
    row_inv = small("row_inv", [P, 16])
    sink = small("sink", [P, DEPTH * 8])
    sink_e = small("sink_e", [P, 16])
    pool_bd = small("pool_bd", [P, 2, P])
    vec_rows, vec_at = [], {}

    def rows(name, ap):
        vec_at[name] = sum(a.shape[0] for a in vec_rows)
        vec_rows.append(ap)

    rows("c", c.rearrange("b (n p) -> (b n) p", p=P))
    rows("c_ctx", c_ctx.rearrange("(n p) -> n p", p=P))
    rows("b_mod", b_mod.rearrange("l (n p) -> (l n) p", p=P))
    rows("norm_g", norm_g.rearrange("l i (n p) -> (l i n) p", p=P))
    rows("final_g", final_g.rearrange("(n p) -> n p", p=P))
    rows("conv_w", conv_w.rearrange("l w (n p) -> (l w n) p", p=P))
    rows("pool_scale", pool_scale.rearrange("l (n p) -> (l n) p", p=P))
    rows("norm_mix", norm_mix_2.rearrange("l (n p) -> (l n) p", p=P))
    rows("b_gate", b_gate_2.rearrange("l (n p) -> (l n) p", p=P))
    rows("norm_ffn", norm_ffn_2.rearrange("l (n p) -> (l n) p", p=P))
    rows("conv_w_2", conv_w_2.rearrange("l w (n p) -> (l w n) p", p=P))
    rows("conv_b_2", conv_b_2.rearrange("l (n p) -> (l n) p", p=P))
    rows("norm_final", norm_final_2.rearrange("(n p) -> n p", p=P))
    n_rows = sum(a.shape[0] for a in vec_rows)
    n_row_tiles = (n_rows + P - 1) // P
    assert n_row_tiles <= 6, n_rows
    vecs = small("vecs", [P, n_row_tiles * P])
    assert top[0] <= nc.sbuf_usable_end, (top[0], nc.sbuf_usable_end)

    row_pieces = []
    r = 0
    for ap in vec_rows:
        done = 0
        while done < ap.shape[0]:
            n = min(ap.shape[0] - done, P - r % P)
            row_pieces.append((r % P, r // P, n, ap[done:done + n, :]))
            done += n
            r += n

    def vec(name, index, n=1):
        i = vec_at[name] + index
        return vecs[:, bass.ds(i, n)] if not isinstance(i, int) else vecs[:, i:i + n]

    def table(name):
        a, b = CONST_COLS[name]
        return const[:, a:b]

    ident, rot, tri = table("ident"), table("rot"), table("tri")

    bank = [nc.alloc_psum_tensor(f"bank{b}", [P, 512], F32) for b in range(8)]
    STAT = bank[4]

    def sem(name):
        return nc.alloc_semaphore(name)

    raw_in = [sem("raw_in0"), sem("raw_in1")]
    s_const = sem("s_const")
    s_rows = sem("s_rows")
    s_tok = sem("s_tok")
    s_bias = sem("s_bias")
    s_small = sem("s_small")
    s_out = sem("s_out")
    hi_done = sem("hi_done")
    lo_done = sem("lo_done")
    acc_done = sem("acc_done")
    acc_free = sem("acc_free")
    mod_done = sem("mod_done")
    mod_ready = sem("mod_ready")
    mod_step = sem("mod_step")
    silu_done = sem("silu_done")
    g_hi_done = sem("g_hi_done")
    g_lo_done = sem("g_lo_done")
    conv1_done = sem("conv1_done")
    g_mul_done = sem("g_mul_done")
    conv0_done = sem("conv0_done")
    sq_step = sem("sq_step")
    stat_done = sem("stat_done")
    rms_done = sem("rms_done")
    rstd_done = sem("rstd_done")
    n_mul = sem("n_mul")
    n_aff = sem("n_aff")
    h_hi_done = sem("h_hi_done")
    h_lo_done = sem("h_lo_done")
    memset_done = sem("memset_done")
    init_t = sem("init_t")
    init_copy = sem("init_copy")
    silu_c_done = sem("silu_c_done")
    bias_done = sem("bias_done")
    bias_pe = sem("bias_pe")
    mix_pe = sem("mix_pe")
    mix_act = sem("mix_act")
    mix_dve = sem("mix_dve")
    vt_t = sem("vt_t")
    vt_copy = sem("vt_copy")
    sc_done = sem("sc_done")
    bias_add = sem("bias_add")
    max_step = sem("max_step")
    max_done = sem("max_done")
    exp_done = sem("exp_done")
    inv_step = sem("inv_step")
    p_ready = sem("p_ready")
    pt_done = sem("pt_done")
    pt_copy = sem("pt_copy")
    pv_done = sem("pv_done")
    o_step = sem("o_step")
    o_done = sem("o_done")
    sb_scores = sem("sb_scores")
    sb_remain = sem("sb_remain")
    sb_scaled = sem("sb_scaled")
    sb_soft = sem("sb_soft")
    sb_diff = sem("sb_diff")
    sb_log = sem("sb_log")
    sb_weight = sem("sb_weight")
    c_split = sem("c_split")
    mix_pool = sem("mix_pool")
    rope_pe = sem("rope_pe")
    rope_dve = sem("rope_dve")
    rope_pool = sem("rope_pool")
    gate_done = sem("gate_done")
    k_swap_done = sem("k_swap_done")
    merge_step = sem("merge_step")
    final_mul = sem("final_mul")
    final_t = sem("final_t")
    final_copy = sem("final_copy")
    s_store = sem("s_store")

    plan = []
    units = [0]
    hidden = [0]
    mods = [0]
    splits = [0]
    GLU_TILES = 2 * DEPTH * FT

    def gemm(kind, n, k, width, source, view="std", **more):
        ph = Phase(kind, n, k, width, source, units[0], view, **more)
        ph.g0 = hidden[0]
        ph.gm0 = hidden[0] - GLU_TILES
        ph.h0 = splits[0] - KD
        if kind == "branch":
            ph.merge0 = 8 * ph.more["layer"]
            ph.h0 = splits[0]
            splits[0] += KD
        if kind in ("glu", "conv_glu"):
            hidden[0] += (n // 2) // (2 if ph.side else 1)
        if kind == "mod" or ph.side:
            ph.mod0 = mods[0]
            ph.mod_layer = mods[0] // 72
            mods[0] += n // (2 if ph.side else 1)
        units[0] += n
        plan.append(("gemm", ph))
        return ph

    n_norm = [0]
    affines = [0]

    def norm(kind, **more):
        nm = dict(kind=kind, r=n_norm[0], h0=splits[0], a0=affines[0], **more)
        if kind in ("mod", "plain"):
            splits[0] += KD
            affines[0] += KD
        plan.append(("norm", nm))
        n_norm[0] += 1

    def kpc(w2d):
        return w2d.rearrange("(k p) c -> p k c", p=P)

    def pair_source(w, third):
        view = kpc(w)

        def source(j, half):
            return view[:, :, bass.ds(half * DFF + third * 1024 + j * 256, 256)]
        return source

    def plain_source(w, col0=0, k0=0, k=KD):
        view = kpc(w)

        def source(cidx):
            return view[:, k0:k0 + k, bass.ds(col0 + cidx * 256, 256)]
        return source

    def modulation(n):
        gemm("mod", n, KD, None, None)

    def ffn(width, w1, w2, seg, stats, conv_layer=None, side=(), after=0):
        for third, tiles in enumerate(THIRDS):
            with_mod = third in side
            gemm("glu" if conv_layer is None else "conv_glu", (4 if with_mod else 2) * tiles, KD, width,
                 pair_source(w1, third), pair=True, layer=conv_layer, third=third, norm=n_norm[0] - 1, side=with_mod)
            if side and third == max(side):
                if after:
                    modulation(after)
                plan.append(("mod_read", dict(end=mods[0] // 24)))
            gemm("residual", KD, tiles, width, plain_source(w2, 0, third * 8, tiles), seg=seg,
                 stats=stats and third == 2, moving="g", norm_next=n_norm[0], hidden_end=hidden[0])

    n_mod = [0]
    atts = []
    n_mix = [0]

    for layer in range(DEPTH):
        last = layer == DEPTH - 1
        if not last:
            modulation(24)
            plan.append(("mod_read", dict(end=1)))
        norm("mod", width=512, seg=layer * 3)
        ffn(512, ffn_w_in[layer, 0], ffn_w_out[layer, 0], layer * 3, True, side=(0,) if last else (0, 1, 2),
            after=8 if last else 4)
        norm("mod", width=512, seg=layer * 3 + 1)
        if last:
            gemm("store", 12, KD, S, plain_source(w_in[layer]), moving="h", dst="U", f0=0, norm=n_norm[0] - 1)
            gemm("store", 8, KD, 512, plain_source(w_in[layer], 1536), moving="h", dst="U", f0=12, norm=n_norm[0] - 1)
        else:
            gemm("store", N_IN, KD, 512, plain_source(w_in[layer]), moving="h", dst="U", f0=0, norm=n_norm[0] - 1)
        plan.append(("mixers", dict(layer=layer, streams=1 if last else 2, index=layer)))
        plan.append(("attend", dict(block=1, layer=layer, streams=1 if last else 2)))
        width = S if last else 512
        gemm("residual", KD, KD, width, plain_source(w_out[layer]), seg=layer * 3 + 1, stats=True, moving="y",
             norm_next=n_norm[0])
        norm("mod", width=width, seg=layer * 3 + 2)
        ffn(width, ffn_w_in[layer, 1], ffn_w_out[layer, 1], layer * 3 + 2, True, side=() if last else (0, 1, 2),
            after=0 if last else 4)
    norm("renorm", gain=("final_g", 0))
    for layer in range(DEPTH):
        norm("plain", gain=("norm_mix", layer * KD))
        gemm("store", N_QKV, KD, S, plain_source(w_in_2[layer]), moving="h", dst="U2", f0=0, norm=n_norm[0] - 1)
        gemm("gate", N_GATE, KD, S, plain_source(w_in_2[layer], N_QKV * P), moving="h", layer=layer)
        plan.append(("attend", dict(block=2, layer=layer, streams=1)))
        br = w_branch_2[layer]

        def branch_source(cidx, br=br):
            return br[cidx // 2].rearrange("(k p) c -> p k c", p=P)[:, :, 512 * (cidx % 2):512 * (cidx % 2) + 512]
        gemm("branch", 12, 4, S, branch_source, view="branch", layer=layer)
        gemm("residual", KD, KD, S, plain_source(w_out_2[layer]), seg=None, stats=True, moving="merged",
             norm_next=n_norm[0])
        norm("plain", gain=("norm_ffn", layer * KD))
        ffn(S, w_up_2[layer], w_down_2[layer], None, True, conv_layer=layer)
    norm("final", gain=("norm_final", 0))
    total = units[0]
    assert mods[0] == 144
    phases = [p for kind, p in plan if kind == "gemm"]
    for a, b in zip(phases, phases[1:] + [None]):
        a.next = b
    unit_view = {}
    for ph in phases:
        for t in range(ph.start, ph.start + ph.n):
            unit_view[t] = ph.view

    calls = []

    def attention(**a):
        calls.append(a)
        return a

    counts = dict(group=0, seg=0, pair=0, head=0, vt=0, sb=0, rope=0)
    for kind, ph in plan:
        if kind != "attend":
            continue
        ph["vt0"] = counts["vt"]
        ph["calls"] = []
        b1 = ph["block"] == 1
        if b1:
            ph["vt_jobs"] = [(tile, 4) for tile in range(4)]
            todo = (["ctx"] if ph["streams"] == 2 else []) + ["near"]
        else:
            ph["vt_jobs"] = [(tile, 2) for tile in range(9)]
            todo = ["swa", "moba"]
        counts["vt"] += len(ph["vt_jobs"])
        ph["rope0"] = counts["rope"]
        if not b1:
            counts["rope"] += 13
        if not b1:
            ph["sb0"] = counts["sb"]
            counts["sb"] += 4
            ph["sb_pair0"] = counts["pair"]
            counts["pair"] += 4
        for what in todo:
            groups = []
            for head in range(8):
                if what == "near":
                    for qt in range(2):
                        groups.append(dict(head=head, segs=[(qt, 0, 512)], blocks=[(0, kb) for kb in range(4)],
                                           last=qt == 1, qt=qt))
                elif what == "ctx":
                    groups.append(dict(head=head, segs=[(0, 0, 256), (1, 256, 512)],
                                       blocks=[(256 * qt + 128 * kb, kb) for kb in range(2) for qt in range(2)],
                                       last=True, qt=None))
                else:
                    groups.append(dict(head=head, segs=[(0, 0, 128), (1, 128, 384)],
                                       blocks=[(0, 0), (128, 0), (256, 1)], last=True, qt=None))
            for g in groups:
                g["n"] = counts["group"]
                counts["group"] += 1
                g["seg0"] = counts["seg"]
                counts["seg"] += len(g["segs"])
            call = dict(what=what, groups=groups, pair0=counts["pair"], head0=counts["head"], layer=ph["layer"],
                        n0=groups[0]["n"])
            call.update(score_banks=[0, 1, 2, 3], pt_banks=[4, 5], out_banks=[6, 7])
            counts["pair"] += 4
            counts["head"] += 8
            ph["calls"].append(call)

    unit_at = mix_d = mix_a = mix_p = 0
    max_count = inv_count = 0
    mix_end = pairs_end = mix_q = pool_end = mod_reads = 0
    for kind, ph in plan:
        if kind == "mod_read":
            mod_reads = ph["end"]
        elif kind == "gemm":
            unit_at = ph.start + ph.n
            ph.more["reads"] = mod_reads
            ph.more["pairs"], ph.more["mix_end"], ph.more["pool_end"] = pairs_end, mix_end, pool_end
        elif kind == "mixers":
            n_s = ph["streams"]
            ph.update(dve0=mix_d, act0=mix_a, pe0=mix_p, unit_end=unit_at)
            ph["d_z"] = mix_d + 1
            mix_end = mix_d = mix_d + 1 + 4 * n_s + 3
            ph["pool0"], ph["mix_end"] = mix_q, mix_d
            ph["q_pool"] = [mix_q + 12 * s + 12 for s in range(n_s)]
            mix_q += 12 * n_s + 2
            pool_end = mix_q
            mix_a += 4 * n_s
            mix_p += 2 * n_s
            mixed = ph
        elif kind == "attend":
            ph.update(unit_end=unit_at, mix_end=mix_end)
            if ph["block"] == 1:
                ph["mixed"] = mixed
            for call in ph["calls"]:
                for g in call["groups"]:
                    max_count += call["what"] in ("ctx", "swa")
                    inv_count += 2 if call["what"] == "swa" else 1
                    g["max_count"], g["inv_count"] = max_count, inv_count
            pairs_end = ph["calls"][-1]["pair0"] + 4

    def attend_order(at_):
        if at_["block"] == 1:
            return [(call["what"], call) for call in at_["calls"]]
        return [("sb", None)] + [(call["what"], call) for call in at_["calls"]]

    def rope_tiles():
        return [0, 1, 2, 3, 4, 18, 19, 20, 21, 22, 23, 24, 25]

    def out_tiles(call, hp):
        what = call["what"]
        if what == "near":
            return H_hi[:, 4 + hp, 0:S], H_lo[:, 4 + hp, 0:S]
        if what == "ctx":
            return H_hi[:, 4 + hp, S:512], H_lo[:, 4 + hp, S:512]
        f = hp + (0 if what == "swa" else 8)
        return O_hi[:, f, :], O_lo[:, f, :]

    def out_of(call, hp):
        return bank[call["out_banks"][hp % len(call["out_banks"])]][:, 0:S]

    T_LAG = 3

    def mod_unit(ph, u):
        if ph.kind == "mod":
            return u
        return {0: 0, 1: 1, 4: 2, 5: 3}.get(u) if ph.side else None

    def own_unit(ph, u):
        return {2: 0, 3: 1, 6: 2, 7: 3}.get(u) if ph.side else u

    def mod_bank(ph, u):
        return bank[5 + u // 4] if ph.side else bank[(ph.start + u) % 4]

    def mod_source(ph, i, j):
        first = ph.mod0 - 72 * ph.mod_layer
        return kpc(w_mod[ph.mod_layer])[:, :, bass.ds((first + 4 * i + 2 * j) * P, 256)]

    def moving_wait(ph, k):
        m = ph.more.get("moving", "h")
        if ph.kind == "branch" or m == "y":
            return None
        if m == "g":
            return g_lo_done, ph.more["hidden_end"] - ph.k + k + 1
        return h_lo_done, ph.h0 + k + 1

    def repeat(eng, n, body, peel_last=False):
        body(0, True, n == 1)
        stop = n - 1 if peel_last else n
        if stop > 2:
            with eng.Fori(1, stop) as i:
                body(i, False, False)
        elif stop == 2:
            body(1, False, n == 2)
        if peel_last and n > 1 and stop >= 1:
            body(n - 1, False, True)

    def at_least(eng, semaphore, value):
        if isinstance(value, int) and value <= 0:
            return
        eng.wait_ge(semaphore, value)

    def needs_peel(ph):
        return ph.next is None or ph.next.view != ph.view

    def half_view(tensor_ap, view, half):
        if view == "std":
            return tensor_ap.rearrange("p (k c) -> p k c", c=256)[:, :, half * P:half * P + P]
        return tensor_ap.rearrange("p (k c) -> p k c", c=512)[:, :, half * 256:half * 256 + 256]

    def slot_view(tensor_ap, view):
        return tensor_ap.rearrange("p (k c) -> p k c", c=P if view == "std" else 256)

    def phase_steps(ph):
        return ph.n // ph.stride, ph.n % ph.stride

    def moving_of(ph):
        m = ph.more.get("moving", "h")
        if ph.kind in ("glu",) or (m == "h" and ph.more.get("dst") == "U") or m == "y":
            return H_hi, H_lo
        if m == "g":
            return (G_hi, G_lo) if ph.more["seg"] is not None else (G2_hi, G2_lo)
        return H2_hi, H2_lo

    def q_tile(what):
        return dict(near=8, ctx=8, swa=0, sb=6, moba=18)[what]

    stack = ExitStack()
    blk = stack.enter_context(nc.Block())

    @blk.sync
    def _(sp):
        sp.dma_start(const[:, :], consts).then_inc(s_const, 16)
        for p0, tile, n, ap in row_pieces:
            sp.dma_start(rows_in[p0:p0 + n, tile, :], ap).then_inc(s_rows, 16)
        sp.dma_start(tokens_in[:, 0:2, :], x.rearrange("b (t p) d -> p (b t) d", p=P)).then_inc(s_tok, 16)
        sp.dma_start(tokens_in[:, 2:4, :], ctx.rearrange("b (t p) d -> p (b t) d", p=P)).then_inc(s_tok, 16)

        def load(ph, chunk, source_ap):
            slot = (ph.start // 2 + chunk[1]) % 2
            at_least(sp, lo_done, 2 * chunk[0] - 2)
            kk, cc = source_ap.shape[1], source_ap.shape[2]
            dst = raw[:, slot, 0:kk * cc].rearrange("p (k c) -> p k c", c=cc)
            sp.dma_start(dst, source_ap).then_inc(raw_in[slot], 16)

        for kind, ph in plan:
            if kind != "gemm":
                continue
            c0 = ph.start // 2
            if ph.kind == "branch":
                for i in range(6):
                    load(ph, (c0 + i, i), ph.source(i))
                continue

            def body(i, first, last):
                c = c0 + ph.stride // 2 * i
                if ph.kind == "mod":
                    load(ph, (c, 0), mod_source(ph, i, 0))
                    load(ph, (c + 1, 1), mod_source(ph, i, 1))
                elif ph.more.get("pair"):
                    if ph.side:
                        load(ph, (c, 0), mod_source(ph, i, 0))
                        load(ph, (c + 1, 1), ph.source(i, 0))
                        load(ph, (c + 2, 0), mod_source(ph, i, 1))
                        load(ph, (c + 3, 1), ph.source(i, 1))
                    else:
                        load(ph, (c, 0), ph.source(i, 0))
                        load(ph, (c + 1, 1), ph.source(i, 1))
                else:
                    load(ph, (c, 0), ph.source(2 * i))
                    load(ph, (c + 1, 1), ph.source(2 * i + 1))
            steps, left = phase_steps(ph)
            repeat(sp, steps, body)
            if left:
                load(ph, (c0 + 2 * steps, 0), ph.source(2 * steps))
        sp.wait_ge(final_copy, 4)
        sp.dma_start(out.rearrange("b (t p) d -> p (b t) d", p=P), tokens_out[:, :, :]).then_inc(s_store, 16)
        sp.wait_ge(s_store, 16)

    @blk.scalar
    def _(act):
        def split(ph, u, i, view):
            t_static = ph.start + u + AHEAD
            tmod = t_static % 4
            slot, half = tmod // 2, tmod % 2
            act.wait_ge(raw_in[slot], 16 * (t_static // 4 + 1) + 4 * ph.stride * i)
            at_least(act, acc_done, ph.start + u + AHEAD - 3 + ph.stride * i)
            act.activation(slot_view(w_hi[:, tmod, :], view), half_view(raw[:, slot, :], view, half),
                           ACT.Copy).then_inc(hi_done, 1)

        def split_ahead(ph, u, i, last):
            if isinstance(i, int) and ph.start + ph.stride * i + u + AHEAD >= total:
                return
            view = ph.view
            if isinstance(i, int):
                view = unit_view[ph.start + ph.stride * i + u + AHEAD]
            split(ph, u, i, view)

        act.wait_ge(init_copy, n_row_tiles)
        for s, name in enumerate(("c", "c_ctx")):
            act.activation(silu_c[:, :, s], vec(name, 0, KD), ACT.Silu).then_inc(silu_c_done, 1)
        act.wait_ge(silu_c_done, 2)
        act.wait_ge(memset_done, 3)
        for s in range(2):
            act.activation(c_pad[:, :, 2 * s], silu_c[:, :, s], ACT.Copy).then_inc(c_split, 1)
        for t in range(AHEAD):
            act.wait_ge(raw_in[t // 2], 16)
            act.activation(slot_view(w_hi[:, t, :], "std"), half_view(raw[:, t // 2, :], "std", t % 2),
                           ACT.Copy).then_inc(hi_done, 1)

        def act_gemm(ph):
            k = ph.kind
            width = ph.width

            def step(i, first, last, n_units=ph.stride):
                for u in range(n_units):
                    t = ph.start + u + ph.stride * i
                    split_ahead(ph, u, i, last)
                    if mod_unit(ph, u) is not None:
                        continue
                    v = own_unit(ph, u)
                    b = (ph.start + v) % 4
                    if k == "glu":
                        step_end = ph.start + ph.stride * (i + 1)
                        if v < 2:
                            act.wait_ge(acc_done, t + 1)
                            at_least(act, acc_free, step_end - ph.stride - 2 + 2 * v)
                            act.activation(sil[:, v, 0:width], bank[b][:, 0:width], ACT.Silu).then_inc(silu_done, 1)
                        else:
                            act.wait_ge(acc_free, step_end + 2 * (v - 3))
                            act.activation(G_hi[:, 2 * i + v - 2, 0:width], g32[:, v - 2, 0:width],
                                           ACT.Copy).then_inc(g_hi_done, 1)
                    elif k == "conv_glu":
                        layer, third = ph.more["layer"], ph.more["third"]
                        f = (0 if u < 2 else FT) + third * 8 + 2 * i + u % 2
                        g = ph.g0 + 2 * i + u % 2
                        if u == 1:
                            silu_conv(ph, i, 0)
                        if u == 2:
                            silu_conv(ph, i, 1)
                        act.wait_ge(acc_done, t + 1)
                        if u < 2:
                            at_least(act, g_mul_done, g - GLU_TILES - 1)
                            dst = sil
                        else:
                            at_least(act, g_lo_done, g - 1)
                            dst = g32
                        act.activation(dst[:, u % 2, 0:S], bank[b][:, 0:S], ACT.Identity,
                                       scale=vec("conv_w_2", (layer * 3 + 2) * 2 * FT + f),
                                       bias=vec("conv_b_2", layer * 2 * FT + f)).then_inc(conv0_done, 1)
                        if u == 3:
                            for e in range(2):
                                gg = ph.gm0 + 2 * i + e
                                act.wait_ge(g_mul_done, gg + 1)
                                act.activation(G2_hi[:, 2 * i + e, :], g32[:, e, 0:S], ACT.Copy).then_inc(g_hi_done, 1)
                    elif k == "gate":
                        act.wait_ge(acc_done, t + 1)
                        act.activation(gates[:, 4 * i + u, :], bank[b][:, 0:S], ACT.Sigmoid,
                                       bias=vec("b_gate", ph.more["layer"] * N_GATE + 4 * i + u)).then_inc(gate_done, 1)
                    elif k == "branch" and i == 2:
                        for e in range(2):
                            f = 2 * u + e
                            act.wait_ge(merge_step, ph.merge0 + 4 + u + 1)
                            ins = act.activation(H2_hi[:, f, :], merged[:, f, :], ACT.Copy)
                        ins.then_inc(h_hi_done, 2)
            n4, left = phase_steps(ph)
            if k == "branch":
                for i in range(n4):
                    step(i, i == 0, i == n4 - 1)
            else:
                repeat(act, n4, step, needs_peel(ph) and not left)
            if left:
                step(n4, False, True, left)

        def silu_conv(ph, i, e):
            act.wait_ge(acc_free, ph.start + 4 * i + e + 1)
            act.activation(sil[:, e, 0:S], sil[:, e, 0:S], ACT.Silu).then_inc(silu_done, 1)

        def act_norm(nm):
            r, width = nm["r"], nm.get("width", S)
            act.activation(warm[:, r:r + 1], eps[:, 0:1], ACT.Sqrt)
            act.wait_ge(stat_done, r + 1)
            act.activation(rstd[:, 0:width], STAT[:, 0:width], ACT.Sqrt, scale=1.0 / D, bias=eps[:, 0:1]) \
               .then_inc(rms_done, 1)
            if nm["kind"] == "mod":
                seg = nm["seg"]
                for k in range(KD):
                    act.wait_ge(n_mul, nm["a0"] + k + 1)
                    for s in range(width // S):
                        ins = act.activation(T1[:, k, s * S:s * S + S], T1[:, k, s * S:s * S + S], ACT.Identity,
                                             scale=modv[:, seg, 1, k, s:s + 1], bias=modv[:, seg, 0, k, s:s + 1])
                    ins.then_inc(n_aff, 1)
            elif nm["kind"] == "plain":
                name, at0 = nm["gain"]
                for k in range(KD):
                    act.wait_ge(n_mul, nm["a0"] + k + 1)
                    act.activation(T2[:, k, :], T2[:, k, :], ACT.Copy, scale=vec(name, at0 + k)).then_inc(n_aff, 1)

        def act_mixers(mx):
            layer = mx["layer"]
            for s in range(mx["streams"]):
                cols = slice(s * S, s * S + S)
                for j in range(2):
                    act.wait_ge(mix_dve, mx["d_z"])
                    act.activation(U[:, 4 + j, cols], U[:, j, cols], ACT.Copy,
                                   scale=vec("conv_w", (layer * 3 + 1) * 2 + j)).then_inc(mix_act, 1)

        def act_pooled(mx):
            layer = mx["layer"]
            for s in range(mx["streams"]):
                for j in range(2):
                    act.wait_ge(mix_pe, mx["pe0"] + 2 * s + j + 1)
                    act.activation(U[:, 6 + j, s * S:s * S + S], bank[2 * s + j][:, 0:S], ACT.Copy,
                                   scale=vec("pool_scale", layer * 2 + j)).then_inc(mix_act, 1)

        def act_attend(at_):
            for what, call in attend_order(at_):
                if what == "sb":
                    act_stick(at_)
                else:
                    act_call(call)
            if at_["block"] == 1:
                act_pooled(at_["mixed"])

        def act_call(call):
            groups = call["groups"]
            n_g = len(groups)
            for j in range(n_g + T_LAG):
                if j >= T_LAG:
                    g = groups[j - T_LAG]
                    n = g["n"]
                    act.wait_ge(pt_done, n + 1)
                    head = 2 * call["pair0"] + g["head"]
                    at_least(act, pv_done, head - 1)
                    pb = bank[call["pt_banks"][(n - call["n0"]) % len(call["pt_banks"])]]
                    e = g["head"] % 2
                    if g["qt"] is None:
                        w = P * len(g["blocks"])
                        act.activation(probs_t[:, e, 0:w], pb[:, 0:w], ACT.Copy).then_inc(pt_copy, 1)
                    else:
                        dst = probs_t[:, e, :].rearrange("p (k q) -> p k q", q=S)[:, :, g["qt"] * P:g["qt"] * P + P]
                        act.activation(dst, pb[:, :].rearrange("p (k q) -> p k q", q=P), ACT.Copy).then_inc(pt_copy, 1)
                if j < n_g:
                    g = groups[j]
                    n = g["n"]
                    act.wait_ge(max_done, n + 1)
                    at_least(act, pt_done, n - 3)
                    for si, (qt, a, b) in enumerate(g["segs"]):
                        col = (g["seg0"] + si) % 16
                        ins = act.activation(probs[:, n % 4, a:b], bank[call["score_banks"][(n - call["n0"]) % len(call["score_banks"])]][:, a:b],
                                             ACT.Exp, bias=neg_max[:, col:col + 1],
                                             scale=SCALE if call["what"] == "ctx" else 1.0,
                                             accum_out=row_sum[:, col:col + 1])
                        if call["what"] == "swa":
                            h = call["layer"] * 8 + g["head"]
                            ins = act.activation(sink_e[:, col:col + 1], sink[:, h:h + 1], ACT.Exp,
                                                 bias=neg_max[:, col:col + 1])
                    ins.then_inc(exp_done, 1)

        def act_stick(at_):
            for j in range(5):
                if j < 4:
                    m = at_["sb0"] + j
                    e_ = sb_e[:, j % 2, :, :]
                    act.wait_ge(sb_scaled, m + 1)
                    at_least(act, sb_remain, m - 1)
                    act.activation(e_, sb_z[:, j % 2, :, :], ACT.Abs).then_inc(sb_log, 1)
                    act.wait_ge(sb_log, 3 * m + 1)
                    act.activation(e_, e_, ACT.Exp, scale=-1.0).then_inc(sb_log, 1)
                    act.wait_ge(sb_log, 3 * m + 2)
                    act.activation(e_, e_, ACT.Ln, bias=ones[:, 0:1]).then_inc(sb_log, 1)
                if j >= 1:
                    m = at_["sb0"] + j - 1
                    z_ = sb_z[:, (j - 1) % 2, :, :]
                    act.wait_ge(sb_diff, m + 1)
                    act.activation(z_, z_, ACT.Exp).then_inc(sb_weight, 1)

        for kind, ph in plan:
            if kind == "gemm":
                act_gemm(ph)
            elif kind == "norm":
                act_norm(ph)
            elif kind == "mixers":
                act_mixers(ph)
            elif kind == "attend":
                act_attend(ph)

    @blk.vector
    def _(dve):
        def split_ahead(ph, u, i):
            if isinstance(i, int) and ph.start + ph.stride * i + u + AHEAD >= total:
                return
            view = ph.view if not isinstance(i, int) else unit_view[ph.start + ph.stride * i + u + AHEAD]
            tmod = (ph.start + u + AHEAD) % 4
            slot, half = tmod // 2, tmod % 2
            dve.wait_ge(hi_done, ph.start + u + AHEAD + 1 + ph.stride * i)
            dve.tensor_tensor(slot_view(w_lo[:, tmod, :], view), half_view(raw[:, slot, :], view, half),
                              slot_view(w_hi[:, tmod, :], view).bitcast(F32), ALU.subtract).then_inc(lo_done, 1)

        for tile in range(n_row_tiles):
            dve.wait_ge(init_t, tile + 1)
            used = min(P, n_rows - tile * P)
            dve.tensor_copy(vecs[:, tile * P:tile * P + used], bank[4 + tile % 2][:, 0:used]).then_inc(init_copy, 1)
        for f in range(KD):
            dve.wait_ge(init_t, n_row_tiles + f + 1)
            dve.tensor_copy(X[:, f, :], bank[f % 4][:, :]).then_inc(init_copy, 1)
        for t in range(AHEAD):
            dve.wait_ge(hi_done, t + 1)
            dve.tensor_tensor(slot_view(w_lo[:, t, :], "std"), half_view(raw[:, t // 2, :], "std", t % 2),
                              slot_view(w_hi[:, t, :], "std").bitcast(F32), ALU.subtract).then_inc(lo_done, 1)

        dve.wait_ge(c_split, 2)
        for s in range(2):
            ins = dve.tensor_tensor(c_pad[:, :, 2 * s + 1], silu_c[:, :, s], c_pad[:, :, 2 * s].bitcast(F32), ALU.subtract)
        ins.then_inc(c_split, 1)

        def dve_mod(seg):
            layer, i = seg // 3, seg % 3
            src = bank[7][:, seg * 48:seg * 48 + 48].rearrange("p (n s) -> p n s", s=2)
            dst = modv[:, seg, :, :, :].rearrange("p a k s -> p (a k) s")
            for s in range(2):
                ins = dve.tensor_tensor(dst[:, :, s], src[:, :, s], vec("b_mod", layer * 72 + i * 24, 24), ALU.add)
            ins.then_inc(mod_step, 1)
            dve.wait_ge(mod_step, seg + 1)
            for s in range(2):
                ins = dve.scalar_tensor_tensor(modv[:, seg, 1, :, s], modv[:, seg, 1, :, s], 1.0,
                                               vec("norm_g", layer * 24 + i * 8, KD), ALU.add, ALU.mult)
            if i != 1:
                ins = dve.tensor_scalar(modv[:, seg, 2, :, :], modv[:, seg, 2, :, :], 0.5, None, ALU.mult)
            ins.then_inc(mod_ready, 1)

        done_segs = [0]

        def dve_gemm(ph):
            k, width = ph.kind, ph.width
            if k == "residual":
                dve.wait_ge(acc_free, ph.start)
                if ph.more["seg"] is not None:
                    dve.wait_ge(mod_ready, ph.more["seg"] + 1)

            def step(i, first, last, n_units=ph.stride):
                for u in range(n_units):
                    t = ph.start + u + ph.stride * i
                    split_ahead(ph, u, i)
                    mu, v = mod_unit(ph, u), own_unit(ph, u)
                    if mu is not None:
                        if mu % 2:
                            dve.wait_ge(acc_done, t + 1)
                            at_least(dve, mod_done, ph.mod0 + 4 * i - 3 + mu)
                            dve.tensor_copy(mod_rows[:, mu // 2, :], mod_bank(ph, u - 1)[:, 0:256]).then_inc(acc_free, 2)
                        continue
                    b = (ph.start + v) % 4
                    if k == "glu":
                        if v >= 2:
                            g = ph.g0 + 2 * i + v - 2
                            dve.wait_ge(acc_done, t + 1)
                            dve.wait_ge(silu_done, g + 1)
                            at_least(dve, g_lo_done, g - 1)
                            dve.tensor_tensor(g32[:, v - 2, 0:width], bank[b][:, 0:width], sil[:, v - 2, 0:width],
                                              ALU.mult).then_inc(acc_free, 2)
                    elif k == "conv_glu":
                        layer, third = ph.more["layer"], ph.more["third"]
                        f = (0 if u < 2 else FT) + third * 8 + 2 * i + u % 2
                        dst = (sil if u < 2 else g32)[:, u % 2, 0:S]
                        m = 2 * ph.gm0 + 4 * i + u
                        dve.wait_ge(conv0_done, m + 1)
                        dve.scalar_tensor_tensor(dst[:, 1:S], bank[b][:, 0:S - 1],
                                                 vec("conv_w_2", (layer * 3 + 1) * 2 * FT + f), dst[:, 1:S],
                                                 ALU.mult, ALU.add).then_inc(conv1_done, 1)
                        dve.wait_ge(conv1_done, m + 1)
                        dve.scalar_tensor_tensor(dst[:, 2:S], bank[b][:, 0:S - 2],
                                                 vec("conv_w_2", layer * 3 * 2 * FT + f), dst[:, 2:S],
                                                 ALU.mult, ALU.add).then_inc(acc_free, 1)
                        if u >= 2:
                            dve.wait_ge(acc_free, t + 1)
                            dve.wait_ge(silu_done, ph.g0 + 2 * i + u - 1)
                            dve.tensor_tensor(g32[:, u - 2, 0:S], g32[:, u - 2, 0:S], sil[:, u - 2, 0:S], ALU.mult) \
                               .then_inc(g_mul_done, 1)
                    elif k == "residual":
                        f = 4 * i + u
                        dve.wait_ge(acc_done, t + 1)
                        if ph.more["seg"] is None:
                            dve.tensor_tensor(X2[:, f, :], bank[b][:, 0:S], X2[:, f, :], ALU.add).then_inc(acc_free, 1)
                        else:
                            for s in range(width // S):
                                cols = slice(s * S, s * S + S)
                                ins = dve.scalar_tensor_tensor(X[:, f, cols], bank[b][:, cols],
                                                               modv[:, ph.more["seg"], 2, f, s:s + 1], X[:, f, cols],
                                                               ALU.mult, ALU.add)
                            ins.then_inc(acc_free, 1)
                    elif k == "store":
                        f = ph.more["f0"] + 4 * i + u
                        dst = U if ph.more["dst"] == "U" else U2
                        dve.wait_ge(acc_done, t + 1)
                        dve.tensor_copy(dst[:, f, 0:width], bank[b][:, 0:width]).then_inc(acc_free, 1)
                    elif k == "gate":
                        dve.wait_ge(gate_done, ph.more["layer"] * N_GATE + 4 * i + u + 1)
                        dve.wait_ge(acc_free, t)
                        dve.nop().then_inc(acc_free, 1)
                    elif k == "branch":
                        g = gates[:, 8 * i + 2 * u:8 * i + 2 * u + 2, :].rearrange("p f t -> p (f t)")
                        m = merged[:, 2 * u:2 * u + 2, :].rearrange("p f t -> p (f t)")
                        tmp = sil[:, u % 2, :]
                        dve.wait_ge(acc_done, t + 1)
                        if i == 0:
                            dve.tensor_tensor(m, bank[b][:, :], g, ALU.mult).then_inc(acc_free, 1)
                        else:
                            dve.tensor_tensor(tmp, bank[b][:, :], g, ALU.mult).then_inc(acc_free, 1)
                            dve.wait_ge(acc_free, t + 1)
                            dve.tensor_tensor(m, m, tmp, ALU.add).then_inc(merge_step, 1)
                            dve.wait_ge(merge_step, ph.merge0 + 4 * (i - 1) + u + 1)
            n4, left = phase_steps(ph)
            if k == "branch":
                for i in range(n4):
                    step(i, i == 0, i == n4 - 1)
            else:
                repeat(dve, n4, step, needs_peel(ph) and not left)
            if left:
                step(n4, False, True, left)

        def dve_norm(nm):
            r, width, kind = nm["r"], nm.get("width", S), nm["kind"]
            dve.wait_ge(rms_done, r + 1)
            dve.reciprocal(rstd[:, 0:width], rstd[:, 0:width]).then_inc(rstd_done, 1)
            dve.wait_ge(rstd_done, r + 1)
            if kind in ("mod", "plain"):
                src, dst, hi = (X, T1, H_hi) if kind == "mod" else (X2, T2, H2_hi)
                if kind == "mod":
                    dve.wait_ge(mod_ready, nm["seg"] + 1)
                m0 = nm["a0"]
                for k in range(KD + 2):
                    if k < KD:
                        dve.tensor_tensor(dst[:, k, 0:width], src[:, k, 0:width], rstd[:, 0:width], ALU.mult) \
                           .then_inc(n_mul, 1)
                    if k >= 2:
                        dve.wait_ge(n_aff, m0 + k - 1)
                        dve.tensor_copy(hi[:, k - 2, 0:width], dst[:, k - 2, 0:width]).then_inc(h_hi_done, 1)
            else:
                name, at0 = nm["gain"]
                for k in range(KD):
                    src, dst = (X, X2) if kind == "renorm" else (X2, T2)
                    if kind == "renorm":
                        dst = T2
                    dve.scalar_tensor_tensor(dst[:, k, :], src[:, k, 0:S], vec(name, at0 + k), rstd[:, 0:S],
                                             ALU.mult, ALU.mult).then_inc(final_mul, 1)
                if kind == "renorm":
                    dve.wait_ge(final_mul, KD)
                    dve.tensor_copy(X2[:, :, :], T2[:, :, :]).then_inc(final_mul, 1)

        def dve_mixers(mx):
            layer, streams = mx["layer"], mx["streams"]
            w = streams * S
            n = [mx["dve0"]]

            def step(ins):
                ins.then_inc(mix_dve, 1)
                n[0] += 1
                dve.wait_ge(mix_dve, n[0])
            dve.wait_ge(acc_free, mx["unit_end"])
            dve.wait_ge(acc_done, mx["unit_end"])
            step(dve.tensor_tensor(U[:, 0:2, 0:w], U[:, 4:6, 0:w], U[:, 0:2, 0:w], ALU.mult))
            assert n[0] == mx["d_z"]
            for s in range(streams):
                a = s * S
                for j in range(2):
                    dve.wait_ge(mix_act, mx["act0"] + 2 * s + j + 1)
                    step(dve.scalar_tensor_tensor(U[:, 4 + j, a + 1:a + S], U[:, j, a:a + S - 1],
                                                  vec("conv_w", layer * 6 + j), U[:, 4 + j, a + 1:a + S],
                                                  ALU.mult, ALU.add))
                    step(dve.scalar_tensor_tensor(U[:, 4 + j, a:a + S - 1], U[:, j, a + 1:a + S],
                                                  vec("conv_w", layer * 6 + 4 + j), U[:, 4 + j, a:a + S - 1],
                                                  ALU.mult, ALU.add))
            step(dve.tensor_tensor(U[:, 4:6, 0:w], U[:, 4:6, 0:w], U[:, 2:4, 0:w], ALU.mult))
            step(dve.tensor_copy(H_hi[:, 0:2, 0:w], U[:, 4:6, 0:w]))
            step(dve.tensor_tensor(H_lo[:, 0:2, 0:w], U[:, 4:6, 0:w], H_hi[:, 0:2, 0:w].bitcast(F32), ALU.subtract))
            assert n[0] == mx["mix_end"]

        def dve_bias(layer):
            near = table("m_near").unsqueeze(1).to_broadcast([P, 8, 64])
            flat = bias_t[:, :, :, :].rearrange("p h r k -> p (h r) k")
            for j in range(6):
                dve.wait_ge(bias_pe, layer * 6 + j + 1)
                dve.tensor_tensor(flat[:, 8 * j:8 * j + 8, :], bank[j % 4][:, :].rearrange("p (r k) -> p r k", k=64), near,
                                  ALU.min).then_inc(bias_done, 1)

        def dve_attend(at_):
            b1 = at_["block"] == 1
            if b1:
                dve_bias(at_["layer"])
                dve.wait_ge(bias_done, 6 * (at_["layer"] + 1))
            for j, (tile, nb) in enumerate(at_["vt_jobs"]):
                m = at_["vt0"] + j
                dve.wait_ge(vt_t, m + 1)
                w = nb * P
                dve.tensor_copy(vt[:, j * w:j * w + w], bank[4 + m % 2][:, 0:w]).then_inc(vt_copy, 1)
            if not b1:
                for j in range(13):
                    m = at_["rope0"] + j
                    tile = rope_tiles()[j]
                    dve.wait_ge(rope_pe, m + 1)
                    at_least(dve, rope_dve, 2 * m - 2)
                    dve.tensor_tensor(rope_t[:, m % 2, :], bank[6 + m % 2][:, 0:S], table("sin"), ALU.mult) \
                       .then_inc(rope_dve, 1)
                    dve.wait_ge(rope_pool, m + 1)
                    dve.wait_ge(rope_dve, 2 * m + 1)
                    dve.tensor_tensor(U2[:, tile, :], U2[:, tile, :], rope_t[:, m % 2, :], ALU.add).then_inc(rope_dve, 1)
                dve.wait_ge(rope_dve, 2 * (at_["rope0"] + 13))
                dve.tensor_copy(k_swap[0:HD, :], U2[HD:P, 4, :])
                dve.tensor_copy(k_swap[HD:P, :], U2[0:HD, 4, :]).then_inc(k_swap_done, 1)
            for what, call in attend_order(at_):
                if what == "sb":
                    dve_stick(at_)
                else:
                    dve_call(call)

        def dve_out(pair, src, hi, lo):
            dve.wait_ge(pv_done, 2 * (pair + 1))
            dve.tensor_copy(hi, src).then_inc(o_step, 1)
            dve.wait_ge(o_step, pair + 1)
            dve.tensor_tensor(lo, src, hi.bitcast(F32), ALU.subtract).then_inc(o_done, 1)

        def dve_call(call):
            groups, what = call["groups"], call["what"]
            n_g = len(groups)
            per_head = n_g // 8
            if what == "swa":
                dve.wait_ge(s_small, 16 + 64 * DEPTH)
            for j in range(n_g + T_LAG + 2):
                if j < n_g:
                    g = groups[j]
                    n = g["n"]
                    sb_ = bank[call["score_banks"][(n - call["n0"]) % len(call["score_banks"])]]
                    dve.wait_ge(sc_done, n + 1)
                    if what == "near":
                        rr = 2 - 2 * g["qt"]
                        dve.scalar_tensor_tensor(sb_[:, 0:S], sb_[:, 0:S], SCALE,
                                                 bias_t[:, g["head"], rr:rr + 4, :].rearrange("p r k -> p (r k)"),
                                                 ALU.mult, ALU.add)
                        dve.tensor_scalar(sb_[:, S:512], sb_[:, S:512], SCALE, None, ALU.mult).then_inc(bias_add, 1)
                    elif what == "ctx":
                        at_least(dve, bias_add, n)
                        dve.nop().then_inc(bias_add, 1)
                    else:
                        mask = table("m_band" if what == "swa" else "m_causal")
                        dve.scalar_tensor_tensor(sb_[:, 0:384], sb_[:, 0:384], SCALE, mask, ALU.mult, ALU.add) \
                           .then_inc(bias_add, 1)
                    dve.wait_ge(bias_add, n + 1)
                    at_least(dve, p_ready, n - 3)
                    c0 = g["seg0"] % 16
                    ns = len(g["segs"])
                    for si, (qt, a, b) in enumerate(g["segs"]):
                        ins = dve.tensor_reduce(neg_max[:, c0 + si:c0 + si + 1], sb_[:, a:b], AX.X, ALU.max,
                                                negate=what != "ctx" and what != "swa")
                    if what == "ctx":
                        ins.then_inc(max_step, 1)
                        dve.wait_ge(max_step, g["max_count"])
                        dve.tensor_scalar(neg_max[:, c0:c0 + ns], neg_max[:, c0:c0 + ns], -SCALE, None, ALU.mult) \
                           .then_inc(max_done, 1)
                    elif what == "swa":
                        ins.then_inc(max_step, 1)
                        dve.wait_ge(max_step, g["max_count"])
                        h = call["layer"] * 8 + g["head"]
                        dve.tensor_scalar(neg_max[:, c0:c0 + ns], neg_max[:, c0:c0 + ns], sink[:, h:h + 1], -1.0,
                                          ALU.max, ALU.mult).then_inc(max_done, 1)
                    else:
                        ins.then_inc(max_done, 1)
                if 1 <= j <= n_g:
                    g = groups[j - 1]
                    n = g["n"]
                    c0, ns = g["seg0"] % 16, len(g["segs"])
                    dve.wait_ge(exp_done, n + 1)
                    if what == "swa":
                        dve.tensor_tensor(row_sum[:, c0:c0 + ns], row_sum[:, c0:c0 + ns], sink_e[:, c0:c0 + ns], ALU.add) \
                           .then_inc(inv_step, 1)
                        dve.wait_ge(inv_step, g["inv_count"] - 1)
                    dve.reciprocal(row_inv[:, c0:c0 + ns], row_sum[:, c0:c0 + ns]).then_inc(inv_step, 1)
                    dve.wait_ge(inv_step, g["inv_count"])
                    for si, (qt, a, b) in enumerate(g["segs"]):
                        ins = dve.tensor_scalar(probs[:, n % 4, a:b], probs[:, n % 4, a:b],
                                                row_inv[:, c0 + si:c0 + si + 1], None, ALU.mult)
                    ins.then_inc(p_ready, 1)
                jj = j - T_LAG - 2
                if jj >= 0 and jj < n_g and groups[jj]["last"] and groups[jj]["head"] % 2 == 1:
                    hp = groups[jj]["head"] // 2
                    hi, lo = out_tiles(call, hp)
                    ob = out_of(call, hp)
                    dve_out(call["pair0"] + hp, ob, hi, lo)

        def dve_stick(at_):
            for j in range(7):
                if j < 4:
                    m = at_["sb0"] + j
                    dve.wait_ge(sb_scores, m + 1)
                    if j >= 2:
                        dve.wait_ge(pv_done, 2 * (at_["sb_pair0"] + j - 1))
                    for e in range(2):
                        ins = dve.scalar_tensor_tensor(sb_z[:, j % 2, e, :], bank[2 * (j % 2) + e][:, 0:384], SCALE,
                                                       table("m_past"), ALU.mult, ALU.add)
                    ins.then_inc(sb_scaled, 1)
                if 1 <= j <= 4:
                    m = at_["sb0"] + j - 1
                    dve.wait_ge(sb_remain, m + 1)
                    for e in range(2):
                        z_ = sb_z[:, (j - 1) % 2, e, :]
                        ins = dve.tensor_tensor(z_, z_, bank[4 + e][:, 0:384], ALU.subtract)
                    ins.then_inc(sb_diff, 1)
                if 3 <= j:
                    o = j - 3
                    dve_out(at_["sb_pair0"] + o, bank[6 + o % 2][:, 0:S], O_hi[:, 4 + o, :], O_lo[:, 4 + o, :])
                if j < 4:
                    m = at_["sb0"] + j
                    dve.wait_ge(sb_log, 3 * m + 3)
                    dve.wait_ge(sb_scaled, m + 1)
                    dve.scalar_tensor_tensor(sb_e[:, j % 2, :, :], sb_z[:, j % 2, :, :], 0.0, sb_e[:, j % 2, :, :],
                                             ALU.max, ALU.add).then_inc(sb_soft, 1)

        for kind, ph in plan:
            if kind == "mod_read":
                dve.wait_ge(mod_done, 24 * ph["end"])
                for seg in range(done_segs[0], ph["end"]):
                    dve_mod(seg)
                done_segs[0] = ph["end"]
            elif kind == "gemm":
                dve_gemm(ph)
            elif kind == "norm":
                dve_norm(ph)
            elif kind == "mixers":
                dve_mixers(ph)
            elif kind == "attend":
                dve_attend(ph)
        for q in range(4):
            dve.wait_ge(final_t, q + 1)
            tb, fh = q // 2, q % 2
            dve.tensor_copy(tokens_out[:, tb, fh * 512:fh * 512 + 512], bank[q][:, :]).then_inc(final_copy, 1)

    @blk.gpsimd
    def _(pool):
        pool.memset(ones[:, :], 1.0)
        pool.memset(eps[:, :], EPS)
        pool.memset(c_pad[:, :, :].bitcast(F32), 0.0)
        pool.memset(pool_bd[:, :, :], 0.0).then_inc(memset_done, 3)
        pool.dma_start(sink[:, :], sinks_2.rearrange("l h -> (l h)").partition_broadcast(P)).then_inc(s_small, 16)

        def pool_w_load(layer):
            for g in range(4):
                lo = HD * (g % 2)
                pool.dma_start(pool_bd[lo:lo + HD, g // 2, lo:lo + HD], pool_w[layer, g]).then_inc(s_small, 16)

        def bias_load(layer):
            for b in range(2):
                for h in range(8):
                    src = bass.AP(tensor=rpb.tensor, offset=rpb[layer, h].offset + (5 - b) * 31 - 48,
                                  ap=[[1, 64], [31, 6], [1, 64]])
                    pool.dma_start(bias_t[64 * b:64 * b + 64, h, :, :], src).then_inc(s_bias, 16)

        pool.wait_ge(memset_done, 3)
        pool_w_load(0)
        bias_load(0)

        def stats_start(r):
            at_least(pool, stat_done, r)
            pool.memset(sq_sum[:, :], 0.0).then_inc(sq_step, 1)

        def stats_tile(r, k, src, width):
            pool.wait_ge(sq_step, 17 * r + 1 + 2 * k)
            pool.tensor_tensor(sq[:, 0:width], src, src, ALU.mult).then_inc(sq_step, 1)
            pool.wait_ge(sq_step, 17 * r + 2 + 2 * k)
            pool.tensor_tensor(sq_sum[:, 0:width], sq_sum[:, 0:width], sq[:, 0:width], ALU.add).then_inc(sq_step, 1)

        stats_start(0)
        for k in range(KD):
            pool.wait_ge(init_copy, n_row_tiles + k + 1)
            stats_tile(0, k, X[:, k, :], 512)

        def pool_gemm(ph):
            k, width = ph.kind, ph.width
            if k in ("glu", "conv_glu"):
                hi, lo = (G_hi, G_lo) if k == "glu" else (G2_hi, G2_lo)

                def step(i, first, last):
                    for e in range(2):
                        g = ph.g0 + 2 * i + e
                        pool.wait_ge(g_hi_done, g + 1)
                        pool.tensor_tensor(lo[:, 2 * i + e, 0:width], g32[:, e, 0:width],
                                           hi[:, 2 * i + e, 0:width].bitcast(F32), ALU.subtract).then_inc(g_lo_done, 1)
                repeat(pool, phase_steps(ph)[0], step)
            elif k == "residual" and ph.more["stats"]:
                r = ph.more["norm_next"]
                pool.wait_ge(acc_done, ph.start + 1)
                stats_start(r)

                def step(i, first, last):
                    for u in range(4):
                        f = 4 * i + u
                        pool.wait_ge(acc_free, ph.start + f + 1)
                        src = X[:, f, 0:width] if ph.more["seg"] is not None else X2[:, f, :]
                        stats_tile(r, f, src, width)
                repeat(pool, 2, step)
            elif k == "branch":
                for u in range(4):
                    for e in range(2):
                        f = 2 * u + e
                        pool.wait_ge(h_hi_done, ph.h0 + 2 * u + 2)
                        pool.tensor_tensor(H2_lo[:, f, :], merged[:, f, :], H2_hi[:, f, :].bitcast(F32),
                                           ALU.subtract).then_inc(h_lo_done, 1)

        def pool_mixers(mx):
            layer, streams = mx["layer"], mx["streams"]
            n = [mx["pool0"]]

            def step(ins):
                ins.then_inc(mix_pool, 1)
                n[0] += 1
                pool.wait_ge(mix_pool, n[0])
            pool.wait_ge(acc_free, mx["unit_end"])
            for s in range(streams):
                a, pad = s * S, 12
                step(pool.memset(pool_a[:, :, :], 0.0))
                step(pool.memset(pool_b[:, :, :], 0.0))
                step(pool.tensor_copy(pool_a[:, :, pad:pad + S], U[:, 6:8, a:a + S]))
                ic = table("inv_count").rearrange("p (j t) -> p j t", t=S)
                src, dst = pool_a, pool_b
                for g, (left, right, lo_, hi_) in enumerate(((1, 0, 1, 280), (1, 1, 2, 279), (2, 2, 4, 277), (4, 4, 8, 272))):
                    step(pool.tensor_tensor(dst[:, :, lo_:hi_], src[:, :, lo_ - left:hi_ - left],
                                           src[:, :, lo_ + right:hi_ + right], ALU.add))
                    rows_ = slice(HD * (g % 2), HD * (g % 2) + HD)
                    step(pool.tensor_tensor(pool_c[rows_, s, g // 2, :], dst[rows_, g // 2, pad:pad + S], ic[rows_, g // 2, :],
                                           ALU.mult))
                    src, dst = dst, src
                step(pool.tensor_tensor(pool_c[:, s, :, :], pool_c[:, s, :, :], U[:, 6:8, a:a + S], ALU.subtract))
                assert n[0] == mx["q_pool"][s]

        def pool_split(mx):
            w = mx["streams"] * S
            pool.wait_ge(mix_act, mx["act0"] + 4 * mx["streams"])
            at = mx["q_pool"][-1]
            src = U[:, 6:8, 0:w]
            pool.tensor_copy(H_hi[:, 2:4, 0:w], src).then_inc(mix_pool, 1)
            pool.wait_ge(mix_pool, at + 1)
            pool.tensor_tensor(H_lo[:, 2:4, 0:w], src, H_hi[:, 2:4, 0:w].bitcast(F32), ALU.subtract).then_inc(mix_pool, 1)

        def pool_norm(nm):
            kind, width = nm["kind"], nm.get("width", S)
            if kind in ("mod", "plain"):
                src, hi, lo = (T1, H_hi, H_lo) if kind == "mod" else (T2, H2_hi, H2_lo)
                for k in range(KD):
                    pool.wait_ge(h_hi_done, nm["h0"] + k + 1)
                    pool.tensor_tensor(lo[:, k, 0:width], src[:, k, 0:width], hi[:, k, 0:width].bitcast(F32),
                                       ALU.subtract).then_inc(h_lo_done, 1)
            elif kind == "renorm":
                r = nm["r"] + 1
                pool.wait_ge(final_mul, KD + 1)
                stats_start(r)
                for k in range(KD):
                    stats_tile(r, k, X2[:, k, :], S)

        for kind, ph in plan:
            if kind == "gemm":
                pool_gemm(ph)
            elif kind == "norm":
                pool_norm(ph)
            elif kind == "mixers":
                pool_mixers(ph)
            elif kind == "attend":
                if ph["block"] == 1:
                    pool_split(ph["mixed"])
                    if ph["layer"] + 1 < DEPTH:
                        pool.wait_ge(o_done, ph["calls"][-1]["pair0"] + 4)
                        pool.wait_ge(mix_pe, 4)
                        pool_w_load(ph["layer"] + 1)
                        bias_load(ph["layer"] + 1)
                else:
                    for j in range(13):
                        m = ph["rope0"] + j
                        tile = rope_tiles()[j]
                        pool.wait_ge(rope_pe, m + 1)
                        pool.tensor_tensor(U2[:, tile, :], U2[:, tile, :], table("cos"), ALU.mult).then_inc(rope_pool, 1)

    @blk.tensor
    def _(pe):
        pe.wait_ge(s_const, 16)
        pe.wait_ge(memset_done, 3)
        pe.wait_ge(s_rows, 16 * len(row_pieces))
        for tile in range(n_row_tiles):
            used = min(P, n_rows - tile * P)
            if tile >= 2:
                pe.wait_ge(init_copy, tile - 1)
            pe.transpose(bank[4 + tile % 2][:, 0:used], rows_in[0:used, tile, :], ident[0:used, 0:used]).then_inc(init_t, 1)
        pe.wait_ge(s_tok, 32)
        for f in range(KD):
            if f >= 4:
                pe.wait_ge(init_copy, n_row_tiles + f - 3)
            for tb in range(4):
                ins = pe.transpose(bank[f % 4][:, tb * P:tb * P + P], tokens_in[:, tb, f * P:f * P + P], ident)
            ins.then_inc(init_t, 1)

        pe.wait_ge(c_split, 3)

        def pe_mod_pair(ph, i, u):
            b = (ph.start + u) % 4
            t = ph.start + u + ph.stride * i
            pe.wait_ge(lo_done, t + 2)
            at_least(pe, acc_free, ph.start + ph.stride * (i - 1) + (4 if u else 2) if ph.side else t - 3)
            for k in range(KD):
                for w in (w_hi, w_lo):
                    ins = pe.matmul(mod_bank(ph, u)[:, 0:256], c_pad[:, k, :], w[:, b:b + 2, k * P:k * P + P],
                                    start=k == 0 and w is w_hi, stop=k == KD - 1 and w is w_lo)
            ins.then_inc(acc_done, 2)

        def pe_mod_turn(ph, i, mu):
            pe.wait_ge(acc_free, ph.start + ph.stride * i + mu // 2 * 2 + 2)
            pe.matmul(bank[7][:, bass.ds(2 * (ph.mod0 + mu) + 8 * i, 2)], mod_rows[:, mu // 2, mu % 2 * P:mu % 2 * P + P],
                      table("pick"), start=True, stop=True).then_inc(mod_done, 1)

        def pe_gemm(ph):
            xh, xl = moving_of(ph)
            if ph.kind == "branch":
                xh, xl = O_hi, O_lo
            width, kk = ph.width, ph.k
            m = ph.more.get("moving", "h")
            if ph.kind == "branch":
                pe.wait_ge(o_done, ph.more["pairs"])
            elif m == "y":
                pe.wait_ge(o_done, ph.more["pairs"])
                pe.wait_ge(mix_dve, ph.more["mix_end"])
                pe.wait_ge(mix_pool, ph.more["pool_end"])
            if ph.kind == "mod" or ph.side:
                at_least(pe, mod_ready, ph.more["reads"])

            def step(i, first, last, n_units=ph.stride):
                for u in range(n_units):
                    t = ph.start + u + ph.stride * i
                    b = (ph.start + u) % 4
                    mu = mod_unit(ph, u)
                    if mu is not None:
                        if mu % 2 == 0:
                            pe_mod_pair(ph, i, u)
                        if mu == 3 and not ph.side:
                            for j in range(4):
                                pe_mod_turn(ph, i, j)
                        continue
                    v = own_unit(ph, u)
                    b_w, b = b, (ph.start + v) % 4
                    joint = first and not ph.side and ph.kind != "branch" and moving_wait(ph, 0) and ph.more.get("moving", "h") == "h"
                    if joint and u == 0:
                        pe.wait_ge(lo_done, t + 2)
                        at_least(pe, acc_free, ph.start)
                        for k in range(kk):
                            pe.wait_ge(*moving_wait(ph, k))
                            for v in range(2):
                                wh, wl = (w[:, (b + v) % 4, k * P:k * P + P] for w in (w_hi, w_lo))
                                o = bank[(b + v) % 4][:, 0:width]
                                pe.matmul(o, wh, xh[:, k, 0:width], start=k == 0, stop=False)
                                pe.matmul(o, wl, xh[:, k, 0:width], start=False, stop=False)
                                ins = pe.matmul(o, wh, xl[:, k, 0:width], start=False, stop=k == kk - 1)
                                if k == kk - 1:
                                    ins.then_inc(acc_done, 1)
                        continue
                    if joint and u == 1:
                        continue
                    pe.wait_ge(lo_done, t + 1)
                    if first or ph.more.get("pair"):
                        value = ph.start + ph.stride * i - (2 if v == 0 else 0)
                    else:
                        value = t - 3
                    at_least(pe, acc_free, value)
                    if ph.kind == "branch":
                        for half in range(2):
                            for k in range(kk):
                                wh = w_hi[:, b, k * 256 + half * P:k * 256 + half * P + P]
                                wl = w_lo[:, b, k * 256 + half * P:k * 256 + half * P + P]
                                o = bank[b][:, half * S:half * S + S]
                                pe.matmul(o, wh, xh[:, 4 * i + k, :], start=k == 0, stop=False)
                                pe.matmul(o, wl, xh[:, 4 * i + k, :], start=False, stop=False)
                                ins = pe.matmul(o, wh, xl[:, 4 * i + k, :], start=False, stop=k == kk - 1)
                    else:
                        for k in range(kk):
                            if first and v == 0 and moving_wait(ph, k):
                                pe.wait_ge(*moving_wait(ph, k))
                            wh, wl = w_hi[:, b_w, k * P:k * P + P], w_lo[:, b_w, k * P:k * P + P]
                            o = bank[b][:, 0:width]
                            pe.matmul(o, wh, xh[:, k, 0:width], start=k == 0, stop=False)
                            pe.matmul(o, wl, xh[:, k, 0:width], start=False, stop=False)
                            ins = pe.matmul(o, wh, xl[:, k, 0:width], start=False, stop=k == kk - 1)
                    ins.then_inc(acc_done, 1)
                    if ph.side and v in (0, 2):
                        for j in range(2):
                            pe_mod_turn(ph, i, v + j)
            n4, left = phase_steps(ph)
            if ph.kind == "branch":
                for i in range(n4):
                    step(i, i == 0, i == n4 - 1)
            else:
                repeat(pe, n4, step)
            if left:
                step(n4, False, True, left)

        def pe_norm(nm):
            r, width = nm["r"], nm.get("width", S)
            pe.wait_ge(sq_step, 17 * (r + 1))
            at_least(pe, rms_done, r)
            pe.matmul(STAT[:, 0:width], ones[:, :], sq_sum[:, 0:width], start=True, stop=True).then_inc(stat_done, 1)
            if nm["kind"] == "final":
                pe.wait_ge(acc_free, total)
                for q in range(4):
                    tb, fh = q // 2, q % 2
                    pe.wait_ge(final_mul, KD + 1 + KD)
                    for f4 in range(4):
                        ins = pe.transpose(bank[q][:, f4 * P:f4 * P + P], T2[:, fh * 4 + f4, tb * P:tb * P + P], ident)
                    ins.then_inc(final_t, 1)

        def pe_mixers(mx):
            pe.wait_ge(s_small, 16 + 64 * (mx["layer"] + 1))
            for s in range(mx["streams"]):
                pe.wait_ge(mix_pool, mx["q_pool"][s])
                for j in range(2):
                    pe.matmul(bank[2 * s + j][:, 0:S], pool_bd[:, j, :], pool_c[:, s, j, :], start=True, stop=True) \
                      .then_inc(mix_pe, 1)

        def pe_attend(at_):
            b1 = at_["block"] == 1
            if b1:
                pe.wait_ge(acc_free, at_["unit_end"])
                layer = at_["layer"]
                pe.wait_ge(s_bias, 16 * 16 * (layer + 1))
                flat = bias_t[:, :, :, :].rearrange("p h r k -> p (h r k)")
                for j in range(6):
                    if j >= 4:
                        pe.wait_ge(bias_done, layer * 6 + j - 3)
                    pe.matmul(bank[j % 4][:, :], table("turn"), flat[:, 512 * j:512 * j + 512], start=True, stop=True) \
                      .then_inc(bias_pe, 1)
                pe.wait_ge(bias_done, layer * 6 + 6)
            else:
                pe.wait_ge(acc_free, at_["unit_end"])
            src = U if b1 else U2
            v_tiles = [16, 17, 18, 19] if b1 else [5] + [14, 15, 16, 17] + [26, 27, 28, 29]
            for j, (tile, nb) in enumerate(at_["vt_jobs"]):
                m = at_["vt0"] + j
                at_least(pe, vt_copy, m - 1)
                for tb in range(nb):
                    ins = pe.transpose(bank[4 + m % 2][:, tb * P:tb * P + P],
                                       src[:, v_tiles[j], tb * P:tb * P + P], ident)
                ins.then_inc(vt_t, 1)
            pe.wait_ge(vt_copy, at_["vt0"] + len(at_["vt_jobs"]))
            if not b1:
                for j in range(13):
                    m = at_["rope0"] + j
                    tile = rope_tiles()[j]
                    at_least(pe, rope_dve, 2 * (m - 1))
                    pe.matmul(bank[6 + m % 2][:, 0:S], rot, U2[:, tile, :], start=True, stop=True).then_inc(rope_pe, 1)
                pe.wait_ge(rope_dve, 2 * (at_["rope0"] + 13))
            for what, call in attend_order(at_):
                if what == "sb":
                    pe_stick(at_)
                else:
                    pe_call(at_, call)
            if b1:
                pe.wait_ge(exp_done, at_["calls"][-1]["groups"][-1]["n"] + 1)
                pe_mixers(at_["mixed"])

        def pv(e, cols_banks, v_cols, pt, ob, q_lists):
            for idx, (vc, pcols, qcols) in enumerate(q_lists):
                ins = pe.matmul(ob[HD * e:HD * e + HD, qcols[0]:qcols[1]], vt[:, vc:vc + HD], pt[:, pcols[0]:pcols[1]],
                                start=idx == 0, stop=idx == len(q_lists) - 1)
            return ins

        def pe_call(at_, call):
            groups, what = call["groups"], call["what"]
            n_g = len(groups)
            per_head = n_g // 8
            src = U if at_["block"] == 1 else U2
            nb = len(call["score_banks"])
            npt = len(call["pt_banks"])
            at_least(pe, o_done, call["pair0"])
            if what == "swa":
                pe.wait_ge(k_swap_done, call["layer"] + 1)
            at_least(pe, exp_done, call["n0"])
            at_least(pe, pt_copy, call["n0"])
            for j in range(n_g + T_LAG + 1):
                if j < n_g:
                    g = groups[j]
                    n, h = g["n"], g["head"]
                    e = h % 2
                    rows_ = slice(HD * e, HD * e + HD)
                    if n - call["n0"] >= nb:
                        pe.wait_ge(exp_done, n - nb + 1)
                    sb_ = bank[call["score_banks"][(n - call["n0"]) % nb]]
                    for si, (qt, a, b) in enumerate(g["segs"]):
                        if what == "near":
                            q = U[rows_, 8 + h // 2, qt * P:qt * P + P]
                            kk = U[rows_, 12 + h // 2, 0:512]
                        elif what == "ctx":
                            q = U[rows_, 8 + h // 2, S + qt * P:S + qt * P + P]
                            kk = U[rows_, 12 + h // 2, S:512]
                        elif what == "swa":
                            q = U2[rows_, h // 2, qt * P:qt * P + P]
                            kk = U2[rows_, 4, 0:b - a] if h // 4 == e else k_swap[rows_, 0:b - a]
                        else:
                            q = U2[rows_, 18 + h // 2, qt * P:qt * P + P]
                            kk = U2[rows_, 22 + h // 2, 0:b - a]
                        ins = pe.matmul(sb_[:, a:b], q, kk, start=True, stop=True)
                    ins.then_inc(sc_done, 1)
                if 0 <= j - T_LAG < n_g:
                    g = groups[j - T_LAG]
                    n = g["n"]
                    pe.wait_ge(p_ready, n + 1)
                    at_least(pe, pt_copy, n - npt + 1)
                    pb = bank[call["pt_banks"][(n - call["n0"]) % npt]]
                    for bi, (col, kb) in enumerate(g["blocks"]):
                        pc = col + (P * kb if what == "near" else 0)
                        ins = pe.transpose(pb[:, bi * P:bi * P + P], probs[:, n % 4, pc:pc + P], ident)
                    ins.then_inc(pt_done, 1)
                jj = j - T_LAG - 1
                if 0 <= jj < n_g and groups[jj]["last"]:
                    g = groups[jj]
                    h, n = g["head"], g["n"]
                    e, hp = h % 2, h // 2
                    pe.wait_ge(pt_copy, n + 1)
                    if e == 0:
                        at_least(pe, o_done, call["pair0"] + hp - len(call["out_banks"]) + 1)
                    ob = out_of(call, hp)
                    if what == "near":
                        ql = [(hp * 512 + kb * P + HD * e, (kb * S, kb * S + S), (0, S)) for kb in range(4)]
                    elif what == "ctx":
                        ql = [(hp * 512 + (2 + kb) * P + HD * e, (kb * S, kb * S + S), (0, S)) for kb in range(2)]
                    else:
                        if what == "swa":
                            v0 = [0 + HD * (h // 4), P + HD * (h // 4)]
                        else:
                            v0 = [(5 + hp) * S + HD * e, (5 + hp) * S + P + HD * e]
                        ql = [(v0[0], (0, S), (0, S)), (v0[1], (S, 384), (P, S))]
                    pv(e, None, None, probs_t[:, e, :], ob, ql).then_inc(pv_done, 1)

        def pe_stick(at_):
            at_least(pe, o_done, at_["sb_pair0"])
            for j in range(6):
                if j < 4:
                    m = at_["sb0"] + j
                    if j >= 2:
                        pe.wait_ge(sb_scaled, m - 1)
                    for e in range(2):
                        rows_ = slice(HD * e, HD * e + HD)
                        q, kk = U2[rows_, 6 + j, :], U2[rows_, 10 + j, :]
                        o = bank[2 * (j % 2) + e]
                        pe.matmul(o[:, 0:S], kk[:, 0:P], q, start=True, stop=True)
                        ins = pe.matmul(o[:, S:384], kk[:, P:S], q[:, P:S], start=True, stop=True)
                    ins.then_inc(sb_scores, 1)
                if j >= 2:
                    o_ = j - 2
                    pe.wait_ge(sb_weight, at_["sb0"] + o_ + 1)
                    at_least(pe, o_done, at_["sb_pair0"] + o_ - 1)
                    for e in range(2):
                        ql = [((1 + o_) * S + HD * e, (0, S), (0, S)), ((1 + o_) * S + P + HD * e, (S, 384), (P, S))]
                        pv(e, None, None, sb_z[:, o_ % 2, e, :], bank[6 + o_ % 2][:, 0:S], ql).then_inc(pv_done, 1)
                if 1 <= j <= 4:
                    m = at_["sb0"] + j - 1
                    pe.wait_ge(sb_soft, m + 1)
                    at_least(pe, sb_diff, m)
                    for e in range(2):
                        x_ = sb_e[:, (j - 1) % 2, e, :]
                        pe.matmul(bank[4 + e][:, 0:S], tri, x_[:, 0:S], start=True, stop=False)
                        pe.matmul(bank[4 + e][:, P:S], ones[:, :], x_[:, S:384], start=False, stop=True)
                        ins = pe.matmul(bank[4 + e][:, S:384], tri, x_[:, S:384], start=True, stop=True)
                    ins.then_inc(sb_remain, 1)

        for kind, ph in plan:
            if kind == "gemm":
                pe_gemm(ph)
            elif kind == "norm":
                pe_norm(ph)
            elif kind == "attend":
                pe_attend(ph)

    stack.close()


INPUTS = ["x", "c", "ctx", "c_ctx", "w_mod", "b_mod", "norm_g", "ffn_w_in", "ffn_w_out", "w_in", "conv_w", "pool_w",
          "pool_scale", "rpb", "w_out", "final_g", "norm_mix_2", "w_in_2", "b_gate_2", "sinks_2", "w_branch_2",
          "w_out_2", "norm_ffn_2", "w_up_2", "conv_w_2", "conv_b_2", "w_down_2", "norm_final_2"]


def kernel(**inputs):
    import numpy as _np
    import concourse.bacc as _bacc
    from concourse.bass_utils import run_bass_kernel_spmd as _run

    nc = _bacc.Bacc("TRN2", target_bir_lowering=False, num_devices=1)
    arrays, aps = {}, {}
    for name in INPUTS:
        arrays[name] = _np.ascontiguousarray(inputs[name])
    arrays["consts"] = CONSTS
    for name, a in arrays.items():
        aps[name] = nc.dram_tensor(name, a.shape, mybir.dt.from_np(a.dtype), kind="ExternalInput").ap()
    aps["out"] = nc.dram_tensor("out", (1, S, D), F32, kind="ExternalOutput").ap()
    build_program(nc, **aps)
    r = _run(nc, [arrays], core_ids=[0])
    return r.results[0]["out"]
```

```python
import concourse.bass as bass
from concourse import mybir
from contextlib import ExitStack
import numpy as np

F32 = mybir.dt.float32
F32R = mybir.dt.float32r
ALU = mybir.AluOpType
ACT = mybir.ActivationFunctionType
AX = mybir.AxisListType
P = 128
D = 1024
KD = D // P
S = 256
DEPTH = 2
DFF = 2816
FT = DFF // P
THIRDS = (8, 8, 6)
EPS = 1e-6
NEG = -1e30
HD = 64
SCALE = HD ** -0.5
N_IN = 20
N_QKV = 30
N_GATE = 24
SLOTS = 4
AHEAD = 3
ROLL = 15 * 31


def constant_table():
    parts = {}
    row = np.arange(P)
    parts["ident"] = np.eye(P)
    pick = np.zeros((P, 2))
    pick[0:2, 0] = pick[2:4, 1] = 1.0
    parts["pick"] = pick
    rot = np.zeros((P, P))
    for m in range(P):
        if m % HD < HD // 2:
            rot[m + HD // 2, m] = -1.0
        else:
            rot[m - HD // 2, m] = 1.0
    parts["rot"] = rot
    parts["turn"] = (row[:, None] // 64 * 64 + 63 - row[:, None] % 64 == row[None, :]).astype(float)
    parts["tri"] = (row[:, None] >= row[None, :]).astype(float)
    inv = (np.float32(10000.0) ** (-np.arange(0, HD, 2, dtype=np.float32) / np.float32(HD))).astype(np.float32)
    ang = np.arange(S, dtype=np.float32)[None, :] * inv[row % (HD // 2)][:, None]
    parts["cos"] = np.cos(ang.astype(np.float32))
    parts["sin"] = np.sin(ang.astype(np.float32))
    causal = np.where(row[None, :] <= row[:, None], 0.0, NEG)
    parts["m_causal"] = np.concatenate([causal, np.zeros((P, P)), causal], 1)
    parts["m_band"] = np.concatenate([causal, np.where(row[None, :] > row[:, None], 0.0, NEG), causal], 1)
    past = np.where(row[:, None] < row[None, :], 0.0, NEG)
    parts["m_past"] = np.concatenate([past, np.zeros((P, P)), past], 1)
    qcol, kcol = row % 64, np.arange(64)
    start = np.clip(qcol - 8, 0, 48)[:, None]
    ok = (kcol[None, :] >= start) & (kcol[None, :] < start + 16)
    parts["m_near"] = np.where(ok, 3.0e38, NEG)
    t = np.arange(S)
    cnt = np.zeros((P, 2, S))
    for g, w in enumerate((2, 4, 8, 16)):
        lo, hi = np.clip(t - w // 2, 0, S), np.clip(t + w - w // 2, 0, S)
        cnt[HD * (g % 2):HD * (g % 2) + HD, g // 2, :] = 1.0 / (hi - lo).astype(np.float32)
    parts["inv_count"] = cnt.reshape(P, 2 * S)
    at, cols = 0, {}
    for name, a in parts.items():
        cols[name] = (at, at + a.shape[1])
        at += a.shape[1]
    return np.concatenate([a.astype(np.float32) for a in parts.values()], 1), cols


CONSTS, CONST_COLS = constant_table()
FIRST_COLS = CONST_COLS["pick"][1]


class Phase:

    def __init__(self, kind, n, k, width, source, start, **more):
        self.kind, self.n, self.k, self.width, self.source, self.start = kind, n, k, width, source, start
        self.more = more
        self.side = more.get("side", False)
        self.stride = 8 if self.side else 4


def build_program(nc, x, c, ctx, c_ctx, w_mod, b_mod, norm_g, ffn_w_in, ffn_w_out, w_in, conv_w, pool_w,
                  pool_scale, rpb, w_out, final_g, norm_mix_2, w_in_2, b_gate_2, sinks_2, w_branch_2,
                  w_out_2, norm_ffn_2, w_up_2, conv_w_2, conv_b_2, w_down_2, norm_final_2, consts, out):
    K = 1024
    base = 17 * K
    region = {}
    at = base
    for name, size in (("x", 16 * K), ("h", 32 * K), ("g", 40 * K), ("raw", 16 * K), ("hi", 16 * K), ("lo", 16 * K),
                       ("mod", 16 * K), ("bias", 12 * K), ("vt", 9 * K + 256), ("scr", 16 * K)):
        region[name] = at
        at += size
    top = [at]

    def fixed(name, shape, dt, offset):
        return nc.alloc_sbuf_tensor_at(name, shape, dt, offset=offset)

    def small(name, shape, dt=F32):
        t = fixed(name, shape, dt, top[0])
        top[0] += (int(np.prod(shape[1:])) * 4 + 31) // 32 * 32
        return t

    X = fixed("X", [P, KD, 512], F32, region["x"])
    H_hi = fixed("H_hi", [P, KD, 512], F32R, region["h"])
    H_lo = fixed("H_lo", [P, KD, 512], F32R, region["h"] + 16 * K)
    G_hi = fixed("G_hi", [P, 8, 512], F32R, region["g"])
    G_lo = fixed("G_lo", [P, 8, 512], F32R, region["g"] + 16 * K)
    U = fixed("U", [P, N_IN, 512], F32, region["g"])
    T1 = fixed("T1", [P, KD, 512], F32, region["g"])
    pool_a = fixed("pool_a", [P, 2, 280], F32, region["mod"] + 6 * K)
    pool_b = fixed("pool_b", [P, 2, 280], F32, region["mod"] + 6 * K + 2240)
    pool_c = fixed("pool_c", [P, 2, 2, S], F32, region["mod"] + 6 * K + 4480)
    tokens_in = fixed("tokens_in", [P, 4, D], F32, region["g"])
    rows_in = fixed("rows_in", [P, 6, P], F32, region["g"] + 16 * K)
    bias_t = fixed("bias_t", [P, 8, 6, 64], F32, region["bias"])
    c_pad = fixed("c_pad", [P, KD, P], F32R, region["mod"])
    mod_rows = fixed("mod_rows", [P, 2, 256], F32, region["mod"] + 4 * K)
    X2 = fixed("X2", [P, KD, S], F32, region["x"] + 24 * K)
    gates = fixed("gates", [P, N_GATE, S], F32, region["x"])
    H2_hi = fixed("H2_hi", [P, KD, S], F32R, region["x"] + 32 * K)
    H2_lo = fixed("H2_lo", [P, KD, S], F32R, region["x"] + 40 * K)
    U2 = fixed("U2", [P, N_QKV, S], F32, region["g"])
    merged = fixed("merged", [P, KD, S], F32, region["g"] + 30 * K)
    T2 = fixed("T2", [P, KD, S], F32, region["g"])
    G2_hi = fixed("G2_hi", [P, 8, S], F32R, region["g"])
    G2_lo = fixed("G2_lo", [P, 8, S], F32R, region["g"] + 8 * K)
    O_hi = fixed("O_hi", [P, 12, S], F32R, region["mod"])
    O_lo = fixed("O_lo", [P, 12, S], F32R, region["mod"] + 12 * K)
    tokens_out = fixed("tokens_out", [P, 2, D], F32, region["g"] + 16 * K)
    raw = fixed("raw", [P, SLOTS, 1024], F32, region["raw"])
    w_hi = fixed("w_hi", [P, SLOTS, 1024], F32R, region["hi"])
    w_lo = fixed("w_lo", [P, SLOTS, 1024], F32R, region["lo"])
    vt = fixed("vt", [P, 9 * S], F32, region["vt"])
    probs = fixed("probs", [P, 4, 512], F32, region["scr"])
    probs_t = fixed("probs_t", [P, 2, 1024], F32, region["scr"] + 8 * K)
    sil = fixed("sil", [P, 2, 512], F32, region["scr"])
    g32 = fixed("g32", [P, 2, 512], F32, region["scr"] + 4 * K)
    sq = fixed("sq", [P, 2, 512], F32, region["scr"] + 8 * K)
    sq_sum = fixed("sq_sum", [P, 512], F32, region["scr"] + 12 * K)
    rstd_diag = fixed("rstd_diag", [P, 4, P], F32, region["scr"] + 14 * K)
    sb_z = fixed("sb_z", [P, 4, 2, 384], F32, region["scr"])
    sb_e = [fixed(f"sb_e{j}", [P, 2, 384], F32, region["scr"] + 12 * K if j == 3 else region["g"] + (30 + 3 * j) * K)
            for j in range(4)]
    k_swap = fixed("k_swap", [P, S], F32, region["bias"] + 8 * K)
    rope_t = fixed("rope_t", [P, 2, S], F32, region["bias"] + 9 * K)

    const = small("const", [P, CONSTS.shape[1]])
    ones = small("ones", [P, P])
    eps = small("eps", [P, 1])
    rstd_tok = small("rstd_tok", [P, 4])
    warm = small("warm", [P, 5 + 8 * DEPTH])
    silu_c = small("silu_c", [P, KD, 2])
    modv = small("modv", [P, 6, 3, KD, 2])
    neg_max = small("neg_max", [P, 16])
    row_sum = small("row_sum", [P, 16])
    row_inv = small("row_inv", [P, 16])
    sink = small("sink", [P, DEPTH * 8])
    sink_e = small("sink_e", [P, 16])
    pool_bd = small("pool_bd", [P, 2, P])
    vec_rows, vec_at = [], {}

    def rows(name, ap):
        vec_at[name] = sum(a.shape[0] for a in vec_rows)
        vec_rows.append(ap)

    rows("c", c.rearrange("b (n p) -> (b n) p", p=P))
    rows("c_ctx", c_ctx.rearrange("(n p) -> n p", p=P))
    rows("b_mod", b_mod.rearrange("l (n p) -> (l n) p", p=P))
    rows("norm_g", norm_g.rearrange("l i (n p) -> (l i n) p", p=P))
    rows("final_g", final_g.rearrange("(n p) -> n p", p=P))
    rows("conv_w", conv_w.rearrange("l w (n p) -> (l w n) p", p=P))
    rows("pool_scale", pool_scale.rearrange("l (n p) -> (l n) p", p=P))
    rows("norm_mix", norm_mix_2.rearrange("l (n p) -> (l n) p", p=P))
    rows("b_gate", b_gate_2.rearrange("l (n p) -> (l n) p", p=P))
    rows("norm_ffn", norm_ffn_2.rearrange("l (n p) -> (l n) p", p=P))
    rows("conv_w_2", conv_w_2.rearrange("l w (n p) -> (l w n) p", p=P))
    rows("conv_b_2", conv_b_2.rearrange("l (n p) -> (l n) p", p=P))
    rows("norm_final", norm_final_2.rearrange("(n p) -> n p", p=P))
    n_rows = sum(a.shape[0] for a in vec_rows)
    n_row_tiles = (n_rows + P - 1) // P
    assert n_row_tiles <= 6, n_rows
    vecs = small("vecs", [P, n_row_tiles * P])
    assert top[0] <= nc.sbuf_usable_end, (top[0], nc.sbuf_usable_end)

    row_pieces = []
    r = 0
    for ap in vec_rows:
        done = 0
        while done < ap.shape[0]:
            n = min(ap.shape[0] - done, P - r % P)
            row_pieces.append((r % P, r // P, n, ap[done:done + n, :]))
            done += n
            r += n

    first_pieces = sum(1 for piece in row_pieces if piece[1] == 0)

    def vec(name, index, n=1):
        i = vec_at[name] + index
        return vecs[:, bass.ds(i, n)] if not isinstance(i, int) else vecs[:, i:i + n]

    def table(name):
        a, b = CONST_COLS[name]
        return const[:, a:b]

    ident, rot, tri = table("ident"), table("rot"), table("tri")

    bank = [nc.alloc_psum_tensor(f"bank{b}", [P, 512], F32) for b in range(8)]
    STAT = bank[4]

    def sem(name):
        return nc.alloc_semaphore(name)

    raw_in = [sem(f"raw_in{slot}") for slot in range(SLOTS)]
    s_ident = sem("s_ident")
    s_tables = sem("s_tables")
    s_rows_first = sem("s_rows_first")
    s_rows = sem("s_rows")
    s_tok = sem("s_tok")
    s_bias = sem("s_bias")
    s_small = sem("s_small")
    hi_done = sem("hi_done")
    lo_done = sem("lo_done")
    acc_done = sem("acc_done")
    acc_free = sem("acc_free")
    mod_done = sem("mod_done")
    mod_ready = sem("mod_ready")
    mod_step = sem("mod_step")
    silu_done = sem("silu_done")
    g_hi_done = sem("g_hi_done")
    g_lo_done = sem("g_lo_done")
    conv1_done = sem("conv1_done")
    g_mul_done = sem("g_mul_done")
    conv0_done = sem("conv0_done")
    sq_done = sem("sq_done")
    sq_added = sem("sq_added")
    stat_done = sem("stat_done")
    rms_done = sem("rms_done")
    rstd_done = sem("rstd_done")
    diag_done = sem("diag_done")
    rstd_spread = sem("rstd_spread")
    n_mul = sem("n_mul")
    n_aff = sem("n_aff")
    h_hi_done = sem("h_hi_done")
    h_lo_done = sem("h_lo_done")
    memset_done = sem("memset_done")
    init_t = sem("init_t")
    init_copy = sem("init_copy")
    silu_c_done = sem("silu_c_done")
    bias_done = sem("bias_done")
    bias_pe = sem("bias_pe")
    mix_pe = sem("mix_pe")
    mix_act = sem("mix_act")
    mix_dve = sem("mix_dve")
    vt_t = sem("vt_t")
    vt_copy = sem("vt_copy")
    sc_done = sem("sc_done")
    bias_add = sem("bias_add")
    max_step = sem("max_step")
    max_done = sem("max_done")
    exp_done = sem("exp_done")
    inv_step = sem("inv_step")
    p_ready = sem("p_ready")
    pt_done = sem("pt_done")
    pt_copy = sem("pt_copy")
    pv_done = sem("pv_done")
    o_step = sem("o_step")
    o_done = sem("o_done")
    sb_scores = sem("sb_scores")
    sb_remain = sem("sb_remain")
    sb_scaled = sem("sb_scaled")
    sb_soft = sem("sb_soft")
    sb_diff = sem("sb_diff")
    sb_log = sem("sb_log")
    sb_weight = sem("sb_weight")
    c_split = sem("c_split")
    mix_pool = sem("mix_pool")
    mix_split = sem("mix_split")
    rope_pe = sem("rope_pe")
    rope_dve = sem("rope_dve")
    rope_pool = sem("rope_pool")
    gate_done = sem("gate_done")
    k_swap_done = sem("k_swap_done")
    merge_step = sem("merge_step")
    final_mul = sem("final_mul")
    final_t = sem("final_t")
    final_copy = sem("final_copy")
    s_store = sem("s_store")

    plan = []
    units = [0]
    hidden = [0]
    mods = [0]
    splits = [0]
    GLU_TILES = 2 * DEPTH * FT

    def gemm(kind, n, k, width, source, **more):
        ph = Phase(kind, n, k, width, source, units[0], **more)
        ph.g0 = hidden[0]
        ph.gm0 = hidden[0] - GLU_TILES
        ph.h0 = splits[0] - KD
        if kind == "branch":
            ph.merge0 = 8 * ph.more["layer"]
            ph.h0 = splits[0]
            splits[0] += KD
        if kind in ("glu", "conv_glu"):
            hidden[0] += (n // 2) // (2 if ph.side else 1)
        if kind == "mod" or ph.side:
            ph.mod0 = mods[0]
            ph.mod_layer = mods[0] // 72
            mods[0] += n // (2 if ph.side else 1)
        units[0] += n
        plan.append(("gemm", ph))
        return ph

    n_norm = [0]
    affines = [0]

    def norm(kind, **more):
        nm = dict(kind=kind, r=n_norm[0], h0=splits[0], a0=affines[0], **more)
        if kind in ("mod", "plain"):
            splits[0] += KD
            affines[0] += KD
        plan.append(("norm", nm))
        n_norm[0] += 1

    def kpc(w2d):
        return w2d.rearrange("(k p) c -> p k c", p=P)

    def pair_source(w, third):
        view = kpc(w)

        def source(i, v):
            return view[:, :, bass.ds(v // 2 * DFF + third * 1024 + i * 256 + v % 2 * P, P)]
        return source

    def plain_source(w, col0=0, k0=0, k=KD):
        view = kpc(w)

        def source(i, v):
            return view[:, k0:k0 + k, bass.ds(col0 + i * 512 + v * P, P)]
        return source

    def modulation(n, **more):
        gemm("mod", n, KD, None, None, **more)

    def ffn(width, w1, w2, seg, stats, conv_layer=None, side=(), after=0):
        for third, tiles in enumerate(THIRDS):
            with_mod = third in side
            gemm("glu" if conv_layer is None else "conv_glu", (4 if with_mod else 2) * tiles, KD, width,
                 pair_source(w1, third), pair=True, layer=conv_layer, third=third, side=with_mod)
            if side and third == max(side):
                if after:
                    modulation(after)
                plan.append(("mod_read", dict(end=mods[0] // 24)))
            gemm("residual", KD, tiles, width, plain_source(w2, 0, third * 8, tiles), seg=seg,
                 stats=stats and third == 2, moving="g", norm_next=n_norm[0], hidden_end=hidden[0])

    for layer in range(DEPTH):
        last = layer == DEPTH - 1
        if not last:
            modulation(4)
            plan.append(("tokens", None))
            modulation(16, squares=True)
            modulation(4)
            plan.append(("mod_read", dict(end=1)))
        norm("mod", width=512, seg=layer * 3)
        ffn(512, ffn_w_in[layer, 0], ffn_w_out[layer, 0], layer * 3, True, side=(0,) if last else (0, 1, 2),
            after=8 if last else 4)
        if not last:
            plan.append(("tables", None))
        norm("mod", width=512, seg=layer * 3 + 1)
        if last:
            gemm("store", 12, KD, S, plain_source(w_in[layer]), moving="h", dst="U", f0=0)
            gemm("store", 8, KD, 512, plain_source(w_in[layer], 1536), moving="h", dst="U", f0=12)
        else:
            gemm("store", N_IN, KD, 512, plain_source(w_in[layer]), moving="h", dst="U", f0=0)
        plan.append(("mixers", dict(layer=layer, streams=1 if last else 2)))
        plan.append(("attend", dict(block=1, layer=layer, streams=1 if last else 2)))
        width = S if last else 512
        gemm("residual", KD, KD, width, plain_source(w_out[layer]), seg=layer * 3 + 1, stats=True, moving="y", mix_layer=layer,
             norm_next=n_norm[0])
        norm("mod", width=width, seg=layer * 3 + 2)
        ffn(width, ffn_w_in[layer, 1], ffn_w_out[layer, 1], layer * 3 + 2, True, side=() if last else (0, 1, 2),
            after=0 if last else 4)
    norm("renorm", gain=("final_g", 0))
    for layer in range(DEPTH):
        norm("plain", gain=("norm_mix", layer * KD))
        gemm("store", N_QKV, KD, S, plain_source(w_in_2[layer]), moving="h", dst="U2", f0=0)
        gates_phase = gemm("gate", N_GATE, KD, S, plain_source(w_in_2[layer], N_QKV * P), moving="h", layer=layer)
        plan.append(("attend", dict(block=2, layer=layer, streams=1, gates=gates_phase)))
        br = w_branch_2[layer]

        def branch_source(i, v, br=br):
            return br[i].rearrange("(k p) c -> p k c", p=P)[:, :, 256 * v:256 * v + 256]
        gemm("branch", 12, 4, S, branch_source, layer=layer)
        gemm("residual", KD, KD, S, plain_source(w_out_2[layer]), seg=None, stats=True, moving="merged",
             norm_next=n_norm[0])
        norm("plain", gain=("norm_ffn", layer * KD))
        ffn(S, w_up_2[layer], w_down_2[layer], None, True, conv_layer=layer)
    norm("final", gain=("norm_final", 0))
    total = units[0]
    assert mods[0] == 144

    counts = dict(group=0, seg=0, pair=0, vt=0, sb=0, rope=0)
    for kind, ph in plan:
        if kind != "attend":
            continue
        ph["vt0"] = counts["vt"]
        ph["calls"] = []
        b1 = ph["block"] == 1
        if b1:
            ph["vt_jobs"] = [(tile, 4) for tile in range(4)]
            todo = (["ctx"] if ph["streams"] == 2 else []) + ["near"]
        else:
            ph["vt_jobs"] = [(tile, 2) for tile in range(9)]
            todo = ["swa", "moba"]
        counts["vt"] += len(ph["vt_jobs"])
        ph["rope0"] = counts["rope"]
        if not b1:
            counts["rope"] += 13
        if not b1:
            ph["sb0"] = counts["sb"]
            counts["sb"] += 4
            ph["sb_pair0"] = counts["pair"]
            counts["pair"] += 4
        for what in todo:
            groups = []
            for head in range(8):
                if what == "near":
                    for qt in range(2):
                        groups.append(dict(head=head, segs=[(qt, 0, 512)], blocks=[(0, kb) for kb in range(4)],
                                           last=qt == 1, qt=qt))
                elif what == "ctx":
                    groups.append(dict(head=head, segs=[(0, 0, 256), (1, 256, 512)],
                                       blocks=[(256 * qt + 128 * kb, kb) for kb in range(2) for qt in range(2)],
                                       last=True, qt=None))
                else:
                    groups.append(dict(head=head, segs=[(0, 0, 128), (1, 128, 384)],
                                       blocks=[(0, 0), (128, 0), (256, 1)], last=True, qt=None))
            for g in groups:
                g["n"] = counts["group"]
                counts["group"] += 1
                g["seg0"] = counts["seg"]
                counts["seg"] += len(g["segs"])
            call = dict(what=what, groups=groups, pair0=counts["pair"], layer=ph["layer"],
                        n0=groups[0]["n"])
            call.update(score_banks=[0, 1, 2, 3], pt_banks=[4, 5], out_banks=[6, 7] if b1 else [6])
            counts["pair"] += 4
            ph["calls"].append(call)

    unit_at = mix_d = mix_a = mix_p = 0
    max_count = inv_count = 0
    mix_end = pairs_end = mix_q = mod_reads = 0
    for kind, ph in plan:
        if kind == "mod_read":
            mod_reads = ph["end"]
        elif kind == "gemm":
            unit_at = ph.start + ph.n
            ph.more["reads"] = mod_reads
            ph.more["pairs"], ph.more["mix_end"] = pairs_end, mix_end
        elif kind == "mixers":
            n_s = ph["streams"]
            ph.update(dve0=mix_d, act0=mix_a, pe0=mix_p, unit_end=unit_at)
            ph["d_z"] = mix_d + 1
            mix_end = mix_d = mix_d + 1 + 4 * n_s + 3
            ph["pool0"], ph["mix_end"] = mix_q, mix_d
            ph["q_pool"] = [mix_q + 12 * s + 12 for s in range(n_s)]
            mix_q += 12 * n_s
            mix_a += 4 * n_s
            mix_p += 2 * n_s
            mixed = ph
        elif kind == "attend":
            ph.update(unit_end=unit_at if ph["block"] == 1 else ph["gates"].start, mix_end=mix_end)
            if ph["block"] == 1:
                ph["mixed"] = mixed
            for call in ph["calls"]:
                for g in call["groups"]:
                    max_count += call["what"] in ("ctx", "swa")
                    inv_count += 2 if call["what"] == "swa" else 1
                    g["max_count"], g["inv_count"] = max_count, inv_count
            pairs_end = ph["calls"][-1]["pair0"] + 4

    def attend_order(at_):
        if at_["block"] == 1:
            return [(call["what"], call) for call in at_["calls"]]
        return [("sb", None)] + [(call["what"], call) for call in at_["calls"]]

    def gate_points(at_, emit):
        left = list(range(N_GATE)) if at_["block"] == 2 else []

        def point():
            if left:
                emit(at_["gates"], left.pop(0))
        return point

    GATE_ROPE = (1, 3, 5, 7, 9, 11)
    GATE_CALL = (2, 4, 6, 8)

    def rope_tiles():
        return [0, 1, 2, 3, 4, 18, 19, 20, 21, 22, 23, 24, 25]

    def out_tiles(call, hp):
        what = call["what"]
        if what == "near":
            return H_hi[:, 4 + hp, 0:S], H_lo[:, 4 + hp, 0:S]
        if what == "ctx":
            return H_hi[:, 4 + hp, S:512], H_lo[:, 4 + hp, S:512]
        f = hp + (0 if what == "swa" else 8)
        return O_hi[:, f, :], O_lo[:, f, :]

    def out_of(call, hp):
        return bank[call["out_banks"][hp % len(call["out_banks"])]][:, 0:S]

    LEAD = 2
    T_LAG = 3

    def mod_unit(ph, u):
        if ph.kind == "mod":
            return u
        return {0: 0, 1: 1, 4: 2, 5: 3}.get(u) if ph.side else None

    def own_unit(ph, u):
        return {2: 0, 3: 1, 6: 2, 7: 3}.get(u) if ph.side else u

    def mod_bank(ph, u):
        return bank[5 + u // 4] if ph.side else bank[(ph.start + u) % 4]

    def mod_source(ph, i, mu):
        first = ph.mod0 - 72 * ph.mod_layer
        return kpc(w_mod[ph.mod_layer])[:, :, bass.ds((first + 4 * i + mu) * P, P)]

    def moving_wait(ph, k):
        m = ph.more.get("moving", "h")
        if ph.kind == "branch" or m == "y":
            return None
        if m == "g":
            return g_lo_done, ph.more["hidden_end"] - ph.k + k + 1
        return h_lo_done, ph.h0 + k + 1

    def repeat(eng, n, body):
        body(0, True, n == 1)
        if n > 2:
            with eng.Fori(1, n) as i:
                body(i, False, False)
        elif n == 2:
            body(1, False, True)

    def at_least(eng, semaphore, value):
        if isinstance(value, int) and value <= 0:
            return
        eng.wait_ge(semaphore, value)

    def phase_steps(ph):
        return ph.n // ph.stride, ph.n % ph.stride

    def moving_of(ph):
        m = ph.more.get("moving", "h")
        if ph.kind in ("glu",) or (m == "h" and ph.more.get("dst") == "U") or m == "y":
            return H_hi, H_lo
        if m == "g":
            return (G_hi, G_lo) if ph.more["seg"] is not None else (G2_hi, G2_lo)
        return H2_hi, H2_lo

    def q_tile(what):
        return dict(near=8, ctx=8, swa=0, sb=6, moba=18)[what]

    stack = ExitStack()
    blk = stack.enter_context(nc.Block())

    @blk.sync
    def _(sp):
        sp.dma_start(const[:, 0:FIRST_COLS], consts[:, 0:FIRST_COLS]).then_inc(s_ident, 16)
        for p0, tile, n, ap in row_pieces:
            if tile == 0:
                sp.dma_start(rows_in[p0:p0 + n, tile, :], ap).then_inc(s_rows_first, 16)

        def sp_tokens():
            for p0, tile, n, ap in row_pieces:
                if tile > 0:
                    sp.dma_start(rows_in[p0:p0 + n, tile, :], ap).then_inc(s_rows, 16)
            sp.dma_start(tokens_in[:, 0:2, :], x.rearrange("b (t p) d -> p (b t) d", p=P)).then_inc(s_tok, 16)
            sp.dma_start(tokens_in[:, 2:4, :], ctx.rearrange("b (t p) d -> p (b t) d", p=P)).then_inc(s_tok, 16)

        def load(ph, i, u):
            t = ph.start + u + ph.stride * i
            slot = (ph.start + u) % SLOTS
            mu = mod_unit(ph, u)
            weights = ph.source(i, own_unit(ph, u)) if mu is None else mod_source(ph, i, mu)
            kk, cc = weights.shape[1], weights.shape[2]
            at_least(sp, lo_done, t - 3)
            sp.dma_start(raw[:, slot, 0:kk * cc].rearrange("p (k c) -> p k c", c=cc), weights).then_inc(raw_in[slot], 16)

        for kind, ph in plan:
            if kind == "tokens":
                sp_tokens()
            elif kind == "tables":
                sp.dma_start(const[:, FIRST_COLS:], consts[:, FIRST_COLS:]).then_inc(s_tables, 16)
            if kind != "gemm":
                continue

            def body(i, first, last, n_units=ph.stride):
                for u in range(n_units):
                    load(ph, i, u)
            steps, left = phase_steps(ph)
            if ph.kind == "branch":
                for i in range(steps):
                    body(i, i == 0, i == steps - 1)
            else:
                repeat(sp, steps, body)
            if left:
                body(steps, False, True, left)
        sp.wait_ge(final_copy, 4)
        sp.dma_start(out.rearrange("b (t p) d -> p (b t) d", p=P), tokens_out[:, :, :]).then_inc(s_store, 16)
        sp.wait_ge(s_store, 16)

    @blk.scalar
    def _(act):
        def split_ahead(ph, u, i):
            t = ph.start + u + AHEAD + ph.stride * i
            slot = (ph.start + u + AHEAD) % SLOTS
            if isinstance(t, int) and t >= total:
                return
            act.wait_ge(raw_in[slot], 16 * ((ph.start + u + AHEAD) // SLOTS + 1) + 16 // SLOTS * ph.stride * i)
            at_least(act, acc_done, t - 3)
            act.activation(w_hi[:, slot, :], raw[:, slot, :], ACT.Copy).then_inc(hi_done, 1)

        act.wait_ge(init_copy, 1)
        for s, name in enumerate(("c", "c_ctx")):
            act.activation(silu_c[:, :, s], vec(name, 0, KD), ACT.Silu).then_inc(silu_c_done, 1)
        act.wait_ge(silu_c_done, 2)
        act.wait_ge(memset_done, 3)
        for s in range(2):
            act.activation(c_pad[:, :, 2 * s], silu_c[:, :, s], ACT.Copy).then_inc(c_split, 1)
        for t in range(AHEAD):
            act.wait_ge(raw_in[t], 16)
            act.activation(w_hi[:, t, :], raw[:, t, :], ACT.Copy).then_inc(hi_done, 1)

        def square(r, k, src):
            if isinstance(k, int):
                at_least(act, sq_added, (KD - 2) * r + (k - 2 if k > 2 else k // 2))
                if k == 1:
                    at_least(act, stat_done, r)
            else:
                act.wait_ge(sq_added, k + (KD - 2) * r - 2)
            act.activation(sq[:, k % 2, 0:src.shape[-1]], src, ACT.Square).then_inc(sq_done, 1)

        def act_gemm(ph):
            k = ph.kind
            squares = k == "residual" and ph.more["stats"]

            def square_after(f):
                act.wait_ge(acc_free, ph.start + f + 1)
                square(ph.more["norm_next"], f, X[:, f, 0:ph.width] if ph.more["seg"] is not None else X2[:, f, :])
            width = ph.width

            def step(i, first, last, n_units=ph.stride):
                for u in range(n_units):
                    t = ph.start + u + ph.stride * i
                    split_ahead(ph, u, i)
                    if squares and not (first and u == 0):
                        square_after(4 * i + u - 1)
                    if ph.more.get("squares") and u % 2:
                        f = 2 * i + u // 2
                        act.wait_ge(init_copy, f + n_row_tiles + 1)
                        at_least(act, sq_added, f - 1)
                        act.activation(sq[:, u // 2, :], X[:, f, :], ACT.Square).then_inc(sq_done, 1)
                    if mod_unit(ph, u) is not None:
                        continue
                    v = own_unit(ph, u)
                    b = (ph.start + v) % 4
                    if k == "glu":
                        step_end = ph.start + ph.stride * (i + 1)
                        if v < 2:
                            act.wait_ge(acc_done, t + 1)
                            at_least(act, acc_free, step_end - ph.stride - 2 + 2 * v)
                            act.activation(sil[:, v, 0:width], bank[b][:, 0:width], ACT.Silu).then_inc(silu_done, 1)
                        else:
                            act.wait_ge(acc_free, step_end + 2 * (v - 3))
                            act.activation(G_hi[:, 2 * i + v - 2, 0:width], g32[:, v - 2, 0:width],
                                           ACT.Copy).then_inc(g_hi_done, 1)
                    elif k == "conv_glu":
                        layer, third = ph.more["layer"], ph.more["third"]
                        if u < 2 and not first:
                            hidden_hi(ph, i - 1, u)
                        f = (0 if u < 2 else FT) + third * 8 + 2 * i + u % 2
                        g = ph.g0 + 2 * i + u % 2
                        if u == 1:
                            silu_conv(ph, i, 0)
                        if u == 2:
                            silu_conv(ph, i, 1)
                        act.wait_ge(acc_done, t + 1)
                        if u < 2:
                            at_least(act, g_mul_done, g - GLU_TILES - 1)
                            dst = sil
                        else:
                            at_least(act, g_lo_done, g - 1)
                            dst = g32
                        act.activation(dst[:, u % 2, 0:S], bank[b][:, 0:S], ACT.Identity,
                                       scale=vec("conv_w_2", (layer * 3 + 2) * 2 * FT + f),
                                       bias=vec("conv_b_2", layer * 2 * FT + f)).then_inc(conv0_done, 1)
                    elif k == "branch" and i == 2:
                        for e in range(2):
                            f = 2 * u + e
                            act.wait_ge(merge_step, ph.merge0 + 4 + u + 1)
                            ins = act.activation(H2_hi[:, f, :], merged[:, f, :], ACT.Copy)
                        ins.then_inc(h_hi_done, 2)
            n4, left = phase_steps(ph)
            if k == "branch":
                for i in range(n4):
                    step(i, i == 0, i == n4 - 1)
            else:
                repeat(act, n4, step)
            if left:
                step(n4, False, True, left)
            if squares:
                square_after(KD - 1)
            if k == "conv_glu":
                for e in range(2):
                    hidden_hi(ph, n4 - 1, e)

        def hidden_hi(ph, i, e):
            act.wait_ge(g_mul_done, ph.gm0 + 2 * i + e + 1)
            act.activation(G2_hi[:, 2 * i + e, :], g32[:, e, 0:S], ACT.Copy).then_inc(g_hi_done, 1)

        def silu_conv(ph, i, e):
            act.wait_ge(acc_free, ph.start + 4 * i + e + 1)
            act.activation(sil[:, e, 0:S], sil[:, e, 0:S], ACT.Silu).then_inc(silu_done, 1)

        def act_norm(nm):
            r, width = nm["r"], nm.get("width", S)
            act.activation(warm[:, r:r + 1], eps[:, 0:1], ACT.Sqrt)
            act.wait_ge(stat_done, r + 1)
            act.activation(rstd_tok[:, 0:width // P], STAT[:, 0:width // P], ACT.Sqrt, scale=1.0 / D, bias=eps[:, 0:1]) \
               .then_inc(rms_done, 1)
            if nm["kind"] == "mod":
                seg = nm["seg"]
                for k in range(KD):
                    act.wait_ge(n_mul, nm["a0"] + k + 1)
                    for s in range(width // S):
                        ins = act.activation(T1[:, k, s * S:s * S + S], T1[:, k, s * S:s * S + S], ACT.Identity,
                                             scale=modv[:, seg, 1, k, s:s + 1], bias=modv[:, seg, 0, k, s:s + 1])
                    ins.then_inc(n_aff, 1)
            elif nm["kind"] == "plain":
                name, at0 = nm["gain"]
                for k in range(KD):
                    act.wait_ge(n_mul, nm["a0"] + k + 1)
                    act.activation(T2[:, k, :], T2[:, k, :], ACT.Copy, scale=vec(name, at0 + k)).then_inc(n_aff, 1)
            elif nm["kind"] == "renorm":
                for k in range(KD):
                    act.wait_ge(final_mul, k + 1)
                    square(r + 1, k, X2[:, k, :])

        def act_mixers(mx):
            layer = mx["layer"]
            for s in range(mx["streams"]):
                cols = slice(s * S, s * S + S)
                for j in range(2):
                    act.wait_ge(mix_dve, mx["d_z"])
                    act.activation(U[:, 4 + j, cols], U[:, j, cols], ACT.Copy,
                                   scale=vec("conv_w", (layer * 3 + 1) * 2 + j)).then_inc(mix_act, 1)

        def act_pooled(mx):
            layer = mx["layer"]
            for s in range(mx["streams"]):
                for j in range(2):
                    act.wait_ge(mix_pe, mx["pe0"] + 2 * s + j + 1)
                    act.activation(U[:, 6 + j, s * S:s * S + S], bank[2 * s + j][:, 0:S], ACT.Copy,
                                   scale=vec("pool_scale", layer * 2 + j)).then_inc(mix_act, 1)

        def gate_evict(ph, q):
            act.wait_ge(acc_done, ph.start + q + 1)
            act.activation(gates[:, q, :], bank[7][:, 0:S], ACT.Identity,
                           bias=vec("b_gate", ph.more["layer"] * N_GATE + q)).then_inc(acc_free, 1)

        multiplied = []

        def evict_gate():
            if multiplied:
                gate_evict(*multiplied.pop())

        def act_gate(ph, q):
            evict_gate()
            split_ahead(ph, q % 4, q // 4)
            multiplied.append((ph, q))

        def act_attend(at_):
            point = gate_points(at_, act_gate)
            if at_["block"] == 2:
                for _ in GATE_ROPE:
                    point()
            for what, call in attend_order(at_):
                if what == "sb":
                    act_stick(at_, point)
                else:
                    act_call(call, point)
            if at_["block"] == 2:
                ph = at_["gates"]
                evict_gate()
                act.wait_ge(acc_free, ph.start + N_GATE)
                for i in range(3):
                    act.activation(gates[:, 8 * i:8 * i + 8, :], gates[:, 8 * i:8 * i + 8, :], ACT.Sigmoid) \
                       .then_inc(gate_done, 1)
            if at_["block"] == 1:
                act_pooled(at_["mixed"])

        def act_call(call, point):
            groups = call["groups"]
            n_g = len(groups)
            for j in range(n_g + T_LAG):
                if j in GATE_CALL:
                    point()
                if j >= T_LAG:
                    g = groups[j - T_LAG]
                    n = g["n"]
                    act.wait_ge(pt_done, n + 1)
                    head = 2 * call["pair0"] + g["head"]
                    at_least(act, pv_done, head - 1)
                    pb = bank[call["pt_banks"][(n - call["n0"]) % len(call["pt_banks"])]]
                    e = g["head"] % 2
                    if g["qt"] is None:
                        w = P * len(g["blocks"])
                        act.activation(probs_t[:, e, 0:w], pb[:, 0:w], ACT.Copy).then_inc(pt_copy, 1)
                    else:
                        dst = probs_t[:, e, :].rearrange("p (k q) -> p k q", q=S)[:, :, g["qt"] * P:g["qt"] * P + P]
                        act.activation(dst, pb[:, :].rearrange("p (k q) -> p k q", q=P), ACT.Copy).then_inc(pt_copy, 1)
                if j < n_g:
                    g = groups[j]
                    n = g["n"]
                    act.wait_ge(max_done, n + 1)
                    at_least(act, pt_done, n - 3)
                    for si, (qt, a, b) in enumerate(g["segs"]):
                        col = (g["seg0"] + si) % 16
                        sb_ = bank[call["score_banks"][(n - call["n0"]) % len(call["score_banks"])]]
                        ins = act.activation(probs[:, n % 4, a:b], sb_[:, a:b],
                                             ACT.Exp, bias=neg_max[:, col:col + 1],
                                             scale=SCALE if call["what"] == "ctx" else 1.0,
                                             accum_out=row_sum[:, col:col + 1])
                        if call["what"] == "swa":
                            h = call["layer"] * 8 + g["head"]
                            ins = act.activation(sink_e[:, col:col + 1], sink[:, h:h + 1], ACT.Exp,
                                                 bias=neg_max[:, col:col + 1])
                    ins.then_inc(exp_done, 1)
                if j % 2:
                    evict_gate()

        def act_stick(at_, point):
            log0 = 3 * at_["sb0"]
            for j in range(4):
                point()
                act.wait_ge(sb_scaled, at_["sb0"] + j + 1)
                act.activation(sb_e[j][:, :, :], sb_z[:, j, :, :], ACT.Abs).then_inc(sb_log, 1)
                act.wait_ge(sb_log, log0 + 2 * j + 1)
                act.activation(sb_e[j][:, :, :], sb_e[j][:, :, :], ACT.Exp, scale=-1.0).then_inc(sb_log, 1)
            for j in range(4):
                act.wait_ge(sb_log, log0 + 8 + j)
                act.activation(sb_e[j][:, :, :], sb_e[j][:, :, :], ACT.Ln, bias=ones[:, 0:1]).then_inc(sb_log, 1)
            for j in range(6):
                point()
                if 1 <= j <= 4:
                    z_ = sb_z[:, j - 1, :, :]
                    act.wait_ge(sb_diff, at_["sb0"] + j)
                    act.activation(z_, z_, ACT.Exp).then_inc(sb_weight, 1)

        for kind, ph in plan:
            if kind == "gemm" and ph.kind != "gate":
                act_gemm(ph)
            elif kind == "norm":
                act_norm(ph)
            elif kind == "mixers":
                act_mixers(ph)
            elif kind == "attend":
                act_attend(ph)

    @blk.vector
    def _(dve):
        def split_ahead(ph, u, i):
            t = ph.start + u + AHEAD + ph.stride * i
            slot = (ph.start + u + AHEAD) % SLOTS
            if isinstance(t, int) and t >= total:
                return
            dve.wait_ge(hi_done, t + 1)
            dve.tensor_tensor(w_lo[:, slot, :], raw[:, slot, :], w_hi[:, slot, :].bitcast(F32),
                              ALU.subtract).then_inc(lo_done, 1)

        def dve_vectors(tile):
            dve.wait_ge(init_t, tile + 1)
            used = min(P, n_rows - tile * P)
            dve.tensor_copy(vecs[:, tile * P:tile * P + used], bank[4 + tile % 2][:, 0:used]).then_inc(init_copy, 1)

        def dve_tokens():
            for tile in range(1, n_row_tiles):
                dve_vectors(tile)
            for f in range(KD):
                dve.wait_ge(init_t, n_row_tiles + f + 1)
                dve.tensor_copy(X[:, f, :], bank[f % 4][:, :]).then_inc(init_copy, 1)

        dve_vectors(0)
        dve.wait_ge(c_split, 2)
        for s in range(2):
            ins = dve.tensor_tensor(c_pad[:, :, 2 * s + 1], silu_c[:, :, s], c_pad[:, :, 2 * s].bitcast(F32), ALU.subtract)
        ins.then_inc(c_split, 1)
        for t in range(AHEAD):
            dve.wait_ge(hi_done, t + 1)
            dve.tensor_tensor(w_lo[:, t, :], raw[:, t, :], w_hi[:, t, :].bitcast(F32), ALU.subtract).then_inc(lo_done, 1)

        def dve_mod(seg):
            layer, i = seg // 3, seg % 3
            src = bank[7][:, seg * 48:seg * 48 + 48].rearrange("p (n s) -> p n s", s=2)
            dst = modv[:, seg, :, :, :].rearrange("p a k s -> p (a k) s")
            for s in range(2):
                ins = dve.tensor_tensor(dst[:, :, s], src[:, :, s], vec("b_mod", layer * 72 + i * 24, 24), ALU.add)
            ins.then_inc(mod_step, 1)
            dve.wait_ge(mod_step, seg + 1)
            for s in range(2):
                ins = dve.scalar_tensor_tensor(modv[:, seg, 1, :, s], modv[:, seg, 1, :, s], 1.0,
                                               vec("norm_g", layer * 24 + i * 8, KD), ALU.add, ALU.mult)
            if i != 1:
                ins = dve.tensor_scalar(modv[:, seg, 2, :, :], modv[:, seg, 2, :, :], 0.5, None, ALU.mult)
            ins.then_inc(mod_ready, 1)

        done_segs = [0]

        def dve_gemm(ph):
            k, width = ph.kind, ph.width
            if k == "residual":
                dve.wait_ge(acc_free, ph.start)
                if ph.more["seg"] is not None:
                    dve.wait_ge(mod_ready, ph.more["seg"] + 1)

            def step(i, first, last, n_units=ph.stride):
                for u in range(n_units):
                    t = ph.start + u + ph.stride * i
                    split_ahead(ph, u, i)
                    mu, v = mod_unit(ph, u), own_unit(ph, u)
                    if mu is not None:
                        if mu % 2:
                            dve.wait_ge(acc_done, t + 1)
                            at_least(dve, mod_done, ph.mod0 + 4 * i - 3 + mu)
                            dve.tensor_copy(mod_rows[:, mu // 2, :], mod_bank(ph, u - 1)[:, 0:256]).then_inc(acc_free, 2)
                        continue
                    b = (ph.start + v) % 4
                    if k == "glu":
                        if v >= 2:
                            g = ph.g0 + 2 * i + v - 2
                            dve.wait_ge(acc_done, t + 1)
                            dve.wait_ge(silu_done, g + 1)
                            at_least(dve, g_lo_done, g - 1)
                            dve.tensor_tensor(g32[:, v - 2, 0:width], bank[b][:, 0:width], sil[:, v - 2, 0:width],
                                              ALU.mult).then_inc(acc_free, 2)
                    elif k == "conv_glu":
                        layer, third = ph.more["layer"], ph.more["third"]
                        f = (0 if u < 2 else FT) + third * 8 + 2 * i + u % 2
                        dst = (sil if u < 2 else g32)[:, u % 2, 0:S]
                        m = 2 * ph.gm0 + 4 * i + u
                        dve.wait_ge(conv0_done, m + 1)
                        dve.scalar_tensor_tensor(dst[:, 1:S], bank[b][:, 0:S - 1],
                                                 vec("conv_w_2", (layer * 3 + 1) * 2 * FT + f), dst[:, 1:S],
                                                 ALU.mult, ALU.add).then_inc(conv1_done, 1)
                        dve.wait_ge(conv1_done, m + 1)
                        dve.scalar_tensor_tensor(dst[:, 2:S], bank[b][:, 0:S - 2],
                                                 vec("conv_w_2", layer * 3 * 2 * FT + f), dst[:, 2:S],
                                                 ALU.mult, ALU.add).then_inc(acc_free, 1)
                        if u >= 2:
                            dve.wait_ge(acc_free, t + 1)
                            dve.wait_ge(silu_done, ph.g0 + 2 * i + u - 1)
                            dve.tensor_tensor(g32[:, u - 2, 0:S], g32[:, u - 2, 0:S], sil[:, u - 2, 0:S], ALU.mult) \
                               .then_inc(g_mul_done, 1)
                    elif k == "residual":
                        f = 4 * i + u
                        dve.wait_ge(acc_done, t + 1)
                        if ph.more["seg"] is None:
                            dve.tensor_tensor(X2[:, f, :], bank[b][:, 0:S], X2[:, f, :], ALU.add).then_inc(acc_free, 1)
                        else:
                            for s in range(width // S):
                                cols = slice(s * S, s * S + S)
                                ins = dve.scalar_tensor_tensor(X[:, f, cols], bank[b][:, cols],
                                                               modv[:, ph.more["seg"], 2, f, s:s + 1], X[:, f, cols],
                                                               ALU.mult, ALU.add)
                            ins.then_inc(acc_free, 1)
                    elif k == "store":
                        f = ph.more["f0"] + 4 * i + u
                        dst = U if ph.more["dst"] == "U" else U2
                        dve.wait_ge(acc_done, t + 1)
                        dve.tensor_copy(dst[:, f, 0:width], bank[b][:, 0:width]).then_inc(acc_free, 1)
                    elif k == "branch":
                        g = gates[:, 8 * i + 2 * u:8 * i + 2 * u + 2, :].rearrange("p f t -> p (f t)")
                        m = merged[:, 2 * u:2 * u + 2, :].rearrange("p f t -> p (f t)")
                        tmp = sil[:, u % 2, :]
                        dve.wait_ge(gate_done, 3 * ph.more["layer"] + i + 1)
                        dve.wait_ge(acc_done, t + 1)
                        if i == 0:
                            dve.tensor_tensor(m, bank[b][:, :], g, ALU.mult).then_inc(acc_free, 1)
                        else:
                            dve.tensor_tensor(tmp, bank[b][:, :], g, ALU.mult).then_inc(acc_free, 1)
                            dve.wait_ge(acc_free, t + 1)
                            dve.tensor_tensor(m, m, tmp, ALU.add).then_inc(merge_step, 1)
                            dve.wait_ge(merge_step, ph.merge0 + 4 * (i - 1) + u + 1)
            n4, left = phase_steps(ph)
            if k == "branch":
                for i in range(n4):
                    step(i, i == 0, i == n4 - 1)
            else:
                repeat(dve, n4, step)
            if left:
                step(n4, False, True, left)

        def dve_norm(nm):
            r, width, kind = nm["r"], nm.get("width", S), nm["kind"]
            dve.wait_ge(rms_done, r + 1)
            dve.reciprocal(rstd_tok[:, 0:width // P], rstd_tok[:, 0:width // P]).then_inc(rstd_done, 1)
            dve.wait_ge(rstd_done, r + 1)
            for tb in range(width // P):
                ins = dve.tensor_scalar(rstd_diag[:, tb, :], ident, rstd_tok[:, tb:tb + 1], None, ALU.mult)
            ins.then_inc(diag_done, 1)
            dve.wait_ge(rstd_spread, r + 1)
            if kind in ("mod", "plain"):
                src, dst, hi = (X, T1, H_hi) if kind == "mod" else (X2, T2, H2_hi)
                if kind == "mod":
                    dve.wait_ge(mod_ready, nm["seg"] + 1)
                m0 = nm["a0"]
                for k in range(KD + 2):
                    if k < KD:
                        dve.tensor_tensor(dst[:, k, 0:width], src[:, k, 0:width], STAT[:, 0:width], ALU.mult) \
                           .then_inc(n_mul, 1)
                    if k >= 2:
                        dve.wait_ge(n_aff, m0 + k - 1)
                        dve.tensor_copy(hi[:, k - 2, 0:width], dst[:, k - 2, 0:width]).then_inc(h_hi_done, 1)
            else:
                name, at0 = nm["gain"]
                for k in range(KD):
                    src, dst = (X, X2) if kind == "renorm" else (X2, T2)
                    dve.scalar_tensor_tensor(dst[:, k, :], src[:, k, 0:S], vec(name, at0 + k), STAT[:, 0:S],
                                             ALU.mult, ALU.mult).then_inc(final_mul, 1)

        def dve_mixers(mx):
            layer, streams = mx["layer"], mx["streams"]
            w = streams * S
            n = [mx["dve0"]]

            def step(ins):
                ins.then_inc(mix_dve, 1)
                n[0] += 1
                dve.wait_ge(mix_dve, n[0])
            dve.wait_ge(acc_free, mx["unit_end"])
            dve.wait_ge(acc_done, mx["unit_end"])
            step(dve.tensor_tensor(U[:, 0:2, 0:w], U[:, 4:6, 0:w], U[:, 0:2, 0:w], ALU.mult))
            assert n[0] == mx["d_z"]
            for s in range(streams):
                a = s * S
                for j in range(2):
                    dve.wait_ge(mix_act, mx["act0"] + 2 * s + j + 1)
                    step(dve.scalar_tensor_tensor(U[:, 4 + j, a + 1:a + S], U[:, j, a:a + S - 1],
                                                  vec("conv_w", layer * 6 + j), U[:, 4 + j, a + 1:a + S],
                                                  ALU.mult, ALU.add))
                    step(dve.scalar_tensor_tensor(U[:, 4 + j, a:a + S - 1], U[:, j, a + 1:a + S],
                                                  vec("conv_w", layer * 6 + 4 + j), U[:, 4 + j, a:a + S - 1],
                                                  ALU.mult, ALU.add))
            step(dve.tensor_tensor(U[:, 4:6, 0:w], U[:, 4:6, 0:w], U[:, 2:4, 0:w], ALU.mult))
            step(dve.tensor_copy(H_hi[:, 0:2, 0:w], U[:, 4:6, 0:w]))
            step(dve.tensor_tensor(H_lo[:, 0:2, 0:w], U[:, 4:6, 0:w], H_hi[:, 0:2, 0:w].bitcast(F32), ALU.subtract))
            assert n[0] == mx["mix_end"]

        def dve_bias(layer):
            near = table("m_near").unsqueeze(1).to_broadcast([P, 8, 64])
            flat = bias_t[:, :, :, :].rearrange("p h r k -> p (h r) k")
            for j in range(6):
                dve.wait_ge(bias_pe, layer * 6 + j + 1)
                dve.tensor_tensor(flat[:, 8 * j:8 * j + 8, :], bank[j % 4][:, :].rearrange("p (r k) -> p r k", k=64), near,
                                  ALU.min).then_inc(bias_done, 1)

        def dve_attend(at_):
            b1 = at_["block"] == 1
            point = gate_points(at_, lambda ph, q: split_ahead(ph, q % 4, q // 4))
            if b1:
                dve_bias(at_["layer"])
                dve.wait_ge(bias_done, 6 * (at_["layer"] + 1))
            for j, (tile, nb) in enumerate(at_["vt_jobs"]):
                m = at_["vt0"] + j
                dve.wait_ge(vt_t, m + 1)
                w = nb * P
                dve.tensor_copy(vt[:, j * w:j * w + w], bank[4 + m % 2][:, 0:w]).then_inc(vt_copy, 1)
            if not b1:
                for j in range(13):
                    m = at_["rope0"] + j
                    tile = rope_tiles()[j]
                    dve.wait_ge(rope_pe, m + 1)
                    at_least(dve, rope_dve, 2 * m - 2)
                    dve.tensor_tensor(rope_t[:, m % 2, :], bank[5 + m % 2][:, 0:S], table("sin"), ALU.mult) \
                       .then_inc(rope_dve, 1)
                    dve.wait_ge(rope_pool, m + 1)
                    dve.wait_ge(rope_dve, 2 * m + 1)
                    dve.tensor_tensor(U2[:, tile, :], U2[:, tile, :], rope_t[:, m % 2, :], ALU.add).then_inc(rope_dve, 1)
                    if j in GATE_ROPE:
                        point()
                dve.wait_ge(rope_dve, 2 * (at_["rope0"] + 13))
                dve.tensor_copy(k_swap[0:HD, :], U2[HD:P, 4, :])
                dve.tensor_copy(k_swap[HD:P, :], U2[0:HD, 4, :]).then_inc(k_swap_done, 1)
            for what, call in attend_order(at_):
                if what == "sb":
                    dve_stick(at_, point)
                else:
                    dve_call(call, point)
            if b1:
                dve_pooled(at_["mixed"])

        def dve_pooled(mx):
            w = mx["streams"] * S
            dve.wait_ge(mix_act, mx["act0"] + 4 * mx["streams"])
            src = U[:, 6:8, 0:w]
            dve.tensor_copy(H_hi[:, 2:4, 0:w], src).then_inc(mix_split, 1)
            dve.wait_ge(mix_split, 2 * mx["layer"] + 1)
            dve.tensor_tensor(H_lo[:, 2:4, 0:w], src, H_hi[:, 2:4, 0:w].bitcast(F32), ALU.subtract).then_inc(mix_split, 1)

        def dve_out(pair, src, hi, lo):
            dve.wait_ge(pv_done, 2 * (pair + 1))
            dve.tensor_copy(hi, src).then_inc(o_step, 1)
            dve.wait_ge(o_step, pair + 1)
            dve.tensor_tensor(lo, src, hi.bitcast(F32), ALU.subtract).then_inc(o_done, 1)

        def dve_call(call, point):
            groups, what = call["groups"], call["what"]
            n_g = len(groups)
            if what == "swa":
                dve.wait_ge(s_small, 16 + 64 * DEPTH)
            for j in range(n_g + T_LAG + 2):
                jj = j - T_LAG - 2
                if jj >= 0 and jj < n_g and groups[jj]["last"] and groups[jj]["head"] % 2 == 1:
                    hp = groups[jj]["head"] // 2
                    hi, lo = out_tiles(call, hp)
                    ob = out_of(call, hp)
                    dve_out(call["pair0"] + hp, ob, hi, lo)
                if j in GATE_CALL:
                    point()
                if j < n_g:
                    g = groups[j]
                    n = g["n"]
                    sb_ = bank[call["score_banks"][(n - call["n0"]) % len(call["score_banks"])]]
                    dve.wait_ge(sc_done, n + 1)
                    if what == "near":
                        rr = 2 - 2 * g["qt"]
                        dve.scalar_tensor_tensor(sb_[:, 0:S], sb_[:, 0:S], SCALE,
                                                 bias_t[:, g["head"], rr:rr + 4, :].rearrange("p r k -> p (r k)"),
                                                 ALU.mult, ALU.add)
                        dve.tensor_scalar(sb_[:, S:512], sb_[:, S:512], SCALE, None, ALU.mult).then_inc(bias_add, 1)
                    elif what == "ctx":
                        at_least(dve, bias_add, n)
                        dve.nop().then_inc(bias_add, 1)
                    else:
                        mask = table("m_band" if what == "swa" else "m_causal")
                        dve.scalar_tensor_tensor(sb_[:, 0:384], sb_[:, 0:384], SCALE, mask, ALU.mult, ALU.add) \
                           .then_inc(bias_add, 1)
                    dve.wait_ge(bias_add, n + 1)
                    at_least(dve, p_ready, n - 3)
                    c0 = g["seg0"] % 16
                    ns = len(g["segs"])
                    for si, (qt, a, b) in enumerate(g["segs"]):
                        ins = dve.tensor_reduce(neg_max[:, c0 + si:c0 + si + 1], sb_[:, a:b], AX.X, ALU.max,
                                                negate=what != "ctx" and what != "swa")
                    if what == "ctx":
                        ins.then_inc(max_step, 1)
                        dve.wait_ge(max_step, g["max_count"])
                        dve.tensor_scalar(neg_max[:, c0:c0 + ns], neg_max[:, c0:c0 + ns], -SCALE, None, ALU.mult) \
                           .then_inc(max_done, 1)
                    elif what == "swa":
                        ins.then_inc(max_step, 1)
                        dve.wait_ge(max_step, g["max_count"])
                        h = call["layer"] * 8 + g["head"]
                        dve.tensor_scalar(neg_max[:, c0:c0 + ns], neg_max[:, c0:c0 + ns], sink[:, h:h + 1], -1.0,
                                          ALU.max, ALU.mult).then_inc(max_done, 1)
                    else:
                        ins.then_inc(max_done, 1)
                if 1 <= j <= n_g:
                    g = groups[j - 1]
                    n = g["n"]
                    c0, ns = g["seg0"] % 16, len(g["segs"])
                    dve.wait_ge(exp_done, n + 1)
                    if what == "swa":
                        dve.tensor_tensor(row_sum[:, c0:c0 + ns], row_sum[:, c0:c0 + ns], sink_e[:, c0:c0 + ns], ALU.add) \
                           .then_inc(inv_step, 1)
                        dve.wait_ge(inv_step, g["inv_count"] - 1)
                    dve.reciprocal(row_inv[:, c0:c0 + ns], row_sum[:, c0:c0 + ns]).then_inc(inv_step, 1)
                    dve.wait_ge(inv_step, g["inv_count"])
                    for si, (qt, a, b) in enumerate(g["segs"]):
                        ins = dve.tensor_scalar(probs[:, n % 4, a:b], probs[:, n % 4, a:b],
                                                row_inv[:, c0 + si:c0 + si + 1], None, ALU.mult)
                    ins.then_inc(p_ready, 1)

        def dve_stick(at_, point):
            log0 = 3 * at_["sb0"]
            for j in range(4):
                dve.wait_ge(sb_scores, at_["sb0"] + j + 1)
                for e in range(2):
                    ins = dve.scalar_tensor_tensor(sb_z[:, j, e, :], bank[2 * (j % 2) + e][:, 0:384], SCALE,
                                                   table("m_past"), ALU.mult, ALU.add)
                ins.then_inc(sb_scaled, 1)
                point()
            for j in range(7):
                if j < 4:
                    dve.wait_ge(sb_log, log0 + 8 + j + 1)
                    if j == 0:
                        dve.wait_ge(sb_scaled, at_["sb0"] + 4)
                    dve.scalar_tensor_tensor(sb_e[j][:, :, :], sb_z[:, j, :, :], 0.0, sb_e[j][:, :, :],
                                             ALU.max, ALU.add).then_inc(sb_soft, 1)
                if j >= 3:
                    o = j - 3
                    dve_out(at_["sb_pair0"] + o, bank[6][:, 0:S], O_hi[:, 4 + o, :], O_lo[:, 4 + o, :])
                if 1 <= j <= 4:
                    dve.wait_ge(sb_remain, at_["sb0"] + j)
                    for e in range(2):
                        z_ = sb_z[:, j - 1, e, :]
                        ins = dve.tensor_tensor(z_, z_, bank[4 + e][:, 0:384], ALU.subtract)
                    ins.then_inc(sb_diff, 1)
                if j <= 5:
                    point()

        for kind, ph in plan:
            if kind == "tokens":
                dve_tokens()
            elif kind == "mod_read":
                dve.wait_ge(mod_done, 24 * ph["end"])
                for seg in range(done_segs[0], ph["end"]):
                    dve_mod(seg)
                done_segs[0] = ph["end"]
            elif kind == "gemm" and ph.kind != "gate":
                dve_gemm(ph)
            elif kind == "norm":
                dve_norm(ph)
            elif kind == "mixers":
                dve_mixers(ph)
            elif kind == "attend":
                dve_attend(ph)
        for q in range(4):
            dve.wait_ge(final_t, q + 1)
            tb, fh = q // 2, q % 2
            dve.tensor_copy(tokens_out[:, tb, fh * 512:fh * 512 + 512], bank[q][:, :]).then_inc(final_copy, 1)

    @blk.gpsimd
    def _(pool):
        pool.memset(ones[:, :], 1.0)
        pool.memset(eps[:, :], EPS)
        pool.memset(c_pad[:, :, :].bitcast(F32), 0.0)
        pool.memset(pool_bd[:, :, :], 0.0).then_inc(memset_done, 3)
        pool.dma_start(sink[:, :], sinks_2.rearrange("l h -> (l h)").partition_broadcast(P)).then_inc(s_small, 16)

        def pool_w_load(layer):
            for g in range(4):
                lo = HD * (g % 2)
                pool.dma_start(pool_bd[lo:lo + HD, g // 2, lo:lo + HD], pool_w[layer, g]).then_inc(s_small, 16)

        def bias_load(layer):
            for b in range(2):
                for h in range(8):
                    src = bass.AP(tensor=rpb.tensor, offset=rpb[layer, h].offset + (5 - b) * 31 - 48,
                                  ap=[[1, 64], [31, 6], [1, 64]])
                    pool.dma_start(bias_t[64 * b:64 * b + 64, h, :, :], src).then_inc(s_bias, 16)

        pool.wait_ge(memset_done, 3)
        pool_w_load(0)
        bias_load(0)

        def square_sum(r, width):
            at_least(pool, stat_done, r)
            for k in range(1, KD - 1):
                pool.wait_ge(sq_done, KD * r + k + 1)
                if k > 1:
                    pool.wait_ge(sq_added, (KD - 2) * r + k - 1)
                pool.tensor_tensor(sq_sum[:, 0:width], sq[:, 0, 0:width] if k == 1 else sq_sum[:, 0:width],
                                   sq[:, k % 2, 0:width], ALU.add).then_inc(sq_added, 1)

        def pool_gemm(ph):
            k, width = ph.kind, ph.width
            if k in ("glu", "conv_glu"):
                hi, lo = (G_hi, G_lo) if k == "glu" else (G2_hi, G2_lo)

                def step(i, first, last):
                    for e in range(2):
                        g = ph.g0 + 2 * i + e
                        pool.wait_ge(g_hi_done, g + 1)
                        pool.tensor_tensor(lo[:, 2 * i + e, 0:width], g32[:, e, 0:width],
                                           hi[:, 2 * i + e, 0:width].bitcast(F32), ALU.subtract).then_inc(g_lo_done, 1)
                repeat(pool, phase_steps(ph)[0], step)
            elif k == "residual" and ph.more["stats"]:
                square_sum(ph.more["norm_next"], width)
            elif k == "branch":
                for u in range(4):
                    for e in range(2):
                        f = 2 * u + e
                        pool.wait_ge(h_hi_done, ph.h0 + 2 * u + 2)
                        pool.tensor_tensor(H2_lo[:, f, :], merged[:, f, :], H2_hi[:, f, :].bitcast(F32),
                                           ALU.subtract).then_inc(h_lo_done, 1)

        def pool_mixers(mx):
            streams = mx["streams"]
            n = [mx["pool0"]]

            def step(ins):
                ins.then_inc(mix_pool, 1)
                n[0] += 1
                pool.wait_ge(mix_pool, n[0])
            pool.wait_ge(acc_free, mx["unit_end"])
            pool.wait_ge(s_tables, 16)
            for s in range(streams):
                a, pad = s * S, 12
                step(pool.memset(pool_a[:, :, :], 0.0))
                step(pool.memset(pool_b[:, :, :], 0.0))
                step(pool.tensor_copy(pool_a[:, :, pad:pad + S], U[:, 6:8, a:a + S]))
                ic = table("inv_count").rearrange("p (j t) -> p j t", t=S)
                src, dst = pool_a, pool_b
                for g, (left, right, lo_, hi_) in enumerate(((1, 0, 1, 280), (1, 1, 2, 279), (2, 2, 4, 277), (4, 4, 8, 272))):
                    step(pool.tensor_tensor(dst[:, :, lo_:hi_], src[:, :, lo_ - left:hi_ - left],
                                           src[:, :, lo_ + right:hi_ + right], ALU.add))
                    rows_ = slice(HD * (g % 2), HD * (g % 2) + HD)
                    step(pool.tensor_tensor(pool_c[rows_, s, g // 2, :], dst[rows_, g // 2, pad:pad + S], ic[rows_, g // 2, :],
                                           ALU.mult))
                    src, dst = dst, src
                step(pool.tensor_tensor(pool_c[:, s, :, :], pool_c[:, s, :, :], U[:, 6:8, a:a + S], ALU.subtract))
                assert n[0] == mx["q_pool"][s]

        def pool_norm(nm):
            kind, width = nm["kind"], nm.get("width", S)
            if kind in ("mod", "plain"):
                src, hi, lo = (T1, H_hi, H_lo) if kind == "mod" else (T2, H2_hi, H2_lo)
                for k in range(KD):
                    pool.wait_ge(h_hi_done, nm["h0"] + k + 1)
                    pool.tensor_tensor(lo[:, k, 0:width], src[:, k, 0:width], hi[:, k, 0:width].bitcast(F32),
                                       ALU.subtract).then_inc(h_lo_done, 1)
            elif kind == "renorm":
                square_sum(nm["r"] + 1, S)

        for kind, ph in plan:
            if kind == "tokens":
                square_sum(0, 512)
            elif kind == "gemm" and ph.kind != "gate":
                pool_gemm(ph)
            elif kind == "norm":
                pool_norm(ph)
            elif kind == "mixers":
                pool_mixers(ph)
            elif kind == "attend":
                if ph["block"] == 1:
                    if ph["layer"] + 1 < DEPTH:
                        pool.wait_ge(o_done, ph["calls"][-1]["pair0"] + 4)
                        pool.wait_ge(mix_pe, 4)
                        pool_w_load(ph["layer"] + 1)
                        bias_load(ph["layer"] + 1)
                else:
                    for j in range(13):
                        m = ph["rope0"] + j
                        tile = rope_tiles()[j]
                        pool.wait_ge(rope_pe, m + 1)
                        pool.tensor_tensor(U2[:, tile, :], U2[:, tile, :], table("cos"), ALU.mult).then_inc(rope_pool, 1)

    @blk.tensor
    def _(pe):
        def pe_vectors(tile):
            used = min(P, n_rows - tile * P)
            if tile >= 2:
                pe.wait_ge(init_copy, tile - 1)
            pe.transpose(bank[4 + tile % 2][:, 0:used], rows_in[0:used, tile, :], ident[0:used, 0:used]).then_inc(init_t, 1)

        def pe_tokens():
            pe.wait_ge(s_rows, 16 * (len(row_pieces) - first_pieces))
            for tile in range(1, n_row_tiles):
                pe_vectors(tile)
            pe.wait_ge(s_tok, 32)
            for f in range(KD):
                if f >= 4:
                    pe.wait_ge(init_copy, n_row_tiles + f - 3)
                for tb in range(4):
                    ins = pe.transpose(bank[f % 4][:, tb * P:tb * P + P], tokens_in[:, tb, f * P:f * P + P], ident)
                ins.then_inc(init_t, 1)
            pe.wait_ge(init_copy, n_row_tiles + KD)

        pe.wait_ge(s_ident, 16)
        pe.wait_ge(memset_done, 3)
        pe.wait_ge(s_rows_first, 16 * first_pieces)
        pe_vectors(0)
        pe.wait_ge(c_split, 3)

        def pe_mod_pair(ph, i, u):
            b = (ph.start + u) % 4
            t = ph.start + u + ph.stride * i
            pe.wait_ge(lo_done, t + 2)
            at_least(pe, acc_free, ph.start + ph.stride * (i - 1) + (4 if u else 2) if ph.side else t - 3)
            for k in range(KD):
                for w in (w_hi, w_lo):
                    ins = pe.matmul(mod_bank(ph, u)[:, 0:256], c_pad[:, k, :], w[:, b:b + 2, k * P:k * P + P],
                                    start=k == 0 and w is w_hi, stop=k == KD - 1 and w is w_lo)
            ins.then_inc(acc_done, 2)

        def pe_mod_turn(ph, i, mu):
            pe.wait_ge(acc_free, ph.start + ph.stride * i + mu // 2 * 2 + 2)
            pe.matmul(bank[7][:, bass.ds(2 * (ph.mod0 + mu) + 8 * i, 2)], mod_rows[:, mu // 2 % 2, mu % 2 * P:mu % 2 * P + P],
                      table("pick"), start=True, stop=True).then_inc(mod_done, 1)

        def pe_gemm(ph):
            xh, xl = moving_of(ph)
            if ph.kind == "branch":
                xh, xl = O_hi, O_lo
            width, kk = ph.width, ph.k
            m = ph.more.get("moving", "h")
            if ph.kind == "branch":
                pe.wait_ge(o_done, ph.more["pairs"])
            elif m == "y":
                pe.wait_ge(o_done, ph.more["pairs"])
                pe.wait_ge(mix_dve, ph.more["mix_end"])
                pe.wait_ge(mix_split, 2 * ph.more["mix_layer"] + 2)
            if ph.kind == "mod" or ph.side:
                at_least(pe, mod_ready, ph.more["reads"])

            def step(i, first, last, n_units=ph.stride):
                for u in range(n_units):
                    t = ph.start + u + ph.stride * i
                    b = (ph.start + u) % 4
                    mu = mod_unit(ph, u)
                    if mu is not None:
                        if mu % 2 == 0:
                            pe_mod_pair(ph, i, u)
                            if not ph.side:
                                for j in (mu - 2, mu - 1):
                                    if mu or not first:
                                        pe_mod_turn(ph, i, j)
                        continue
                    v = own_unit(ph, u)
                    b_w, b = b, (ph.start + v) % 4
                    joint = first and not ph.side and ph.kind != "branch" and moving_wait(ph, 0) and m in ("h", "g")
                    if joint and u == 0:
                        pe.wait_ge(lo_done, t + 2)
                        if m == "g":
                            pe.wait_ge(acc_free, ph.start - 2)
                            if ph.more["seg"] is not None:
                                pe.wait_ge(silu_done, ph.more["hidden_end"])
                            order = [(v, k) for v in range(2) for k in range(kk - 2)] + \
                                    [(v, k) for k in range(kk - 2, kk) for v in range(2)]
                        else:
                            at_least(pe, acc_free, ph.start)
                            order = [(v, k) for k in range(kk) for v in range(2)]
                        for v, k in order:
                            if v == 0:
                                pe.wait_ge(*moving_wait(ph, k))
                            wh, wl = (w[:, (b + v) % 4, k * P:k * P + P] for w in (w_hi, w_lo))
                            o = bank[(b + v) % 4][:, 0:width]
                            pe.matmul(o, wh, xh[:, k, 0:width], start=k == 0, stop=False)
                            pe.matmul(o, wl, xh[:, k, 0:width], start=False, stop=False)
                            ins = pe.matmul(o, wh, xl[:, k, 0:width], start=False, stop=k == kk - 1)
                            if k == kk - 1:
                                ins.then_inc(acc_done, 1)
                        continue
                    if joint and u == 1:
                        continue
                    pe.wait_ge(lo_done, t + 1)
                    if first or ph.more.get("pair"):
                        value = ph.start + ph.stride * i - (2 if v == 0 else 0)
                    else:
                        value = t - 3
                    at_least(pe, acc_free, value)
                    if ph.kind == "branch":
                        for half in range(2):
                            for k in range(kk):
                                wh = w_hi[:, b, k * 256 + half * P:k * 256 + half * P + P]
                                wl = w_lo[:, b, k * 256 + half * P:k * 256 + half * P + P]
                                o = bank[b][:, half * S:half * S + S]
                                pe.matmul(o, wh, xh[:, 4 * i + k, :], start=k == 0, stop=False)
                                pe.matmul(o, wl, xh[:, 4 * i + k, :], start=False, stop=False)
                                ins = pe.matmul(o, wh, xl[:, 4 * i + k, :], start=False, stop=k == kk - 1)
                    else:
                        for k in range(kk):
                            if first and v == 0 and moving_wait(ph, k):
                                pe.wait_ge(*moving_wait(ph, k))
                            wh, wl = w_hi[:, b_w, k * P:k * P + P], w_lo[:, b_w, k * P:k * P + P]
                            o = bank[b][:, 0:width]
                            pe.matmul(o, wh, xh[:, k, 0:width], start=k == 0, stop=False)
                            pe.matmul(o, wl, xh[:, k, 0:width], start=False, stop=False)
                            ins = pe.matmul(o, wh, xl[:, k, 0:width], start=False, stop=k == kk - 1)
                    ins.then_inc(acc_done, 1)
                    if ph.side and v in (0, 2):
                        for j in range(2):
                            pe_mod_turn(ph, i, v + j)
            n4, left = phase_steps(ph)
            if ph.kind == "branch":
                for i in range(n4):
                    step(i, i == 0, i == n4 - 1)
            else:
                repeat(pe, n4, step)
            if left:
                step(n4, False, True, left)
            if ph.kind == "mod":
                for j in (2, 3):
                    pe_mod_turn(ph, n4 - 1, j)

        spread_read = []

        def pe_norm(nm):
            r, width = nm["r"], nm.get("width", S)
            if spread_read:
                pe.wait_ge(*spread_read[-1])
            pe.wait_ge(sq_added, (KD - 2) * (r + 1))
            for tb in range(width // P):
                pe.matmul(STAT[:, tb:tb + 1], sq_sum[:, tb * P:tb * P + P], ones[:, 0:1], start=tb == 0, stop=False)
            pe.wait_ge(sq_done, KD * (r + 1))
            for tb in range(width // P):
                ins = pe.matmul(STAT[:, tb:tb + 1], sq[:, 1, tb * P:tb * P + P], ones[:, 0:1], start=False,
                                stop=tb == width // P - 1)
            ins.then_inc(stat_done, 1)
            pe.wait_ge(diag_done, r + 1)
            pe.matmul(STAT[:, 0:width], ones[:, :], rstd_diag[:, 0:width // P, :], start=True, stop=True) \
              .then_inc(rstd_spread, 1)
            spread_read.append((n_mul, nm["a0"] + KD) if nm["kind"] in ("mod", "plain") else (final_mul, KD))
            if nm["kind"] == "final":
                pe.wait_ge(acc_free, total)
                for q in range(4):
                    tb, fh = q // 2, q % 2
                    pe.wait_ge(final_mul, KD + KD)
                    for f4 in range(4):
                        ins = pe.transpose(bank[q][:, f4 * P:f4 * P + P], T2[:, fh * 4 + f4, tb * P:tb * P + P], ident)
                    ins.then_inc(final_t, 1)

        def pe_mixers(mx):
            pe.wait_ge(s_small, 16 + 64 * (mx["layer"] + 1))
            for s in range(mx["streams"]):
                pe.wait_ge(mix_pool, mx["q_pool"][s])
                for j in range(2):
                    pe.matmul(bank[2 * s + j][:, 0:S], pool_bd[:, j, :], pool_c[:, s, j, :], start=True, stop=True) \
                      .then_inc(mix_pe, 1)

        def pe_gate(ph, q):
            t = ph.start + q
            pe.wait_ge(lo_done, t + 1)
            pe.wait_ge(acc_free, t)
            for k in range(KD):
                wh, wl = (w[:, t % SLOTS, k * P:k * P + P] for w in (w_hi, w_lo))
                o = bank[7][:, 0:S]
                pe.matmul(o, wh, H2_hi[:, k, :], start=k == 0, stop=False)
                pe.matmul(o, wl, H2_hi[:, k, :], start=False, stop=False)
                ins = pe.matmul(o, wh, H2_lo[:, k, :], start=False, stop=k == KD - 1)
            ins.then_inc(acc_done, 1)

        def pe_attend(at_):
            b1 = at_["block"] == 1
            point = gate_points(at_, pe_gate)
            pe.wait_ge(s_tables, 16)
            if b1:
                pe.wait_ge(acc_free, at_["unit_end"])
                layer = at_["layer"]
                pe.wait_ge(s_bias, 16 * 16 * (layer + 1))
                flat = bias_t[:, :, :, :].rearrange("p h r k -> p (h r k)")
                for j in range(6):
                    if j >= 4:
                        pe.wait_ge(bias_done, layer * 6 + j - 3)
                    pe.matmul(bank[j % 4][:, :], table("turn"), flat[:, 512 * j:512 * j + 512], start=True, stop=True) \
                      .then_inc(bias_pe, 1)
                pe.wait_ge(bias_done, layer * 6 + 6)
            else:
                pe.wait_ge(acc_free, at_["unit_end"])
            src = U if b1 else U2
            v_tiles = [16, 17, 18, 19] if b1 else [5] + [14, 15, 16, 17] + [26, 27, 28, 29]
            for j, (tile, nb) in enumerate(at_["vt_jobs"]):
                m = at_["vt0"] + j
                at_least(pe, vt_copy, m - 1)
                for tb in range(nb):
                    ins = pe.transpose(bank[4 + m % 2][:, tb * P:tb * P + P],
                                       src[:, v_tiles[j], tb * P:tb * P + P], ident)
                ins.then_inc(vt_t, 1)
            pe.wait_ge(vt_copy, at_["vt0"] + len(at_["vt_jobs"]))
            if not b1:
                for j in range(13):
                    m = at_["rope0"] + j
                    tile = rope_tiles()[j]
                    at_least(pe, rope_dve, 2 * (m - 1))
                    pe.matmul(bank[5 + m % 2][:, 0:S], rot, U2[:, tile, :], start=True, stop=True).then_inc(rope_pe, 1)
                    if j in GATE_ROPE:
                        point()
                pe.wait_ge(rope_dve, 2 * (at_["rope0"] + 13))
            for what, call in attend_order(at_):
                if what == "sb":
                    pe_stick(at_, point)
                else:
                    pe_call(at_, call, point)
            if b1:
                pe.wait_ge(exp_done, at_["calls"][-1]["groups"][-1]["n"] + 1)
                pe_mixers(at_["mixed"])

        def pv(e, pt, ob, q_lists):
            for idx, (vc, pcols, qcols) in enumerate(q_lists):
                ins = pe.matmul(ob[HD * e:HD * e + HD, qcols[0]:qcols[1]], vt[:, vc:vc + HD], pt[:, pcols[0]:pcols[1]],
                                start=idx == 0, stop=idx == len(q_lists) - 1)
            return ins

        def pe_call(at_, call, point):
            groups, what = call["groups"], call["what"]
            n_g = len(groups)
            nb = len(call["score_banks"])
            npt = len(call["pt_banks"])
            at_least(pe, o_done, call["pair0"])
            if what == "swa":
                pe.wait_ge(k_swap_done, call["layer"] + 1)
            at_least(pe, exp_done, call["n0"])
            at_least(pe, pt_copy, call["n0"])
            for j in range(-LEAD, n_g + T_LAG + 1):
                if j + LEAD < n_g:
                    g = groups[j + LEAD]
                    n, h = g["n"], g["head"]
                    e = h % 2
                    rows_ = slice(HD * e, HD * e + HD)
                    if n - call["n0"] >= nb:
                        pe.wait_ge(exp_done, n - nb + 1)
                    sb_ = bank[call["score_banks"][(n - call["n0"]) % nb]]
                    for si, (qt, a, b) in enumerate(g["segs"]):
                        if what == "near":
                            q = U[rows_, 8 + h // 2, qt * P:qt * P + P]
                            kk = U[rows_, 12 + h // 2, 0:512]
                        elif what == "ctx":
                            q = U[rows_, 8 + h // 2, S + qt * P:S + qt * P + P]
                            kk = U[rows_, 12 + h // 2, S:512]
                        elif what == "swa":
                            q = U2[rows_, h // 2, qt * P:qt * P + P]
                            kk = U2[rows_, 4, 0:b - a] if h // 4 == e else k_swap[rows_, 0:b - a]
                        else:
                            q = U2[rows_, 18 + h // 2, qt * P:qt * P + P]
                            kk = U2[rows_, 22 + h // 2, 0:b - a]
                        ins = pe.matmul(sb_[:, a:b], q, kk, start=True, stop=True)
                    ins.then_inc(sc_done, 1)
                if 0 <= j - T_LAG < n_g:
                    g = groups[j - T_LAG]
                    n = g["n"]
                    pe.wait_ge(p_ready, n + 1)
                    at_least(pe, pt_copy, n - npt + 1)
                    pb = bank[call["pt_banks"][(n - call["n0"]) % npt]]
                    for bi, (col, kb) in enumerate(g["blocks"]):
                        pc = col + (P * kb if what == "near" else 0)
                        ins = pe.transpose(pb[:, bi * P:bi * P + P], probs[:, n % 4, pc:pc + P], ident)
                    ins.then_inc(pt_done, 1)
                if j in GATE_CALL:
                    point()
                jj = j - T_LAG - 1
                if 0 <= jj < n_g and groups[jj]["last"]:
                    g = groups[jj]
                    h, n = g["head"], g["n"]
                    e, hp = h % 2, h // 2
                    pe.wait_ge(pt_copy, n + 1)
                    if e == 0:
                        at_least(pe, o_done, call["pair0"] + hp - len(call["out_banks"]) + 1)
                    ob = out_of(call, hp)
                    if what == "near":
                        ql = [(hp * 512 + kb * P + HD * e, (kb * S, kb * S + S), (0, S)) for kb in range(4)]
                    elif what == "ctx":
                        ql = [(hp * 512 + (2 + kb) * P + HD * e, (kb * S, kb * S + S), (0, S)) for kb in range(2)]
                    else:
                        if what == "swa":
                            v0 = [0 + HD * (h // 4), P + HD * (h // 4)]
                        else:
                            v0 = [(5 + hp) * S + HD * e, (5 + hp) * S + P + HD * e]
                        ql = [(v0[0], (0, S), (0, S)), (v0[1], (S, 384), (P, S))]
                    pv(e, probs_t[:, e, :], ob, ql).then_inc(pv_done, 1)

        def pe_stick(at_, point):
            at_least(pe, o_done, at_["sb_pair0"])
            for j in range(4):
                if j >= 2:
                    pe.wait_ge(sb_scaled, at_["sb0"] + j - 1)
                for e in range(2):
                    rows_ = slice(HD * e, HD * e + HD)
                    q, kk = U2[rows_, 6 + j, :], U2[rows_, 10 + j, :]
                    o = bank[2 * (j % 2) + e]
                    pe.matmul(o[:, 0:S], kk[:, 0:P], q, start=True, stop=True)
                    ins = pe.matmul(o[:, S:384], kk[:, P:S], q[:, P:S], start=True, stop=True)
                ins.then_inc(sb_scores, 1)
                point()
            for j in range(6):
                if j < 4:
                    pe.wait_ge(sb_soft, at_["sb0"] + j + 1)
                    at_least(pe, sb_diff, at_["sb0"] + j)
                    for e in range(2):
                        x_ = sb_e[j][:, e, :]
                        pe.matmul(bank[4 + e][:, 0:S], tri, x_[:, 0:S], start=True, stop=False)
                        pe.matmul(bank[4 + e][:, P:S], ones[:, :], x_[:, S:384], start=False, stop=True)
                        ins = pe.matmul(bank[4 + e][:, S:384], tri, x_[:, S:384], start=True, stop=True)
                    ins.then_inc(sb_remain, 1)
                point()
                if j >= 2:
                    o_ = j - 2
                    pe.wait_ge(sb_weight, at_["sb0"] + o_ + 1)
                    at_least(pe, o_done, at_["sb_pair0"] + o_)
                    for e in range(2):
                        ql = [((1 + o_) * S + HD * e, (0, S), (0, S)), ((1 + o_) * S + P + HD * e, (S, 384), (P, S))]
                        pv(e, sb_z[:, o_, e, :], bank[6][:, 0:S], ql).then_inc(pv_done, 1)

        for kind, ph in plan:
            if kind == "tokens":
                pe_tokens()
            elif kind == "gemm" and ph.kind != "gate":
                pe_gemm(ph)
            elif kind == "norm":
                pe_norm(ph)
            elif kind == "attend":
                pe_attend(ph)

    stack.close()


INPUTS = ["x", "c", "ctx", "c_ctx", "w_mod", "b_mod", "norm_g", "ffn_w_in", "ffn_w_out", "w_in", "conv_w", "pool_w",
          "pool_scale", "rpb", "w_out", "final_g", "norm_mix_2", "w_in_2", "b_gate_2", "sinks_2", "w_branch_2",
          "w_out_2", "norm_ffn_2", "w_up_2", "conv_w_2", "conv_b_2", "w_down_2", "norm_final_2"]


def kernel(**inputs):
    import numpy as _np
    import concourse.bacc as _bacc
    from concourse.bass_utils import run_bass_kernel_spmd as _run

    nc = _bacc.Bacc("TRN2", target_bir_lowering=False, num_devices=1)
    arrays, aps = {}, {}
    for name in INPUTS:
        arrays[name] = _np.ascontiguousarray(inputs[name])
    arrays["consts"] = CONSTS
    for name, a in arrays.items():
        aps[name] = nc.dram_tensor(name, a.shape, mybir.dt.from_np(a.dtype), kind="ExternalInput").ap()
    aps["out"] = nc.dram_tensor("out", (1, S, D), F32, kind="ExternalOutput").ap()
    build_program(nc, **aps)
    r = _run(nc, [arrays], core_ids=[0])
    return r.results[0]["out"]
```
